# Optimizing a Trainium2 kernel written in Bass

```python
import math
import jax, jax.numpy as jnp
from jax import lax
import numpy as np

D_MODEL = 1024
BATCH = 1
SEQ = 1024
DEPTH = 1

BLOCK = 128
FOX_HEADS = 8
FOX_HD = 64
SWA_HEADS = 8
SWA_KV = 2
SWA_HD = 64
WINDOW = 128
POOL_WINDOWS = (2, 4, 8, 16)
POOL_GROUPS = 4
POOL_GW = 128
POOL_W = POOL_GROUPS * POOL_GW
CONV_W = 512
CONV_K = 31
N_BRANCH = 4
PEER_HEADS = 8
PEER_DQ = 256
N_KEYS = 128
N_EXPERTS = N_KEYS * N_KEYS
PEER_TOPK = 16
PEER_CHUNK = 128
LN_EPS = 1e-5
ALPHA = (2 * DEPTH) ** 0.25
BETA = (8 * DEPTH) ** -0.25
IN_SIZES = (FOX_HEADS * FOX_HD, FOX_HEADS * FOX_HD, FOX_HEADS * FOX_HD, FOX_HEADS,
            SWA_HEADS * SWA_HD, SWA_KV * SWA_HD, SWA_KV * SWA_HD,
            POOL_W, 2 * CONV_W, N_BRANCH * D_MODEL)
D_IN = 3 * FOX_HEADS * FOX_HD + FOX_HEADS + SWA_HEADS * SWA_HD + 2 * SWA_KV * SWA_HD + POOL_W + 2 * CONV_W + N_BRANCH * D_MODEL

kernel_name = "fox_pool_conv_swa_peer_deepnorm_hybrid"

def layer_norm(x, g, b):
    xf = x.astype(jnp.float32)
    mu = xf.mean(-1, keepdims=True)
    var = jnp.mean(jnp.square(xf - mu), -1, keepdims=True)
    return ((xf - mu) * lax.rsqrt(var + LN_EPS) * g + b).astype(x.dtype)

def alibi_slopes(n):
    return 2.0 ** (-8.0 * jnp.arange(1, n + 1, dtype=jnp.float32) / n)

def forgetting_attention(q, k, v, f_logit):
    B, S, H, Dh = q.shape
    nb = S // BLOCK
    c = jnp.cumsum(jax.nn.log_sigmoid(f_logit.astype(jnp.float32)), axis=1)
    ck = c.transpose(0, 2, 1)
    qb = q.reshape(B, nb, BLOCK, H, Dh).swapaxes(0, 1)
    cb = c.reshape(B, nb, BLOCK, H).swapaxes(0, 1)
    starts = jnp.arange(nb) * BLOCK
    k_pos = jnp.arange(S)
    scale = Dh ** -0.5

    def one_block(args):
        q_blk, c_blk, start = args
        s = jnp.einsum('bqhd,bkhd->bhqk', q_blk, k, preferred_element_type=jnp.float32) * scale
        s = s + c_blk.transpose(0, 2, 1)[..., None] - ck[:, :, None, :]
        q_pos = start + jnp.arange(BLOCK)
        s = jnp.where(k_pos[None, :] <= q_pos[:, None], s, -jnp.inf)
        p = jax.nn.softmax(s, axis=-1)
        return jnp.einsum('bhqk,bkhd->bqhd', p.astype(v.dtype), v)

    out = lax.map(one_block, (qb, cb, starts))
    return out.swapaxes(0, 1).reshape(B, S, H * Dh)

def sliding_window_gqa(q, k, v, sinks):
    B, S, Hq, Dh = q.shape
    G = k.shape[2]
    R = Hq // G
    nb = S // BLOCK
    qb = q.reshape(B, nb, BLOCK, G, R, Dh)

    def band(t):
        tb = t.reshape(B, nb, BLOCK, G, Dh)
        prev = jnp.concatenate([jnp.zeros_like(tb[:, :1]), tb[:, :-1]], axis=1)
        return jnp.concatenate([prev, tb], axis=2)

    kb, vb = band(k), band(v)
    s = jnp.einsum('bnqgrd,bnkgd->bngrqk', qb, kb, preferred_element_type=jnp.float32) * (Dh ** -0.5)
    qi = jnp.arange(BLOCK)[:, None]
    kj = jnp.arange(2 * BLOCK)[None, :]
    dist = qi + BLOCK - kj
    key_pos = jnp.arange(nb)[:, None, None] * BLOCK - BLOCK + kj[None]
    valid = (dist >= 0)[None] & (dist < WINDOW)[None] & (key_pos >= 0)
    slopes = alibi_slopes(Hq).reshape(G, R)
    s = s - slopes[None, None, :, :, None, None] * dist.astype(jnp.float32)
    s = jnp.where(valid[None, :, None, None], s, -jnp.inf)
    sink = sinks.astype(jnp.float32).reshape(G, R)[None, None, :, :, None, None]
    m = jnp.maximum(s.max(-1, keepdims=True), sink)
    e = jnp.exp(s - m)
    p = e / (e.sum(-1, keepdims=True) + jnp.exp(sink - m))
    o = jnp.einsum('bngrqk,bnkgd->bnqgrd', p.astype(v.dtype), vb)
    return o.reshape(B, S, Hq * Dh)

def multiscale_pool(x, w_grp, scale):
    B, S, C = x.shape
    xf = x.astype(jnp.float32)
    maxw = max(POOL_WINDOWS)
    csp = jnp.concatenate([jnp.zeros((B, maxw, C), jnp.float32), jnp.cumsum(xf, axis=1)], axis=1)
    outs = []
    for g, w in enumerate(POOL_WINDOWS):
        lo, hi = g * POOL_GW, (g + 1) * POOL_GW
        win_sum = csp[:, maxw:, lo:hi] - csp[:, maxw - w:maxw - w + S, lo:hi]
        cnt = jnp.minimum(jnp.arange(1, S + 1), w).astype(jnp.float32)[None, :, None]
        outs.append(win_sum / cnt - xf[:, :, lo:hi])
    p = jnp.stack(outs, axis=2).astype(x.dtype)
    y = jnp.einsum('bsgc,gcd->bsgd', p, w_grp).reshape(B, S, C)
    return y * scale

def conformer_conv(u, w_dw, b_dw, ln_g, ln_b):
    a, gt = jnp.split(u, 2, axis=-1)
    h = a * jax.nn.sigmoid(gt)
    hp = jnp.pad(h, ((0, 0), (CONV_K - 1, 0), (0, 0)))
    h = lax.conv_general_dilated(hp, w_dw[:, None, :].astype(h.dtype), window_strides=(1,), padding='VALID',
                                 dimension_numbers=('NWC', 'WIO', 'NWC'), feature_group_count=CONV_W) + b_dw
    return jax.nn.silu(layer_norm(h, ln_g, ln_b))

def hybrid_mixer(x, w_in, b_f, sinks, pool_w, pool_scale, dw_w, dw_b, cln_g, cln_b,
                 p_fox, p_swa, p_pool, p_conv, w_out):
    B, S, D = x.shape
    h = jnp.einsum('bsd,de->bse', x, w_in)
    pts, acc = [], 0
    for n in IN_SIZES[:-1]:
        acc += n
        pts.append(acc)
    q_f, k_f, v_f, f_l, q_s, k_s, v_s, x_pool, x_conv, gl = jnp.split(h, pts, axis=-1)
    y_fox = forgetting_attention(q_f.reshape(B, S, FOX_HEADS, FOX_HD), k_f.reshape(B, S, FOX_HEADS, FOX_HD),
                                 v_f.reshape(B, S, FOX_HEADS, FOX_HD), f_l + b_f)
    y_swa = sliding_window_gqa(q_s.reshape(B, S, SWA_HEADS, SWA_HD), k_s.reshape(B, S, SWA_KV, SWA_HD),
                               v_s.reshape(B, S, SWA_KV, SWA_HD), sinks)
    y_pool = multiscale_pool(x_pool, pool_w, pool_scale)
    y_conv = conformer_conv(x_conv, dw_w, dw_b, cln_g, cln_b)
    gates = jax.nn.sigmoid(gl.reshape(B, S, N_BRANCH, D))
    merged = (gates[:, :, 0] * (y_fox @ p_fox) + gates[:, :, 1] * (y_pool @ p_pool)
              + gates[:, :, 2] * (y_conv @ p_conv) + gates[:, :, 3] * (y_swa @ p_swa))
    return merged @ w_out

def peer_ffn(x, w_q, sub_k1, sub_k2, u_tab, v_tab):
    B, S, D = x.shape
    T = B * S
    xt = x.reshape(T, D)
    q = (xt @ w_q).reshape(T, PEER_HEADS, 2, PEER_DQ // 2)
    s1 = jnp.einsum('thc,nc->thn', q[:, :, 0], sub_k1, preferred_element_type=jnp.float32)
    s2 = jnp.einsum('thc,nc->thn', q[:, :, 1], sub_k2, preferred_element_type=jnp.float32)
    v1, i1 = lax.top_k(s1, PEER_TOPK)
    v2, i2 = lax.top_k(s2, PEER_TOPK)
    cand_s = (v1[..., :, None] + v2[..., None, :]).reshape(T, PEER_HEADS, PEER_TOPK * PEER_TOPK)
    cand_i = (i1[..., :, None] * N_KEYS + i2[..., None, :]).reshape(T, PEER_HEADS, PEER_TOPK * PEER_TOPK)
    top_s, top_j = lax.top_k(cand_s, PEER_TOPK)
    idx = jnp.take_along_axis(cand_i, top_j, axis=-1)
    g = jax.nn.softmax(top_s, axis=-1).astype(x.dtype)
    nc = T // PEER_CHUNK
    idx = idx.reshape(nc, PEER_CHUNK, PEER_HEADS * PEER_TOPK)
    g = g.reshape(nc, PEER_CHUNK, PEER_HEADS * PEER_TOPK)
    xc = xt.reshape(nc, PEER_CHUNK, D)

    def one_chunk(args):
        xb, ib, gb = args
        act = jax.nn.gelu(jnp.einsum('cd,ced->ce', xb, u_tab[ib]), approximate=False)
        return jnp.einsum('ce,ced->cd', gb * act, v_tab[ib])

    return lax.map(one_chunk, (xc, idx, g)).reshape(B, S, D)

def setup_inputs(seed: int = 0) -> dict:
    key = jax.random.key(seed)
    ks = jax.random.split(key, 32)
    n = lambda k, shape: jax.random.normal(k, shape, jnp.float32)
    L, D = DEPTH, D_MODEL
    return {
        "x": n(ks[0], (BATCH, SEQ, D)),
        "w_in": n(ks[1], (L, D, D_IN)) * D ** -0.5,
        "b_f": 3.0 + 0.5 * n(ks[2], (L, FOX_HEADS)),
        "swa_sinks": 0.5 * n(ks[3], (L, SWA_HEADS)),
        "pool_w": n(ks[4], (L, POOL_GROUPS, POOL_GW, POOL_GW)) * POOL_GW ** -0.5,
        "pool_scale": 1.0 + 0.1 * n(ks[5], (L, POOL_W)),
        "dw_w": n(ks[6], (L, CONV_K, CONV_W)) * CONV_K ** -0.5,
        "dw_b": 0.02 * n(ks[7], (L, CONV_W)),
        "conv_ln_g": 1.0 + 0.1 * n(ks[8], (L, CONV_W)),
        "conv_ln_b": 0.02 * n(ks[9], (L, CONV_W)),
        "p_fox": n(ks[10], (L, FOX_HEADS * FOX_HD, D)) * (FOX_HEADS * FOX_HD) ** -0.5 * BETA,
        "p_swa": n(ks[11], (L, SWA_HEADS * SWA_HD, D)) * (SWA_HEADS * SWA_HD) ** -0.5 * BETA,
        "p_pool": n(ks[12], (L, POOL_W, D)) * POOL_W ** -0.5 * BETA,
        "p_conv": n(ks[13], (L, CONV_W, D)) * CONV_W ** -0.5 * BETA,
        "w_out": n(ks[14], (L, D, D)) * D ** -0.5 * BETA,
        "ln1_g": 1.0 + 0.1 * n(ks[15], (L, D)),
        "ln1_b": 0.02 * n(ks[16], (L, D)),
        "peer_wq": n(ks[17], (L, D, PEER_HEADS * PEER_DQ)) * D ** -0.5,
        "peer_k1": n(ks[18], (L, N_KEYS, PEER_DQ // 2)) * (PEER_DQ // 2) ** -0.5,
        "peer_k2": n(ks[19], (L, N_KEYS, PEER_DQ // 2)) * (PEER_DQ // 2) ** -0.5,
        "peer_u": n(ks[20], (L, N_EXPERTS, D)) * D ** -0.5,
        "peer_v": n(ks[21], (L, N_EXPERTS, D)) * BETA,
        "ln2_g": 1.0 + 0.1 * n(ks[22], (L, D)),
        "ln2_b": 0.02 * n(ks[23], (L, D)),
    }

def reference(x, w_in, b_f, swa_sinks, pool_w, pool_scale, dw_w, dw_b, conv_ln_g, conv_ln_b,
              p_fox, p_swa, p_pool, p_conv, w_out, ln1_g, ln1_b,
              peer_wq, peer_k1, peer_k2, peer_u, peer_v, ln2_g, ln2_b):
    for l in range(DEPTH):
        mix = hybrid_mixer(x, w_in[l], b_f[l], swa_sinks[l], pool_w[l], pool_scale[l], dw_w[l], dw_b[l],
                           conv_ln_g[l], conv_ln_b[l], p_fox[l], p_swa[l], p_pool[l], p_conv[l], w_out[l])
        x = layer_norm(ALPHA * x + mix, ln1_g[l], ln1_b[l])
        ffn = peer_ffn(x, peer_wq[l], peer_k1[l], peer_k2[l], peer_u[l], peer_v[l])
        x = layer_norm(ALPHA * x + ffn, ln2_g[l], ln2_b[l])
    return x


_drawn_inputs = setup_inputs


def setup_inputs(seed=0):
    import zlib

    import numpy as np

    out = dict(_drawn_inputs(seed))
    spreads = {}
    factors = {'swa_sinks': 3.414, 'dw_b': 3.362, 'conv_ln_b': 4.731, 'ln2_b': 2.923}
    for name, (base, spread) in spreads.items():
        noise = np.random.default_rng([zlib.crc32(name.encode()), seed]).standard_normal(out[name].shape)
        drawn = base * np.exp(spread * noise) if base else spread * noise
        out[name] = __import__('jax').numpy.asarray(drawn.astype(out[name].dtype))
    for name, factor in factors.items():
        out[name] = (out[name] * factor).astype(out[name].dtype)
    return out
```

```python
from contextlib import ExitStack

import concourse.bass as bass
from concourse import mybir
import numpy as np

ALU = mybir.AluOpType
ACT = mybir.ActivationFunctionType
AX = mybir.AxisListType
F32 = mybir.dt.float32
F16 = mybir.dt.float16
BF16 = mybir.dt.bfloat16
U32 = mybir.dt.uint32

P = 128
D = 1024
T = 1024
KD = D // P
NCH = T // P
H = 8
HD = 64
CK = 31
NB = 4
TOPK = 16
NKEY = 128
NSEL = H * TOPK
SC = 0.125
EPS = 1e-5
ALPHA = 2.0 ** 0.25
WS = 256.0
RWS = 1.0 / WS

B_T = 25
B_ALL = 30
S_PO, S_QS, S_QF, S_KF, S_KS, S_VF, S_VS = 0, 4, 8, 12, 16, 17, 21
S_CA, S_CG = S_QF, S_KF
NSLOT = 22
S_X1 = 12
S_WO = 0
CW = 256
NQ = D // CW


def await_ge(eng, sem, value):
    eng.wait_ge(sem, value)
    if not isinstance(value, int):
        eng.nop(nofuse=True)


def mm3(pe, out, a_hi, a_lo, b_hi, b_lo, first, last):
    pe.matmul(out, a_hi, b_hi, start=first, stop=False)
    pe.matmul(out, a_hi, b_lo, start=False, stop=False)
    return pe.matmul(out, a_lo, b_hi, start=False, stop=last)


def project(nc, ctx, M, A):
    sem = lambda n: ctx.enter_context(nc.semaphore(n))
    Tt, xh, xl, hc, cacc, wf, wh, wl, pa, pb, sq, rs = (
        M[n] for n in "T xh xl hc cacc wf wh wl pa pb sq rs".split())
    ps = M["ps"]
    cv = M["chan"]
    yT_pool, yT_conv = M["yT_pool"], M["yT_conv"]
    w_in = [sem("w_in0"), sem("w_in1")]
    x_in = [sem("x_in0"), sem("x_in1")]
    c_in = sem("consts_in")
    x_hi, x_lo = sem("x_hi"), sem("x_lo")
    w_scaled, w_ready = sem("w_scaled"), sem("w_ready")
    unit_done, evac = sem("unit_done"), sem("evac")
    sig, h_done = sem("conv_sigmoid"), sem("conv_gated")
    tap = sem("conv_tap")
    f_split, f_lo, f_mm = sem("f_split"), sem("f_lo"), sem("f_mm")
    mean_mm, centred, squared, sq_used, std, normed, silu = (
        sem(n) for n in "mean_mm centred squared sq_used conv_std normed silu".split())
    conv_hi = sem("conv_hi")
    win, pool_mm, pool_hi, pool_lo = sem("windows"), sem("pool_mm"), sem("pool_hi"), sem("pool_lo")
    d_pool = sem("d_pool")
    block = ctx.enter_context(nc.Block())

    xf = Tt[:, 0:KD, :]

    @block.sync
    def _(sp):
        for b in range(2):
            sp.dma_start(wf[b][:], A["w_t"][b]).then_inc(w_in[b], 16)
        for i in range(2):
            sp.dma_start(xf[:, 4 * i:4 * i + 4], A["x_t"][:, 4 * i:4 * i + 4]).then_inc(x_in[i], 16)
        for dst, src in M["const_loads"]:
            sp.dma_start(dst, src).then_inc(c_in, 16)
        with sp.Fori(1, B_ALL // 2) as i:
            for s in range(2):
                sp.wait_ge(w_ready, 2 * i + (s - 1))
                sp.dma_start(wf[s][:], A["w_t"][bass.ds(2 * i + s, 1)].rearrange("o p k c -> p (o k) c")
                             ).then_inc(w_in[s], 16)

    @block.scalar
    def _(act):
        def split(b, s):
            act.wait_ge(w_in[s], b * 8 + (16 - 8 * s))
            act.activation(wh[s][:], wf[s][:], ACT.Copy, scale=WS)
            act.activation(wf[s][:], wf[s][:], ACT.Copy, scale=WS).then_inc(w_scaled, 1)

        def evacuate(b, s, slot):
            for half in range(2):
                act.wait_ge(unit_done, 2 * b + (half + 1))
                act.activation(Tt[:, bass.ds(slot, 1), half * 512:half * 512 + 512].rearrange(
                    "p o c -> p (o c)"), ps[:, 2 * s + half, :], ACT.Copy, scale=RWS).then_inc(evac, 1)

        split(0, 0)
        split(1, 1)
        for k in range(KD):
            if k % 4 == 0:
                act.wait_ge(x_in[k // 4], 16)
            act.activation(xh[:, k, :], xf[:, k, :], ACT.Copy).then_inc(x_hi, 1)
        act.wait_ge(x_lo, KD)
        with act.Fori(0, 4) as i:
            for s in range(2):
                evacuate(2 * i + s, s, 2 * i + (s + 8))
                split(2 * i + (s + 2), s)
        act.drain()
        for g in range(4):
            act.activation(Tt[:, S_CG + g, :], Tt[:, S_CG + g, :], ACT.Sigmoid).then_inc(sig, 1)
        with act.Fori(4, 8) as i:
            for s in range(2):
                evacuate(2 * i + s, s, 2 * i + (s - 8))
                split(2 * i + (s + 2), s)
        act.wait_ge(h_done, 4)
        with act.Fori(8, 12) as i:
            for s in range(2):
                evacuate(2 * i + s, s, 2 * i + (s - 8))
                split(2 * i + (s + 2), s)
        act.wait_ge(c_in, 16 * len(M["const_loads"]))
        act.activation(M["fwh"][:], M["fwf"][:], ACT.Copy, scale=WS)
        act.activation(M["fwf"][:], M["fwf"][:], ACT.Copy, scale=WS).then_inc(f_split, 1)
        for b in range(24, B_ALL):
            s = b % 2
            evacuate(b, s, b - 8)
            if b + 2 < B_ALL:
                split(b + 2, s)
            if b in (25, 27):
                for g in range(b - 25, b - 23):
                    act.wait_ge(centred, g + 1)
                    if g >= 2:
                        act.wait_ge(sq_used, g - 1)
                    act.activation(sq[g % 2][:], cacc[:, g, :], ACT.Square).then_inc(squared, 1)
        act.wait_ge(f_mm, 1)
        act.activation(M["fz"][:], ps[0:H, 0:2, :].rearrange("p a b -> p (a b)"), ACT.Identity,
                       scale=RWS, bias=M["bf"][:, 0:1]).then_inc(evac, 1)
        act.wait_ge(sq_used, 4)
        act.activation(rs[:], ps[:, 6:8, :].rearrange("p a b -> p (a b)"), ACT.Sqrt,
                       bias=M["eps"][:, 0:1]).then_inc(std, 1)
        for g in range(4):
            act.wait_ge(normed, g + 1)
            act.activation(cacc[:, g, :], cacc[:, g, :], ACT.Silu, scale=cv[:, 1, g:g + 1],
                           bias=cv[:, 2, g:g + 1]).then_inc(silu, 1)
            act.wait_ge(silu, g + 1)
            act.activation(yT_conv[:, g, :, 0, :], cacc[:, g, :].rearrange("p (a b) -> p a b", a=NCH),
                           ACT.Copy).then_inc(conv_hi, 1)
        for g in range(4):
            act.wait_ge(pool_mm, g + 1)
            act.activation(yT_pool[:, g, :, 0, :], ps[:, 4 + 2 * (g % 2):6 + 2 * (g % 2), :].rearrange(
                "p a (b c) -> p (a b) c", b=4), ACT.Copy, scale=cv[:, 3, g:g + 1]).then_inc(pool_hi, 1)

    @block.gpsimd
    def _(pool):
        for s in range(2):
            pool.wait_ge(w_scaled, s + 1)
            nc.gpsimd.tensor_tensor(wl[s][:], wf[s][:], wh[s][:], ALU.subtract).then_inc(w_ready, 1)
        with pool.Fori(1, B_ALL // 2) as i:
            for s in range(2):
                await_ge(pool, w_scaled, 2 * i + (s + 1))
                nc.gpsimd.tensor_tensor(wl[s][:], wf[s][:], wh[s][:], ALU.subtract).then_inc(w_ready, 1)
        pool.wait_ge(f_split, 1)
        nc.gpsimd.tensor_tensor(M["fwl"][:], M["fwf"][:], M["fwh"][:], ALU.subtract).then_inc(f_lo, 1)

    @block.tensor
    def _(pe):
        def unit(s, half, by_token):
            out = ps[:, 2 * s + half, :]
            if not by_token:
                tok = slice(512 * half, 512 * half + 512)
                for k in range(KD):
                    m = mm3(pe, out, wh[s][:, k, :], wl[s][:, k, :], xh[:, k, tok], xl[:, k, tok],
                            k == 0, k == KD - 1)
            else:
                for q in range(4):
                    tok = slice(512 * half + P * q, 512 * half + P * q + P)
                    for k in range(KD):
                        m = mm3(pe, out[:, P * q:P * q + P], xh[:, k, tok], xl[:, k, tok],
                                wh[s][:, k, :], wl[s][:, k, :], k == 0, k == KD - 1)
            m.then_inc(unit_done, 1)

        def block_of(b, s, by_token, first=False):
            pe.wait_ge(w_ready, b + 1)
            for half in range(2):
                if not first:
                    pe.wait_ge(evac, 2 * b + (half - 3))
                unit(s, half, by_token)

        pe.wait_ge(x_lo, KD)
        pe.wait_ge(x_hi, KD)
        for s in range(2):
            block_of(s, s, False, first=True)
        with pe.Fori(1, 12) as i:
            for s in range(2):
                block_of(2 * i + s, s, False)
        for b in range(24, B_ALL):
            block_of(b, b % 2, b >= B_T)
            if b == 25:
                pe.wait_ge(tap, 4 * CK)
                for half in range(2):
                    for g in range(4):
                        m = pe.matmul(ps[:, 4 + half, :], M["mean_w"][:], cacc[:, g, 512 * half:512 * half + 512],
                                      start=g == 0, stop=g == 3)
                m.then_inc(mean_mm, 1)
            if b in (27, 29):
                for g in range(b - 27, b - 25):
                    pe.wait_ge(squared, g + 1)
                    for half in range(2):
                        m = pe.matmul(ps[:, 6 + half, :], M["mean_w"][:], sq[g % 2][:, 512 * half:512 * half + 512],
                                      start=g == 0, stop=g == 3)
                    m.then_inc(sq_used, 1)
        pe.wait_ge(f_lo, 1)
        pe.wait_ge(evac, 2 * B_ALL)
        for half in range(2):
            tok = slice(512 * half, 512 * half + 512)
            for k in range(KD):
                m = mm3(pe, ps[0:H, half, :], M["fwh"][:, k, :], M["fwl"][:, k, :], xh[:, k, tok],
                        xl[:, k, tok], k == 0, k == KD - 1)
        m.then_inc(f_mm, 1)
        for g in range(4):
            pe.wait_ge(win, g + 1)
            if g == 0:
                pe.wait_ge(centred, 4)
            if g == 1:
                pe.wait_ge(std, 1)
            if g >= 2:
                pe.wait_ge(pool_lo, g - 1)
            for half in range(2):
                m = pe.matmul(ps[:, 4 + 2 * (g % 2) + half, :], M["pw"][:, g, :],
                              Tt[:, S_PO + g, 512 * half:512 * half + 512], start=True, stop=True)
            m.then_inc(pool_mm, 1)

    @block.vector
    def _(dve):
        nc.vector.memset(M["eps"][:], EPS)
        nc.vector.memset(M["mean_w"][:], 1.0 / 512)
        nc.vector.memset(hc[:, :, 0:CK - 1], 0.0)
        nc.vector.memset(pa[:, 0:16], 0.0)
        nc.vector.memset(pb[:, 0:16], 0.0)
        for k in range(KD):
            dve.wait_ge(x_hi, k + 1)
            nc.vector.tensor_tensor(xl[:, k, :], xf[:, k, :], xh[:, k, :], ALU.subtract).then_inc(x_lo, 1)
        for g in range(4):
            dve.wait_ge(sig, g + 1)
            nc.vector.tensor_tensor(hc[:, g, CK - 1:], Tt[:, S_CA + g, :], Tt[:, S_CG + g, :],
                                    ALU.mult).then_inc(h_done, 1)
        dve.wait_ge(h_done, 4)
        dve.wait_ge(c_in, 16 * len(M["const_loads"]))
        with dve.Fori(0, 2) as q:
            for k in range(CK):
                for r in range(2):
                    g = 2 * q + r
                    acc = cacc[:, bass.ds(g, 1), :].rearrange("p o c -> p (o c)")
                    src = hc[:, bass.ds(g, 1), k:k + T].rearrange("p o c -> p (o c)")
                    w = M["dw"][:, bass.ds(g, 1), k:k + 1].rearrange("p o c -> p (o c)")
                    if k == 0:
                        nc.vector.tensor_scalar(acc, src, w, cv[:, 0, bass.ds(g, 1)], ALU.mult, ALU.add
                                                ).then_inc(tap, 1)
                    else:
                        dve.wait_ge(tap, q * (2 * CK) + (2 * k + r - 1))
                        nc.vector.scalar_tensor_tensor(acc, src, w, acc, ALU.mult, ALU.add).then_inc(tap, 1)
        dve.wait_ge(evac, 2 * 12)
        n = 0
        for g in range(4):
            bufs = [pa, pb]
            nc.vector.tensor_copy(pa[:, 16:], Tt[:, S_PO + g, :]).then_inc(d_pool, 1)
            n += 1
            for s in range(g + 1):
                src, dst = bufs[s % 2], bufs[(s + 1) % 2]
                dve.wait_ge(d_pool, n)
                nc.vector.tensor_tensor(dst[:, 16:], src[:, 16:], src[:, 16 - 2 ** s:16 + T - 2 ** s],
                                        ALU.add).then_inc(d_pool, 1)
                n += 1
            R = bufs[(g + 1) % 2]
            dve.wait_ge(d_pool, n)
            nc.vector.tensor_tensor(M["p16"][:], R[:, 16:32], M["rc"][:, g, :], ALU.mult).then_inc(d_pool, 1)
            nc.vector.scalar_tensor_tensor(Tt[:, S_PO + g, 16:], R[:, 32:], 0.5 ** (g + 1),
                                           Tt[:, S_PO + g, 16:], ALU.mult, ALU.subtract)
            n += 1
            dve.wait_ge(d_pool, n)
            nc.vector.tensor_tensor(Tt[:, S_PO + g, 0:16], M["p16"][:], Tt[:, S_PO + g, 0:16],
                                    ALU.subtract).then_inc(win, 1)
            dve.wait_ge(win, g + 1)
        dve.wait_ge(tap, 4 * CK)
        dve.wait_ge(mean_mm, 1)
        for g in range(4):
            nc.vector.tensor_tensor(cacc[:, g, :], cacc[:, g, :], ps[:, 4:6, :].rearrange("p a b -> p (a b)"),
                                    ALU.subtract).then_inc(centred, 1)
        dve.wait_ge(std, 1)
        nc.vector.reciprocal(rs[:], rs[:])
        dve.drain()
        for g in range(4):
            nc.vector.tensor_tensor(cacc[:, g, :], cacc[:, g, :], rs[:], ALU.mult).then_inc(normed, 1)
        for g in range(4):
            dve.wait_ge(conv_hi, g + 1)
            nc.vector.tensor_tensor(yT_conv[:, g, :, 1, :], cacc[:, g, :].rearrange("p (a b) -> p a b", a=NCH),
                                    yT_conv[:, g, :, 0, :], ALU.subtract)
        for g in range(4):
            dve.wait_ge(pool_hi, g + 1)
            nc.vector.scalar_tensor_tensor(
                yT_pool[:, g, :, 1, :], ps[:, 4 + 2 * (g % 2):6 + 2 * (g % 2), :].rearrange("p a (b c) -> p (a b) c", b=4),
                cv[:, 3, g:g + 1], yT_pool[:, g, :, 0, :], ALU.mult, ALU.subtract).then_inc(pool_lo, 1)



def attention(nc, ctx, M, A):
    sem = lambda n: ctx.enter_context(nc.semaphore(n))
    Tt, ps = M["T"], M["ps"]
    cb, sb, pt, nb, rsum, ident = (M[n] for n in "cb sb pt nb rsum ident".split())
    yT_fox, yT_swa = M["yT_fox"], M["yT_swa"]
    units = [(j, q, r) for j in range(4) for q in range(NCH) for r in range(2)]
    NU = len(units)

    groups = []
    fox_groups, y_group = {}, {}
    for u in range(NU + 2):
        if u < NU:
            q = units[u][1]
            fox_groups[u] = []
            for a in range(0, q + 1, 4):
                fox_groups[u].append(len(groups))
                groups.append(("p", u, a, min(4, q + 1 - a)))
        if u >= 3 and u % 2:
            y_group[u - 2] = len(groups)
            groups.append(("y",) + units[u - 2][:2])
    sp_groups, sy_group = {}, {}
    for n in range(NCH):
        sp_groups[n] = []
        for a in range(0, 16, 4):
            sp_groups[n].append(len(groups))
            groups.append(("sp", n, a, 4))
        sy_group[n] = len(groups)
        groups.append(("sy", n))

    f_abs, f_exp, f_ln, f_z, f_c = (sem(n) for n in "f_abs f_exp f_ln f_sig f_cum".split())
    cb_mm, cb_done = sem("decay_mm"), sem("decay_copied")
    s_done, s_read, p_done = sem("scores"), sem("scores_read"), sem("probs")
    t_done = sem("transposed")
    t_copied = [sem("t_copied_even"), sem("t_copied_odd")]
    y_hi, y_lo = sem("y_hi"), sem("y_lo")
    pv, y_done = sem("pv"), sem("y_written")
    ws_done, ws_max, ws_exp, ws_den, ws_pv, ws_y = (
        sem(n) for n in "swa_scores swa_max swa_exp swa_den swa_pv swa_y".split())
    block = ctx.enter_context(nc.Block())

    def group_free(eng, g):
        if g >= 2:
            eng.wait_ge(t_copied[g % 2], g // 2)

    def copied(ins, g):
        ins.then_inc(t_copied[g % 2], 1)

    def scores_bank(u):
        return 2 * (u % 2)

    @block.scalar
    def _(act):
        fz, ft = M["fz"], M["ft"]
        act.activation(ft[:], fz[:], ACT.Abs).then_inc(f_abs, 1)
        act.wait_ge(f_abs, 1)
        act.activation(ft[:], ft[:], ACT.Exp, scale=-1.0).then_inc(f_exp, 1)
        act.wait_ge(f_exp, 1)
        act.activation(ft[:], ft[:], ACT.Ln, bias=1.0).then_inc(f_ln, 1)

        def copy_group(g):
            kind = groups[g][0]
            bank = ps[:, 4 + g % 2, :]
            act.wait_ge(t_done, g + 1)
            if kind == "p":
                _, u, a, nblk = groups[g]
                if a:
                    if u >= 2:
                        act.wait_ge(pv, u - 1)
                    copied(act.activation(pt[u % 2][:, a:a + nblk, :].rearrange("p a b -> p (a b)"),
                                          bank[:, 0:P * nblk], ACT.Copy), g)
            elif kind == "y":
                _, j, q = groups[g]
                act.activation(yT_fox[:, j, q, 0, :], bank[:, 0:P], ACT.Copy).then_inc(y_hi, 1)
            elif kind == "sp":
                _, n, a, nblk = groups[g]
                if a >= 8:
                    if n >= 1:
                        act.wait_ge(ws_pv, n)
                    copied(act.activation(M["spt"][:, a:a + 4, :].rearrange("p a b -> p (a b)"),
                                          bank, ACT.Copy), g)
            else:
                _, n = groups[g]
                act.activation(yT_swa[:, :, n, 0, :], bank.rearrange("p (a b) -> p a b", a=4),
                               ACT.Copy).then_inc(y_hi, 1)

        for i in range(2 * H):
            act.wait_ge(cb_mm, i + 1)
            act.activation(cb[:, i // 2, 512 * (i % 2):512 * (i % 2) + 512], ps[:, 6 + i % 2, :],
                           ACT.Copy).then_inc(cb_done, 1)
        for u in range(NU + 3):
            if u < NU:
                W = (units[u][1] + 1) * P
                act.wait_ge(s_read, u + 1)
                act.activation(sb[u % 3][:, 0:W], sb[u % 3][:, 0:W], ACT.Exp, scale=-1.0,
                               bias=nb[:, u % 4:u % 4 + 1], accum_out=rsum[:, u % 4:u % 4 + 1]).then_inc(p_done, 1)
            if 1 <= u <= NU:
                for g in fox_groups[u - 1]:
                    copy_group(g)
            if u - 3 in y_group:
                copy_group(y_group[u - 3])

        for n in range(NCH):
            k0 = P if n == 0 else 0
            act.wait_ge(ws_max, 2 * n + 2)
            if n >= 1:
                act.wait_ge(t_done, sp_groups[n - 1][-1] + 1)
            act.activation(M["es"][:], M["snb"][:], ACT.Exp).then_inc(ws_exp, 1)
            for h in range(H):
                act.activation(M["sp"][:, h, k0:], ps[:, h // 2, 256 * (h % 2) + k0:256 * (h % 2) + 256],
                               ACT.Exp, scale=SC, bias=M["wnb"][:, h:h + 1],
                               accum_out=M["wrs"][:, h:h + 1]).then_inc(ws_exp, 1)
            for g in sp_groups[n]:
                copy_group(g)
            copy_group(sy_group[n])

    @block.tensor
    def _(pe):
        def scores(u):
            j, q, r = units[u]
            b0 = scores_bank(u)
            W = (q + 1) * P
            if u >= 2:
                pe.wait_ge(s_read, u - 1)
            lo = r * HD
            qs = Tt[lo:lo + HD, S_QF + j, q * P:q * P + P]
            for c in range(0, W, 512):
                w = min(512, W - c)
                m = pe.matmul(ps[:, b0 + c // 512, 0:w], qs, Tt[lo:lo + HD, S_KF + j, c:c + w],
                              start=True, stop=c + w < W)
            d = q * P
            pe.matmul(ps[:, b0 + d // 512, d % 512:d % 512 + P], M["ident_b"][:], M["fox_mask"][:],
                      start=False, stop=True).then_inc(s_done, 1)

        def turn(g):
            group_free(pe, g)
            kind = groups[g][0]
            bank = ps[:, 4 + g % 2, :]
            if kind == "p":
                _, u, a, nblk = groups[g]
                for b in range(nblk):
                    m = pe.transpose(bank[:, P * b:P * b + P], sb[u % 3][:, P * (a + b):P * (a + b) + P], ident[:])
            elif kind == "y":
                _, j, q = groups[g]
                m = pe.transpose(bank[:, 0:P], Tt[:, S_QF + j, q * P:q * P + P], ident[:])
            elif kind == "sp":
                _, n, a, nblk = groups[g]
                for b in range(nblk):
                    h, kb = (a + b) // 2, (a + b) % 2
                    m = pe.transpose(bank[:, P * b:P * b + P], M["sp"][:, h, P * kb:P * kb + P], ident[:])
            else:
                _, n = groups[g]
                for j in range(4):
                    m = pe.transpose(bank[:, P * j:P * j + P], Tt[:, S_QS + j, n * P:n * P + P], ident[:])
            m.then_inc(t_done, 1)

        def values(u):
            j, q, r = units[u]
            for g in fox_groups[u]:
                pe.wait_ge(t_copied[g % 2], g // 2 + 1)
            if u >= 2:
                pe.wait_ge(y_done, u - 1)
            for b in range(q + 1):
                m = pe.matmul(ps[:, 6 + u % 2, 0:HD], pt[u % 2][:, b, :],
                              Tt[:, S_VF + j, b * P + r * HD:b * P + r * HD + HD], start=b == 0, stop=b == q)
            m.then_inc(pv, 1)

        pe.wait_ge(f_c, 1)
        for i in range(2 * H):
            if i >= 2:
                pe.wait_ge(cb_done, i - 1)
            pe.matmul(ps[:, 6 + i % 2, :], M["sel"][:, i // 2, :],
                      M["negc"][:, 512 * (i % 2):512 * (i % 2) + 512], start=True, stop=True).then_inc(cb_mm, 1)
        pe.wait_ge(cb_done, 2 * H)
        scores(0)
        for u in range(NU + 2):
            if u + 1 < NU:
                scores(u + 1)
            if u < NU:
                pe.wait_ge(p_done, u + 1)
                for g in fox_groups[u]:
                    turn(g)
            if 1 <= u <= NU:
                values(u - 1)
            if u - 2 in y_group:
                pe.wait_ge(y_done, u - 1)
                turn(y_group[u - 2])

        for n in range(NCH):
            k0 = P if n == 0 else 0
            if n >= 1:
                pe.wait_ge(ws_exp, 9 * n)
            for h in range(H):
                r, j = h // 4, h % 4
                lo = r * HD
                out = ps[:, h // 2, 256 * (h % 2) + k0:256 * (h % 2) + 256]
                pe.matmul(out, Tt[lo:lo + HD, S_QS + j, n * P:n * P + P],
                          Tt[lo:lo + HD, S_KS, (n - 1) * P + k0:(n + 1) * P], start=True, stop=False)
                m = pe.matmul(out, M["slope"][:, h, :], M["swa_mask"][:, k0:], start=False, stop=True)
            m.then_inc(ws_done, 1)
            pe.wait_ge(ws_exp, 9 * n + 9)
            for g in sp_groups[n]:
                turn(g)
            for g in sp_groups[n]:
                pe.wait_ge(t_copied[g % 2], g // 2 + 1)
            if n >= 1:
                pe.wait_ge(ws_y, n)
            for h in range(H):
                r = h // 4
                for kb in range(1 if n == 0 else 0, 2):
                    c = n - 1 + kb
                    m = pe.matmul(ps[:, 6, HD * h:HD * h + HD], M["spt"][:, 2 * h + kb, :],
                                  Tt[:, S_VS, c * P + r * HD:c * P + r * HD + HD],
                                  start=kb == (1 if n == 0 else 0), stop=kb == 1)
            m.then_inc(ws_pv, 1)
            pe.wait_ge(ws_y, n + 1)
            turn(sy_group[n])

    @block.vector
    def _(dve):
        fz, ft = M["fz"], M["ft"]
        nc.vector.tensor_copy(M["ident_b"][:], ident[:])
        nc.vector.tensor_copy(M["fox_mask"][:], M["masks"][:, 256:384])
        nc.vector.tensor_copy(M["swa_mask"][:], M["masks"][:, 0:256])
        for h in range(H):
            nc.vector.tensor_scalar(M["slope"][:, h, :], ident[:], M["masks"][:, 512 + h:513 + h], None, ALU.mult)
        dve.wait_ge(f_ln, 1)
        nc.vector.scalar_tensor_tensor(fz[:], fz[:], 0.0, ft[:], ALU.min, ALU.subtract).then_inc(f_z, 1)
        nc.vector.memset(M["ones_t"][:], 1.0).then_inc(f_z, 1)
        dve.wait_ge(f_z, 2)
        nc.vector.tensor_tensor_scan(ft[:], M["ones_t"][:], fz[:], 0.0, ALU.mult, ALU.add).then_inc(f_z, 1)
        dve.wait_ge(f_z, 3)
        nc.vector.tensor_scalar(M["negc"][:], ft[:], -1.0 / SC, None, ALU.mult).then_inc(f_c, 1)

        def copy_group(g):
            kind = groups[g][0]
            bank = ps[:, 4 + g % 2, :]
            if kind == "p":
                _, u, a, nblk = groups[g]
                if a == 0:
                    dve.wait_ge(t_done, g + 1)
                    if u >= 2:
                        dve.wait_ge(pv, u - 1)
                    copied(nc.vector.tensor_copy(pt[u % 2][:, 0:nblk, :].rearrange("p a b -> p (a b)"),
                                                 bank[:, 0:P * nblk]), g)
            elif kind == "y":
                _, j, q = groups[g]
                dve.wait_ge(y_hi, j * NCH + q + 1)
                copied(nc.vector.tensor_tensor(yT_fox[:, j, q, 1, :], bank[:, 0:P], yT_fox[:, j, q, 0, :],
                                               ALU.subtract), g)
            elif kind == "sp":
                _, n, a, nblk = groups[g]
                if a < 8:
                    dve.wait_ge(t_done, g + 1)
                    if n >= 1:
                        dve.wait_ge(ws_pv, n)
                    copied(nc.vector.tensor_copy(M["spt"][:, a:a + 4, :].rearrange("p a b -> p (a b)"), bank), g)
            else:
                _, n = groups[g]
                dve.wait_ge(y_hi, 4 * NCH + n + 1)
                copied(nc.vector.tensor_tensor(yT_swa[:, :, n, 1, :], bank.rearrange("p (a b) -> p a b", a=4),
                                               yT_swa[:, :, n, 0, :], ALU.subtract), g)

        def finish(u):
            j, q, r = units[u]
            dve.wait_ge(p_done, u + 1)
            nc.vector.reciprocal(rsum[:, u % 4:u % 4 + 1], rsum[:, u % 4:u % 4 + 1])
            dve.drain()
            dve.wait_ge(pv, u + 1)
            c = q * P + r * HD
            nc.vector.tensor_scalar(Tt[:, S_QF + j, c:c + HD], ps[:, 6 + u % 2, 0:HD],
                                    rsum[:, u % 4:u % 4 + 1], None, ALU.mult).then_inc(y_done, 1)

        dve.wait_ge(cb_done, 2 * H)
        for u in range(NU + 3):
            if u < NU:
                j, q, r = units[u]
                W = (q + 1) * P
                b0 = scores_bank(u)
                dve.wait_ge(s_done, u + 1)
                if u >= 3:
                    dve.wait_ge(t_done, fox_groups[u - 3][-1] + 1)
                nc.vector.tensor_tensor_reduce(
                    sb[u % 3][:, 0:W], ps[:, b0:b0 + 2, :].rearrange("p a b -> p (a b)")[:, 0:W],
                    cb[:, 2 * j + r, 0:W], -SC, 3e38, ALU.add, ALU.min, nb[:, u % 4:u % 4 + 1]).then_inc(s_read, 1)
            if 1 <= u <= NU:
                for g in fox_groups[u - 1]:
                    copy_group(g)
            if 2 <= u <= NU + 1:
                finish(u - 2)
            if u - 3 in y_group:
                copy_group(y_group[u - 3])

        nc.vector.memset(M["sp"][:, :, 0:P], 0.0)
        for n in range(NCH):
            k0 = P if n == 0 else 0
            dve.wait_ge(ws_done, n + 1)
            nc.vector.tensor_reduce(M["wmx"][:], ps[:, 0:4, :].rearrange("p a (b c) -> p (a b) c", b=2)[:, :, k0:],
                                    AX.X, ALU.max)
            dve.drain()
            nc.vector.scalar_tensor_tensor(M["wnb"][:], M["wmx"][:], SC, M["sinks"][:], ALU.mult, ALU.max)
            dve.drain()
            nc.vector.tensor_tensor(M["snb"][:], M["sinks"][:], M["wnb"][:], ALU.subtract).then_inc(ws_max, 1)
            dve.drain()
            nc.vector.tensor_scalar(M["wnb"][:], M["wnb"][:], -1.0, None, ALU.mult).then_inc(ws_max, 1)
            for g in sp_groups[n][:2]:
                copy_group(g)
            dve.wait_ge(ws_exp, 9 * n + 9)
            nc.vector.tensor_tensor(M["wden"][:], M["wrs"][:], M["es"][:], ALU.add)
            dve.drain()
            nc.vector.reciprocal(M["wden"][:], M["wden"][:])
            dve.drain()
            dve.wait_ge(ws_pv, n + 1)
            for r in range(2):
                ins = nc.vector.tensor_tensor(
                    Tt[:, S_QS:S_QS + 4, n * P + r * HD:n * P + r * HD + HD],
                    ps[:, 6, 256 * r:256 * r + 256].rearrange("p (a b) -> p a b", a=4),
                    M["wden"][:, 4 * r:4 * r + 4].rearrange("p (a o) -> p a o", o=1).to_broadcast([P, 4, HD]),
                    ALU.mult)
            ins.then_inc(ws_y, 1)
            copy_group(sy_group[n])


def merge(nc, ctx, M, A):
    sem = lambda n: ctx.enter_context(nc.semaphore(n))
    Tt, ps, xh, xl, sf, sh, sl, sg, tmp = (M[n] for n in "T ps xh xl sf sh sl sg tmp".split())
    yT = [M[n] for n in ("yT_fox", "yT_pool", "yT_conv", "yT_swa")]
    s_in = [sem("strip_in0"), sem("strip_in1")]
    scaled, ready, strip_used = sem("strip_scaled"), sem("strip_ready"), sem("strip_used")
    gate_mm, y_mm, gate, product = sem("gate_mm"), sem("y_mm"), sem("gate"), sem("product")
    free = sem("banks_free")
    block = ctx.enter_context(nc.Block())

    @block.sync
    def _(sp):
        for s in range(2):
            sp.dma_start(sf[s][:], A["strips"][s]).then_inc(s_in[s], 16)
        with sp.Fori(1, NQ * NB // 2) as i:
            for s in range(2):
                sp.wait_ge(ready, 2 * i + (s - 1))
                sp.dma_start(sf[s][:], A["strips"][bass.ds(2 * i + s, 1)].rearrange("o p k c -> p (o k) c")
                             ).then_inc(s_in[s], 16)

    @block.scalar
    def _(act):
        def split(i, s):
            act.wait_ge(s_in[s], 8 * i + (16 - 8 * s))
            act.activation(sh[s][:], sf[s][:], ACT.Copy, scale=WS)
            act.activation(sf[s][:], sf[s][:], ACT.Copy, scale=WS).then_inc(scaled, 1)

        def strips(cq, last):
            for b in range(NB):
                if b < NB - 1 or not last:
                    act.wait_ge(free, 32 * cq + (8 * b + 4))
                    split(4 * cq + (b + 1), (b + 1) % 2)
                for c in range(NCH):
                    i = 32 * cq + (8 * b + c)
                    act.wait_ge(gate_mm, i + 1)
                    act.wait_ge(free, i + 1)
                    act.activation(sg[c % 4][:], ps[:, c % 4, 0:CW], ACT.Sigmoid, scale=RWS).then_inc(gate, 1)

        split(0, 0)
        with act.Fori(0, NQ - 1) as cq:
            strips(cq, False)
        strips(NQ - 1, True)

    @block.gpsimd
    def _(pool):
        with pool.Fori(0, NQ * NB // 2) as i:
            for s in range(2):
                await_ge(pool, scaled, 2 * i + (s + 1))
                nc.gpsimd.tensor_tensor(sl[s][:], sf[s][:], sh[s][:], ALU.subtract).then_inc(ready, 1)

    @block.tensor
    def _(pe):
        with pe.Fori(0, NQ) as cq:
            for b in range(NB):
                s = b % 2
                pe.wait_ge(ready, 4 * cq + (b + 1))
                for c in range(NCH):
                    i = 32 * cq + (8 * b + c)
                    tok = slice(P * c, P * c + P)
                    pe.wait_ge(free, i + 1)
                    for k in range(KD):
                        m = mm3(pe, ps[:, c % 4, 0:CW], xh[:, k, tok], xl[:, k, tok], sh[s][:, k, :],
                                sl[s][:, k, :], k == 0, k == KD - 1)
                    m.then_inc(gate_mm, 1)
                    for j in range(4):
                        m = mm3(pe, ps[:, 4 + c % 4, 0:CW], yT[b][:, j, c, 0, :], yT[b][:, j, c, 1, :],
                                sh[s][:, KD + j, :], sl[s][:, KD + j, :], j == 0, j == 3)
                    m.then_inc(y_mm, 1)

    @block.vector
    def _(dve):
        nc.vector.memset(tmp[0][:], 0.0).then_inc(free, 4)
        with dve.Fori(0, NQ) as cq:
            for b in range(NB):
                for c in range(NCH):
                    i = 32 * cq + (8 * b + c)
                    out = Tt[:, S_X1 + c, bass.ds(cq * CW, CW)]
                    dve.wait_ge(gate, i + 1)
                    dve.wait_ge(y_mm, i + 1)
                    if b == 0:
                        nc.vector.scalar_tensor_tensor(out, ps[:, 4 + c % 4, 0:CW], RWS, sg[c % 4][:],
                                                       ALU.mult, ALU.mult).then_inc(free, 1)
                    else:
                        nc.vector.scalar_tensor_tensor(tmp[c % 2][:], ps[:, 4 + c % 4, 0:CW], RWS, sg[c % 4][:],
                                                       ALU.mult, ALU.mult).then_inc(free, 1)
                        dve.wait_ge(free, i + 5)
                        nc.vector.tensor_tensor(out, out, tmp[c % 2][:], ALU.add)


def layer_norm(nc, dve, M, row, rstd_wait, gain, shift, out):
    st, mv = M["st"], M["mv"]
    for i in range(2):
        nc.vector.bn_stats(st[:, i, :], row[:, 512 * i:512 * i + 512])
    dve.drain()
    nc.vector.bn_aggr(mv[:], st[:].rearrange("p a b -> p (a b)")).then_inc(M["var_done"], 1)
    rstd_wait()
    nc.vector.reciprocal(M["rstd"][:], M["std"][:])
    nc.vector.scalar_tensor_tensor(row, row, mv[:, 0:1], gain, ALU.subtract, ALU.mult)
    dve.drain()
    return nc.vector.scalar_tensor_tensor(out, row, M["rstd"][:, 0:1], shift, ALU.mult, ALU.add)


def first_norm(nc, ctx, M, A):
    sem = lambda n: ctx.enter_context(nc.semaphore(n))
    Tt, ps, ident, mh, ml, row = (M[n] for n in "T ps ident mh ml row".split())
    wo, wq = M["wo"], M["wq"]
    wof = [Tt[:, 8 + i, :] for i in range(2)]
    wqf = [Tt[:, 10 + i, :].rearrange("p (k c) -> p k c", k=KD) for i in range(2)]
    xin = [Tt[:, 20 + i, :] for i in range(2)]
    wo_in, wq_in, x_in = ([sem(f"{n}{i}") for i in range(2)] for n in ("wo_in", "wq_in", "xc_in"))
    ln_in = sem("ln_in")
    wo_scaled, wo_ready, wq_scaled, wq_ready = (sem(n) for n in "wo_scaled wo_ready wq_scaled wq_ready".split())
    turned, m_hi, m_lo, mix, summed, root = (sem(n) for n in "turned m_hi m_lo mix_mm summed root".split())
    M["var_done"] = sem("var_done")
    x1_done = sem("x1_done")
    block = ctx.enter_context(nc.Block())

    @block.sync
    def _(sp):
        for i in range(2):
            sp.dma_start(wof[i], A["w_o"][i]).then_inc(wo_in[i], 16)
            sp.dma_start(xin[i], A["x"][P * i:P * i + P]).then_inc(x_in[i], 16)
        for k in range(2, KD):
            sp.wait_ge(wo_ready, k - 1)
            sp.dma_start(wof[k % 2], A["w_o"][k]).then_inc(wo_in[k % 2], 16)
        sp.dma_start(M["ln"][:], A["ln"][:, 0:2]).then_inc(ln_in, 16)
        sp.dma_start(M["ln2"][:], A["ln"][:, 2:4]).then_inc(ln_in, 16)
        sp.dma_start(M["kt"][:, 0, :], A["k1_t"]).then_inc(ln_in, 16)
        sp.dma_start(M["kt"][:, 1, :], A["k2_t"]).then_inc(ln_in, 16)
        sp.dma_start(M["iota"][:], A["iota"]).then_inc(ln_in, 16)
        for c in range(NCH):
            for i in range(2):
                if c:
                    sp.wait_ge(wq_ready, 2 * c + i - 1)
                sp.dma_start(wqf[i], A["w_q"][2 * c + i]).then_inc(wq_in[i], 16)
            if 1 <= c < NCH - 1:
                sp.wait_ge(summed, c)
                sp.dma_start(xin[(c + 1) % 2], A["x"][P * (c + 1):P * (c + 2)]).then_inc(x_in[(c + 1) % 2], 16)
        sp.wait_ge(ln_in, 80)

    @block.scalar
    def _(act):
        for k in range(KD):
            act.wait_ge(wo_in[k % 2], 16 * (k // 2 + 1))
            act.activation(wo[:, k, 0, :], wof[k % 2], ACT.Copy, scale=WS)
            act.activation(wof[k % 2], wof[k % 2], ACT.Copy, scale=WS).then_inc(wo_scaled, 1)
        for c in range(NCH + 1):
            if c < NCH:
                act.wait_ge(turned, c + 1)
                if c >= 2:
                    act.wait_ge(mix, c - 1)
                act.activation(mh[c % 2][:], ps[:, 2 * (c % 2):2 * (c % 2) + 2, :].rearrange("p a b -> p (a b)"),
                               ACT.Copy).then_inc(m_hi, 1)
            if c:
                act.wait_ge(M["var_done"], c)
                act.activation(M["std"][:], M["mv"][:, 1:2], ACT.Sqrt, bias=M["eps"][:, 0:1]).then_inc(root, 1)
            for b in (2 * c, 2 * c + 1):
                if b < 2 * H:
                    act.wait_ge(wq_in[b % 2], 16 * (b // 2 + 1))
                    act.activation(wq[:, b, 0, :, :], wqf[b % 2], ACT.Copy, scale=WS)
                    act.activation(wqf[b % 2], wqf[b % 2], ACT.Copy, scale=WS).then_inc(wq_scaled, 1)

    @block.gpsimd
    def _(pool):
        for k in range(KD):
            pool.wait_ge(wo_scaled, k + 1)
            nc.gpsimd.tensor_tensor(wo[:, k, 1, :], wof[k % 2], wo[:, k, 0, :], ALU.subtract).then_inc(wo_ready, 1)
        for b in range(2 * H):
            pool.wait_ge(wq_scaled, b + 1)
            nc.gpsimd.tensor_tensor(wq[:, b, 1, :, :], wqf[b % 2], wq[:, b, 0, :, :], ALU.subtract).then_inc(wq_ready, 1)

    @block.tensor
    def _(pe):
        def turn(c):
            if c >= 2:
                pe.wait_ge(m_lo, c - 1)
            for k in range(KD):
                m = pe.transpose(ps[:, 2 * (c % 2) + k // 4, P * (k % 4):P * (k % 4) + P],
                                 Tt[:, S_X1 + c, P * k:P * k + P], ident[:])
            m.then_inc(turned, 1)

        turn(0)
        for c in range(NCH):
            if c + 1 < NCH:
                turn(c + 1)
            if c == 0:
                pe.wait_ge(wo_ready, KD)
            pe.wait_ge(m_lo, c + 1)
            if c >= 2:
                pe.wait_ge(summed, c - 1)
            for k in range(KD):
                for a, b in ((0, 0), (0, 1), (1, 0)):
                    lhs = (mh, ml)[a][c % 2][:, P * k:P * k + P]
                    for half in range(2):
                        m = pe.matmul(ps[:, 4 + 2 * (c % 2) + half, :], lhs, wo[:, k, b, 512 * half:512 * half + 512],
                                      start=k == a == b == 0, stop=k == KD - 1 and a == 1)
            m.then_inc(mix, 1)

    @block.vector
    def _(dve):
        for c in range(NCH + 1):
            if c < NCH:
                dve.wait_ge(m_hi, c + 1)
                nc.vector.tensor_tensor(ml[c % 2][:], ps[:, 2 * (c % 2):2 * (c % 2) + 2, :].rearrange("p a b -> p (a b)"),
                                        mh[c % 2][:], ALU.subtract).then_inc(m_lo, 1)
            if c:
                d = c - 1
                if d == 0:
                    dve.wait_ge(ln_in, 80)
                dve.wait_ge(x_in[d % 2], 16 * (d // 2 + 1))
                nc.vector.tensor_scalar(xin[d % 2], xin[d % 2], ALPHA, None, ALU.mult)
                dve.drain()
                dve.wait_ge(mix, d + 1)
                nc.vector.scalar_tensor_tensor(row[:], ps[:, 4 + 2 * (d % 2):6 + 2 * (d % 2), :].rearrange(
                    "p a b -> p (a b)"), RWS, xin[d % 2], ALU.mult, ALU.add).then_inc(summed, 1)
                dve.drain()
                layer_norm(nc, dve, M, row[:], lambda: dve.wait_ge(root, d + 1), M["ln"][:, 0, :], M["ln"][:, 1, :],
                           Tt[:, S_X1 + d, :]).then_inc(x1_done, 1)
                dve.drain()


def experts(nc, ctx, M, A, out):
    sem = lambda n: ctx.enter_context(nc.semaphore(n))
    Tt, ps, ident, wq = (M[n] for n in "T ps ident wq".split())
    xc, xth, xtl, qt, sc, cand, oh, kt = (M[n] for n in "xc xth xtl qt sc cand oh kt".split())
    v16, ix, ixf, pos, posf, sel_a, sel_b = (M[n] for n in "v16 ix ixf pos posf sel_a sel_b".split())
    top, topj, gg, gsum, idx_next, idx, hid, act_t, wgt, acc = (
        M[n] for n in "top topj gg gsum idx_next idx hid act_t wgt acc".split())
    ring = M["ring"]
    NR = len(ring)
    landed = [sem(f"landed{i}") for i in range(NR)]
    free = sem("ring_free")
    chosen, copied_x, turned, x_hi, x_lo = (sem(n) for n in "chosen x1_copied x1_turned x1_hi x1_lo".split())
    q_mm, q_out, s_mm, s_out = (sem(n) for n in "q_mm q_out s_mm s_out".split())
    exp_in, exp_out, selected, gelu = (sem(n) for n in "exp_in exp_out selected gelu".split())
    root, row_done = sem("root2"), sem("row_done")
    stored = sem("acc_free")
    M["var_done"] = sem("var2_done")
    block = ctx.enter_context(nc.Block())

    @block.gpsimd
    def _(pool):
        with pool.Fori(0, NCH) as c:
            await_ge(pool, chosen, c + 1)
            for i in range(2 * NSEL):
                if i % 4 == 0:
                    await_ge(pool, free, 256 * c + (i + 4))
                table = A["u"] if i < NSEL else A["v"]
                e = i % NSEL
                nc.gpsimd.indirect_dma_start(
                    ring[i % NR], None, table, bass.IndirectOffsetOnAxis(ap=idx[:, e:e + 1], axis=0)
                ).then_inc(landed[i % NR], 16)

    @block.sync
    def _(sp):
        with sp.Fori(0, NCH) as c:
            sp.wait_ge(row_done, c + 1)
            sp.dma_start(out[bass.ds(P * c, P), :], acc[0][:]).then_inc(stored, 16)
        sp.wait_ge(stored, 16 * NCH + 16)

    @block.tensor
    def _(pe):
        def queries(n):
            pe.wait_ge(copied_x, n + 1)
            for k in range(KD):
                m = pe.transpose(ps[:, k // 4, P * (k % 4):P * (k % 4) + P], xc[:, P * k:P * k + P], ident[:])
            m.then_inc(turned, 1)
            pe.wait_ge(x_lo, n + 1)
            for b in range(2 * H):
                for k in range(KD):
                    m = mm3(pe, ps[:, 4 + b // 4, P * (b % 4):P * (b % 4) + P], wq[:, b, 0, k, :], wq[:, b, 1, k, :],
                            xth[:, P * k:P * k + P], xtl[:, P * k:P * k + P], k == 0, k == KD - 1)
                if b % 4 == 3:
                    m.then_inc(q_mm, 1)
            for b in range(2 * H):
                if b % 4 == 0:
                    pe.wait_ge(q_out, 4 * n + (b // 4 + 1))
                m = pe.matmul(ps[:, b // 4, P * (b % 4):P * (b % 4) + P], qt[:, b, :], kt[:, b % 2, :],
                              start=True, stop=True)
                if b % 4 == 3:
                    m.then_inc(s_mm, 1)

        queries(0)
        with pe.Fori(1, NCH) as n:
            pe.wait_ge(s_out, 4 * n)
            queries(n)

    @block.scalar
    def _(act):
        def copy_x(n):
            act.activation(xc[:], Tt[:, bass.ds(S_X1 + n, 1), :].rearrange("p o c -> p (o c)"), ACT.Copy
                           ).then_inc(copied_x, 1)

        def queries(n):
            act.wait_ge(turned, n + 1)
            act.activation(xth[:], ps[:, 0:2, :].rearrange("p a b -> p (a b)"), ACT.Copy).then_inc(x_hi, 1)
            for i in range(4):
                act.wait_ge(q_mm, 4 * n + (i + 1))
                act.activation(qt[:, 4 * i:4 * i + 4, :].rearrange("p a b -> p (a b)"), ps[:, 4 + i, :], ACT.Copy,
                               scale=RWS).then_inc(q_out, 1)
            for i in range(4):
                act.wait_ge(s_mm, 4 * n + (i + 1))
                act.activation(sc[:, 4 * i:4 * i + 4, :].rearrange("p a b -> p (a b)"), ps[:, i, :], ACT.Copy
                               ).then_inc(s_out, 1)

        def weights(n):
            act.wait_ge(exp_in, n + 1)
            act.activation(gg[:], gg[:], ACT.Exp).then_inc(exp_out, 1)

        def gates(c):
            act.wait_ge(free, 256 * c + (NR + NSEL))
            act.activation(act_t[:], hid[:], ACT.Gelu).then_inc(gelu, 1)

        def root_of(c):
            act.wait_ge(M["var_done"], c + 1)
            act.activation(M["std"][:], M["mv"][:, 1:2], ACT.Sqrt, bias=M["eps"][:, 0:1]).then_inc(root, 1)

        copy_x(0)
        queries(0)
        weights(0)
        with act.Fori(0, NCH - 1) as c:
            copy_x(c + 1)
            act.wait_ge(selected, c + 1)
            queries(c + 1)
            gates(c)
            weights(c + 1)
            root_of(c)
        gates(NCH - 1)
        root_of(NCH - 1)

    @block.vector
    def _(dve):
        def x_low(n):
            dve.wait_ge(x_hi, n + 1)
            nc.vector.tensor_tensor(xtl[:], ps[:, 0:2, :].rearrange("p a b -> p (a b)"), xth[:], ALU.subtract
                                    ).then_inc(x_lo, 1)

        def choose(k, n):
            if k == 0:
                await_ge(dve, s_out, 4 * n + 4)
            if k < 16:
                nc.vector.max(v16[:, k, 0:8], sc[:, k, :])
                if k == 15:
                    dve.drain()
            elif k < 48:
                b = (k - 16) // 2
                if k % 2 == 0:
                    nc.vector.max_index(ix[:, b, 0:8], v16[:, b, 0:8], sc[:, b, :])
                else:
                    nc.vector.match_replace(sc[:, b, :], v16[:, b, 0:8], sc[:, b, :], -3e38)
                if k == 47:
                    dve.drain()
            elif k < 64:
                nc.vector.max(v16[:, k - 48, 8:16], sc[:, k - 48, :])
                if k == 63:
                    dve.drain()
            elif k < 80:
                nc.vector.max_index(ix[:, k - 64, 8:16], v16[:, k - 64, 8:16], sc[:, k - 64, :])
            elif k < 88:
                h = k - 80
                nc.vector.tensor_tensor(
                    cand[:, h, :].rearrange("p (a b) -> p a b", a=16),
                    v16[:, 2 * h, :].rearrange("p (a o) -> p a o", o=1).to_broadcast([P, 16, 16]),
                    v16[:, 2 * h + 1:2 * h + 2, :].to_broadcast([P, 16, 16]), ALU.add)
                if k == 87:
                    dve.drain()
            elif k < 96:
                nc.vector.max(top[:, k - 88, 0:8], cand[:, k - 88, :])
                if k == 95:
                    dve.drain()
            elif k < 112:
                h = (k - 96) // 2
                if k % 2 == 0:
                    nc.vector.max_index(pos[:, h, 0:8], top[:, h, 0:8], cand[:, h, :])
                else:
                    nc.vector.match_replace(cand[:, h, :], top[:, h, 0:8], cand[:, h, :], -3e38)
                if k == 111:
                    dve.drain()
            elif k < 120:
                nc.vector.max(top[:, k - 112, 8:16], cand[:, k - 112, :])
                if k == 119:
                    dve.drain()
            elif k < 128:
                nc.vector.max_index(pos[:, k - 120, 8:16], top[:, k - 120, 8:16], cand[:, k - 120, :])
                if k == 127:
                    dve.drain()
            elif k == 128:
                nc.vector.tensor_tensor(gg[:].rearrange("p (h k) -> p h k", h=H), top[:],
                                        top[:, :, 0:1].to_broadcast([P, H, TOPK]), ALU.subtract).then_inc(exp_in, 1)
                nc.vector.tensor_copy(ixf, ix[:])
                nc.vector.tensor_scalar(topj[:, 0, :], pos[:].rearrange("p h k -> p (h k)"), 4, None,
                                        ALU.logical_shift_right)
                nc.vector.tensor_scalar(topj[:, 1, :], pos[:].rearrange("p h k -> p (h k)"), 15, None,
                                        ALU.bitwise_and)
                dve.drain()
            elif k == 129:
                nc.vector.tensor_copy(posf, topj)
                dve.drain()
            elif k in (130, 134):
                s = (k - 130) // 4
                nc.vector.tensor_tensor(oh[:], posf[:, s, :].rearrange("p (a o) -> p a o", o=1).to_broadcast([P, NSEL, 16]),
                                        M["iota"][:].rearrange("p (o a) -> p o a", o=1).to_broadcast([P, NSEL, 16]),
                                        ALU.is_equal)
                dve.drain()
            elif k in (131, 135):
                s = (k - 131) // 4
                for h in range(H):
                    nc.vector.tensor_tensor(oh[:, 16 * h:16 * h + 16, :], oh[:, 16 * h:16 * h + 16, :],
                                            ixf[:, 2 * h + s:2 * h + s + 1, :].to_broadcast([P, 16, 16]), ALU.mult)
                dve.drain()
            elif k in (132, 136):
                s = (k - 132) // 4
                nc.vector.tensor_reduce((sel_a, sel_b)[s], oh[:], AX.X, ALU.add)
                dve.drain()
            elif k == 137:
                nc.vector.scalar_tensor_tensor(idx_next[:], sel_a, float(NKEY), sel_b, ALU.mult, ALU.add)
                dve.wait_ge(exp_out, n + 1)
                nc.vector.tensor_reduce(gsum[:], gg[:].rearrange("p (h k) -> p h k", h=H), AX.X, ALU.add)
                dve.drain()
            elif k == 138:
                nc.vector.reciprocal(gsum[:], gsum[:])
                dve.drain()
            elif k == 139:
                nc.vector.tensor_tensor(gg[:].rearrange("p (h k) -> p h k", h=H), gg[:].rearrange("p (h k) -> p h k", h=H),
                                        gsum[:].rearrange("p (h o) -> p h o", o=1).to_broadcast([P, H, TOPK]),
                                        ALU.mult).then_inc(selected, 1)
                dve.drain()

        def chunk(c, more):
            x1 = M["x1c"][:]
            nc.vector.tensor_copy(x1, Tt[:, bass.ds(S_X1 + c, 1), :].rearrange("p o c -> p (o c)"))
            dve.drain()
            for e in range(NSEL):
                r = e % NR
                dve.wait_ge(landed[r], 256 * c + 16 * (e // NR + 1))
                nc.vector.tensor_tensor_reduce(ring[r], ring[r], x1, 1.0, 0.0, ALU.mult, ALU.add,
                                               hid[:, e:e + 1]).then_inc(free, 1)
                if e == 8 and more:
                    x_low(c + 1)
            dve.wait_ge(gelu, c + 1)
            nc.vector.tensor_tensor(wgt[:], gg[:], act_t[:], ALU.mult)
            dve.drain()
            for e in range(NSEL):
                i = NSEL + e
                r = i % NR
                dve.wait_ge(landed[r], 256 * c + 16 * (i // NR + 1))
                if e == NSEL - 1 and more:
                    dve.nop(nofuse=True)
                    nc.vector.tensor_copy(idx[:], idx_next[:]).then_inc(chosen, 1)
                if e < 2:
                    if e == 0:
                        dve.wait_ge(stored, 16 * c + 16)
                    nc.vector.tensor_scalar(acc[e][:], ring[r], wgt[:, e:e + 1], None, ALU.mult).then_inc(free, 1)
                else:
                    dve.wait_ge(free, 256 * c + (NR + i - 1))
                    nc.vector.scalar_tensor_tensor(acc[e % 2][:], ring[r], wgt[:, e:e + 1], acc[e % 2][:],
                                                   ALU.mult, ALU.add).then_inc(free, 1)
                if more and e < 70:
                    choose(2 * e, c + 1)
                    choose(2 * e + 1, c + 1)
            dve.drain()
            nc.vector.tensor_tensor(acc[0][:], acc[0][:], acc[1][:], ALU.add)
            dve.drain()
            nc.vector.scalar_tensor_tensor(acc[0][:], x1, ALPHA, acc[0][:], ALU.mult, ALU.add)
            dve.drain()
            layer_norm(nc, dve, M, acc[0][:], lambda: dve.wait_ge(root, c + 1), M["ln2"][:, 0, :],
                       M["ln2"][:, 1, :], acc[0][:]).then_inc(row_done, 1)

        nc.vector.memset(hid[:], 0.0).then_inc(free, NR)
        nc.vector.memset(wgt[:], 0.0).then_inc(stored, 16)
        x_low(0)
        for k in range(140):
            choose(k, 0)
        nc.vector.tensor_copy(idx[:], idx_next[:]).then_inc(chosen, 1)
        with dve.Fori(0, NCH - 1) as c:
            chunk(c, True)
        chunk(NCH - 1, False)


def build_mix(nc, ctx, A, out=None, dump=None):
    keep = lambda n, s, d: ctx.enter_context(nc.sbuf_tensor(n, s, d))
    M = {}
    M["T"] = keep("tiles", [P, NSLOT, T], F32)
    M["ps"] = ctx.enter_context(nc.psum_tensor("ps", [P, 8, 512], F32))
    M["ident"] = keep("ident", [P, P], F32)
    M["eps"] = keep("eps", [P, 1], F32)
    Tt = M["T"]

    def pair_view(ap):
        return ap.bitcast(F16).rearrange("p j (q h c) -> p j q h c", q=NCH, h=2)

    M["yT_fox"] = pair_view(Tt[:, S_QF:S_QF + 4, :])
    M["yT_pool"] = pair_view(Tt[:, S_PO:S_PO + 4, :])
    M["yT_swa"] = pair_view(Tt[:, S_QS:S_QS + 4, :])
    with ExitStack() as early:
        sb = lambda n, s, d: early.enter_context(nc.sbuf_tensor(n, s, d))
        M["xh"], M["xl"] = sb("x_hi_t", [P, KD, T], F16), sb("x_lo_t", [P, KD, T], F16)
        hc_raw = sb("conv_in", [P, 4 * (T + CK - 1)], F32)
        M["hc"] = hc_raw[:].rearrange("p (g t) -> p g t", g=4)
        M["yT_conv"] = pair_view(hc_raw[:, 0:4 * T].rearrange("p (j t) -> p j t", j=4))
        M["fz"] = sb("forget", [H, T], F32)
        M["sinks"] = sb("sinks_sb", [P, H], F32)
        M["masks"] = sb("masks_sb", [P, 512 + H], F32)
        M["sel"] = sb("sel_sb", [H, H, P], F32)
        with ExitStack() as c1:
            s1 = lambda n, s, d: c1.enter_context(nc.sbuf_tensor(n, s, d))
            M["cacc"] = s1("conv_acc", [P, 4, T], F32)
            M["wf"] = [s1(f"w_f32_{i}", [P, KD, P], F32) for i in range(2)]
            M["wh"] = [s1(f"w_hi_{i}", [P, KD, P], F16) for i in range(2)]
            M["wl"] = [s1(f"w_lo_{i}", [P, KD, P], F16) for i in range(2)]
            M["pa"], M["pb"] = s1("window_a", [P, 16 + T], F32), s1("window_b", [P, 16 + T], F32)
            M["sq"] = [s1(f"square_{i}", [P, T], F32) for i in range(2)]
            M["rs"] = s1("conv_rstd", [P, T], F32)
            M["chan"] = s1("chan_sb", [P, 4, 4], F32)
            M["dw"] = s1("dw_sb", [P, 4, CK], F32)
            M["pw"] = s1("pool_w_sb", [P, 4, P], F32)
            M["rc"] = s1("rc_sb", [P, 4, 16], F32)
            M["p16"] = s1("p16", [P, 16], F32)
            M["bf"] = s1("b_f_sb", [H, 1], F32)
            M["fwf"] = s1("wf_f32", [P, KD, H], F32)
            M["fwh"], M["fwl"] = s1("wf_hi", [P, KD, H], F16), s1("wf_lo", [P, KD, H], F16)
            M["mean_w"] = s1("mean_w", [P, P], F32)
            M["const_loads"] = [
                (M["chan"][:], A["chan"]), (M["dw"][:], A["dw"]), (M["pw"][:], A["pool_w"]),
                (M["rc"][:], A["rc"]), (M["bf"][:], A["b_f"]), (M["fwf"][:], A["w_f"]),
                (M["sinks"][:], A["sinks"]), (M["masks"][:], A["masks"]), (M["sel"][:], A["sel"]),
                (M["ident"][:], A["masks"][:, 384:512])]
            project(nc, c1, M, A)
        with ExitStack() as c2:
            s2 = lambda n, s, d: c2.enter_context(nc.sbuf_tensor(n, s, d))
            M["cb"] = s2("decay", [P, H, T], F32)
            probs = s2("probs_sb", [P, 3, T], F32)
            M["sb"] = [probs[:, i, :] for i in range(3)]
            turned = s2("probs_t", [P, 16, P], F32)
            M["pt"] = [turned[:, 0:8, :], turned[:, 8:16, :]]
            M["ft"], M["ones_t"], M["negc"] = (probs[0:H, i, :] for i in range(3))
            M["sp"] = probs[:, 0:2, :].rearrange("p a (h k) -> p (a h) k", h=4)
            M["spt"] = turned
            M["nb"], M["rsum"] = s2("nb", [P, 4], F32), s2("rsum", [P, 4], F32)
            M["ident_b"] = s2("ident_b", [P, P], BF16)
            M["fox_mask"] = s2("fox_mask", [P, P], BF16)
            M["swa_mask"] = s2("swa_mask", [P, 2 * P], BF16)
            M["slope"] = s2("slope", [P, H, P], BF16)
            for n in "wmx wnb snb es wrs wden".split():
                M[n] = s2(n, [P, H], F32)
            attention(nc, c2, M, A)
        if dump:
            z = ctx.enter_context(nc.semaphore("dumped"))
            block = early.enter_context(nc.Block())

            @block.sync
            def _(sp):
                sp.dma_start(dump[1][:, 0:NSLOT * T].rearrange("p (a b) -> p a b", a=NSLOT), Tt[:]).then_inc(z, 16)
                sp.dma_start(dump[0], hc_raw[:, 0:4 * T]).then_inc(z, 16)
                sp.dma_start(dump[2], M["fz"][:]).then_inc(z, 16)
                sp.wait_ge(z, 48)

        if out is None:
            return
        with ExitStack() as c3:
            s3 = lambda n, s, d: c3.enter_context(nc.sbuf_tensor(n, s, d))
            M["sf"] = [s3(f"strip_f32_{i}", [P, KD + 4, CW], F32) for i in range(2)]
            M["sh"] = [s3(f"strip_hi_{i}", [P, KD + 4, CW], F16) for i in range(2)]
            M["sl"] = [s3(f"strip_lo_{i}", [P, KD + 4, CW], F16) for i in range(2)]
            M["sg"] = [s3(f"gate_{i}", [P, CW], F32) for i in range(4)]
            M["tmp"] = [s3(f"product_{i}", [P, CW], F32) for i in range(2)]
            merge(nc, c3, M, A)
    with ExitStack() as late:
        sb = lambda n, s, d: late.enter_context(nc.sbuf_tensor(n, s, d))
        M["wq"] = sb("wq_pairs", [P, 2 * H, 2, KD, P], F16)
        M["ln2"] = sb("ln2_sb", [P, 2, D], F32)
        M["kt"] = sb("keys_t", [P, 2, NKEY], F32)
        M["iota"] = sb("iota_sb", [P, 16], F32)
        M["st"], M["mv"] = sb("bn_st", [P, 2, 6], F32), sb("bn_mv", [P, 2], F32)
        M["std"], M["rstd"] = sb("std", [P, 1], F32), sb("rstd", [P, 1], F32)
        M["wo"] = Tt[:, S_WO:S_WO + 8, :].bitcast(F16).rearrange("p k (h c) -> p k h c", h=2)
        with ExitStack() as c4:
            s4 = lambda n, s, d: c4.enter_context(nc.sbuf_tensor(n, s, d))
            M["ln"] = s4("ln1_sb", [P, 2, D], F32)
            M["mh"] = [s4(f"m_hi_{i}", [P, D], F16) for i in range(2)]
            M["ml"] = [s4(f"m_lo_{i}", [P, D], F16) for i in range(2)]
            M["row"] = s4("row", [P, D], F32)
            first_norm(nc, c4, M, A)
        with ExitStack() as c5:
            s5 = lambda n, s, d: c5.enter_context(nc.sbuf_tensor(n, s, d))
            M["xth"], M["xtl"] = s5("x1t_hi", [P, D], F16), s5("x1t_lo", [P, D], F16)
            qc = s5("queries_or_sums", [P, 2 * H, P], F32)
            so = s5("scores_or_onehot", [P, 2 * H, NKEY], F32)
            M["qt"], M["cand"] = qc, qc[:].rearrange("p (h a) b -> p h (a b)", a=2)
            M["sc"], M["oh"] = so, so[:].rearrange("p a (b c) -> p (a b) c", c=16)
            M["v16"], M["ix"] = s5("best_keys", [P, 2 * H, 16], F32), s5("best_key_ids", [P, 2 * H, 16], U32)
            M["top"], M["pos"] = s5("best_sums", [P, H, 16], F32), s5("best_places", [P, H, 16], U32)
            M["ixf"] = qc[:, 0:2, :].rearrange("p a (b c) -> p (a b) c", c=16)
            M["topj"], M["posf"] = qc[:, 2:4, :].bitcast(U32), qc[:, 4:6, :]
            M["sel_a"], M["sel_b"] = qc[:, 6, :], qc[:, 7, :]
            M["x1c"] = s5("x1_chunk", [P, D], F32)
            for n in "gg hid act_t wgt".split():
                M[n] = s5(n, [P, NSEL], F32)
            M["gsum"] = s5("gsum", [P, H], F32)
            M["idx_next"], M["idx"] = s5("idx_next", [P, NSEL], U32), s5("idx", [P, NSEL], U32)
            M["acc"] = [s5(f"acc{i}", [P, D], F32) for i in range(2)]
            M["xc"] = M["acc"][1]
            extra = [s5(f"ring_extra{i}", [P, D], F32) for i in range(2)]
            M["ring"] = [Tt[:, i, :] for i in list(range(12)) + [20, 21]] + [e[:] for e in extra]
            experts(nc, c5, M, A, out)


def layout(x, w_in, b_f, swa_sinks, pool_w, pool_scale, dw_w, dw_b, conv_ln_g, conv_ln_b,
           p_fox, p_swa, p_pool, p_conv, w_out, ln1_g, ln1_b,
           peer_wq, peer_k1, peer_k2, peer_u, peer_v, ln2_g, ln2_b):
    x = np.asarray(x)[0]
    w = np.asarray(w_in)[0]
    sizes = [512, 512, 512, 8, 512, 128, 128, 512, 512, 512, 4 * D]
    names = "qf kf vf f qs ks vs po ca cg gl".split()
    at = dict(zip(names, zip(np.cumsum([0] + sizes[:-1]), sizes)))
    cols = {n: w[:, a:a + s] for n, (a, s) in at.items()}
    swa = np.concatenate([np.r_[j * HD:(j + 1) * HD, (4 + j) * HD:(5 + j) * HD] for j in range(4)])
    cols["qs"] = cols["qs"][:, swa]
    wt = np.concatenate([cols[n] for n in "ca cg po qs qf kf ks vf vs".split()], 1)
    assert wt.shape[1] == B_ALL * P

    def kblocks(m, width):
        k = m.shape[0] // P
        return m.reshape(k, P, -1, width).transpose(2, 1, 0, 3)

    def rows(v):
        return np.broadcast_to(np.asarray(v)[0][None, :], (P, np.asarray(v).shape[1]))

    def chans(v):
        return np.asarray(v)[0].reshape(-1, P).T

    gl = cols["gl"].reshape(D, NB, D)
    ps_ = {"fox": np.asarray(p_fox)[0], "pool": np.asarray(p_pool)[0], "conv": np.asarray(p_conv)[0],
           "swa": np.asarray(p_swa)[0][swa]}
    strips = np.stack([np.concatenate([kblocks(gl[:, b], CW), kblocks(ps_[n], CW)], 2)
                       for b, n in enumerate(["fox", "pool", "conv", "swa"])], 1)
    i, j = np.arange(P)[:, None], np.arange(2 * P)[None, :]
    dist = i + P - j
    swa_mask = np.where((dist >= 0) & (dist < P), -8.0 * dist, -1e30)
    fox_mask = np.where(np.arange(P)[None, :] <= i, 0.0, -1e30)
    slopes = np.repeat(2.0 ** -np.arange(1, H + 1)[None, :], P, 0)
    masks = np.concatenate([swa_mask, fox_mask, np.eye(P), slopes], 1)
    sel = np.zeros((H, H, P))
    for h in range(H):
        sel[h, h] = 1.0
    rc = np.zeros((P, 4, 16))
    for g in range(4):
        rc[:, g] = 1.0 / np.minimum(np.arange(1, 17), 2 ** (g + 1))
    out = {
        "x": x, "x_t": x.T.reshape(KD, P, T).transpose(1, 0, 2),
        "w_t": kblocks(wt, P), "w_f": kblocks(cols["f"], H)[0],
        "strips": strips.reshape(NQ * NB, P, 12, CW),
        "w_o": np.asarray(w_out)[0].reshape(KD, P, D),
        "w_q": kblocks(np.asarray(peer_wq)[0], P),
        "b_f": np.asarray(b_f)[0][:, None], "sinks": rows(swa_sinks),
        "pool_w": np.asarray(pool_w)[0].transpose(1, 0, 2),
        "chan": np.stack([chans(dw_b), chans(conv_ln_g), chans(conv_ln_b), chans(pool_scale)], 1),
        "dw": np.asarray(dw_w)[0].reshape(CK, 4, P).transpose(2, 1, 0),
        "ln": np.stack([rows(ln1_g), rows(ln1_b), rows(ln2_g), rows(ln2_b)], 1),
        "k1_t": np.asarray(peer_k1)[0].T, "k2_t": np.asarray(peer_k2)[0].T,
        "u": np.asarray(peer_u)[0], "v": np.asarray(peer_v)[0],
        "masks": masks, "sel": sel, "rc": rc,
        "iota": np.repeat(np.arange(16.0)[None, :], P, 0),
    }
    return {n: np.ascontiguousarray(a, np.float32) for n, a in out.items()}


def kernel(**inputs):
    import concourse.bacc as bacc
    from concourse.bass_utils import run_bass_kernel_spmd

    nc = bacc.Bacc("TRN2", target_bir_lowering=False, num_devices=1)
    arrays = layout(**inputs)
    A = {n: nc.dram_tensor(n, a.shape, mybir.dt.from_np(a.dtype), kind="ExternalInput").ap()
         for n, a in arrays.items()}
    out = nc.dram_tensor("out", (T, D), F32, kind="ExternalOutput").ap()
    with ExitStack() as ctx:
        build_mix(nc, ctx, A, out)
    r = run_bass_kernel_spmd(nc, [arrays], core_ids=[0])
    return r.results[0]["out"].reshape(1, T, D)
```

```python
from contextlib import ExitStack

import concourse.bass as bass
from concourse import mybir
import numpy as np

ALU = mybir.AluOpType
ACT = mybir.ActivationFunctionType
AX = mybir.AxisListType
F32 = mybir.dt.float32
F16 = mybir.dt.float16
BF16 = mybir.dt.bfloat16
U32 = mybir.dt.uint32

P = 128
D = 1024
T = 1024
KD = D // P
NCH = T // P
H = 8
HD = 64
CK = 31
NB = 4
TOPK = 16
NKEY = 128
NSEL = H * TOPK
NEXP = NKEY * NKEY
ND = NCH // 2
DT = ND * P
NU = 2
SC = 0.125
EPS = 1e-5
ALPHA = 2.0 ** 0.25
WS = 256.0
RWS = 1.0 / WS

B_T = 25
B_ALL = 30
S_PO, S_QS, S_QF, S_KF, S_KS, S_VF, S_VS = 0, 4, 8, 12, 16, 17, 21
S_CA, S_CG = S_QF, S_KF
NSLOT = 22
S_X1 = 12
S_WO = 0
CW = 256
NQ = D // CW


def await_ge(eng, sem, value):
    eng.wait_ge(sem, value)
    if not isinstance(value, int):
        eng.nop(nofuse=True)


def mm3(pe, out, a_hi, a_lo, b_hi, b_lo, first, last):
    pe.matmul(out, a_hi, b_hi, start=first, stop=False)
    pe.matmul(out, a_hi, b_lo, start=False, stop=False)
    return pe.matmul(out, a_lo, b_hi, start=False, stop=last)


def project(nc, ctx, M, A):
    sem = lambda n: ctx.enter_context(nc.semaphore(n))
    Tt, xh, xl, hc, cacc, wf, wh, wl, pa, pb, sq, rs = (
        M[n] for n in "T xh xl hc cacc wf wh wl pa pb sq rs".split())
    ps = M["ps"]
    cv = M["chan"]
    yT_pool, yT_conv = M["yT_pool"], M["yT_conv"]
    w_in = [sem("w_in0"), sem("w_in1")]
    x_in = [sem("x_in0"), sem("x_in1")]
    c_in = sem("consts_in")
    x_hi, x_lo = sem("x_hi"), sem("x_lo")
    w_scaled, w_ready = sem("w_scaled"), sem("w_ready")
    unit_done, evac = sem("unit_done"), sem("evac")
    sig, h_done = sem("conv_sigmoid"), sem("conv_gated")
    tap = sem("conv_tap")
    f_split, f_lo, f_mm = sem("f_split"), sem("f_lo"), sem("f_mm")
    mean_mm, centred, squared, sq_used, std, normed, silu = (
        sem(n) for n in "mean_mm centred squared sq_used conv_std normed silu".split())
    conv_hi = sem("conv_hi")
    win, pool_mm, pool_hi, pool_lo = sem("windows"), sem("pool_mm"), sem("pool_hi"), sem("pool_lo")
    d_pool = sem("d_pool")
    block = ctx.enter_context(nc.Block())

    xf = Tt[:, 0:KD, :]

    @block.sync
    def _(sp):
        for b in range(2):
            sp.dma_start(wf[b][:], A["w_t"][b]).then_inc(w_in[b], 16)
        for i in range(2):
            sp.dma_start(xf[:, 4 * i:4 * i + 4], A["x_t"][:, 4 * i:4 * i + 4]).then_inc(x_in[i], 16)
        for dst, src in M["const_loads"]:
            sp.dma_start(dst, src).then_inc(c_in, 16)
        with sp.Fori(1, B_ALL // 2) as i:
            for s in range(2):
                sp.wait_ge(w_ready, 2 * i + (s - 1))
                sp.dma_start(wf[s][:], A["w_t"][bass.ds(2 * i + s, 1)].rearrange("o p k c -> p (o k) c")
                             ).then_inc(w_in[s], 16)

    @block.scalar
    def _(act):
        def split(b, s):
            act.wait_ge(w_in[s], b * 8 + (16 - 8 * s))
            act.activation(wh[s][:], wf[s][:], ACT.Copy, scale=WS)
            act.activation(wf[s][:], wf[s][:], ACT.Copy, scale=WS).then_inc(w_scaled, 1)

        def evacuate(b, s, slot):
            for half in range(2):
                act.wait_ge(unit_done, 2 * b + (half + 1))
                act.activation(Tt[:, bass.ds(slot, 1), half * 512:half * 512 + 512].rearrange(
                    "p o c -> p (o c)"), ps[:, 2 * s + half, :], ACT.Copy, scale=RWS).then_inc(evac, 1)

        split(0, 0)
        split(1, 1)
        for k in range(KD):
            if k % 4 == 0:
                act.wait_ge(x_in[k // 4], 16)
            act.activation(xh[:, k, :], xf[:, k, :], ACT.Copy).then_inc(x_hi, 1)
        act.wait_ge(x_lo, KD)
        with act.Fori(0, 4) as i:
            for s in range(2):
                evacuate(2 * i + s, s, 2 * i + (s + 8))
                split(2 * i + (s + 2), s)
        act.drain()
        for g in range(4):
            act.activation(Tt[:, S_CG + g, :], Tt[:, S_CG + g, :], ACT.Sigmoid).then_inc(sig, 1)
        with act.Fori(4, 8) as i:
            for s in range(2):
                evacuate(2 * i + s, s, 2 * i + (s - 8))
                split(2 * i + (s + 2), s)
        act.wait_ge(h_done, 4)
        with act.Fori(8, 12) as i:
            for s in range(2):
                evacuate(2 * i + s, s, 2 * i + (s - 8))
                split(2 * i + (s + 2), s)
        act.wait_ge(c_in, 16 * len(M["const_loads"]))
        act.activation(M["fwh"][:], M["fwf"][:], ACT.Copy, scale=WS)
        act.activation(M["fwf"][:], M["fwf"][:], ACT.Copy, scale=WS).then_inc(f_split, 1)
        for b in range(24, B_ALL):
            s = b % 2
            evacuate(b, s, b - 8)
            if b + 2 < B_ALL:
                split(b + 2, s)
            if b in (25, 27):
                for g in range(b - 25, b - 23):
                    act.wait_ge(centred, g + 1)
                    if g >= 2:
                        act.wait_ge(sq_used, g - 1)
                    act.activation(sq[g % 2][:], cacc[:, g, :], ACT.Square).then_inc(squared, 1)
        act.wait_ge(f_mm, 1)
        act.activation(M["fz"][:], ps[0:H, 0:2, :].rearrange("p a b -> p (a b)"), ACT.Identity,
                       scale=RWS, bias=M["bf"][:, 0:1]).then_inc(evac, 1)
        act.wait_ge(sq_used, 4)
        act.activation(rs[:], ps[:, 6:8, :].rearrange("p a b -> p (a b)"), ACT.Sqrt,
                       bias=M["eps"][:, 0:1]).then_inc(std, 1)
        for g in range(4):
            act.wait_ge(normed, g + 1)
            act.activation(cacc[:, g, :], cacc[:, g, :], ACT.Silu, scale=cv[:, 1, g:g + 1],
                           bias=cv[:, 2, g:g + 1]).then_inc(silu, 1)
            act.wait_ge(silu, g + 1)
            act.activation(yT_conv[:, g, :, 0, :], cacc[:, g, :].rearrange("p (a b) -> p a b", a=NCH),
                           ACT.Copy).then_inc(conv_hi, 1)
        for g in range(4):
            act.wait_ge(pool_mm, g + 1)
            act.activation(yT_pool[:, g, :, 0, :], ps[:, 4 + 2 * (g % 2):6 + 2 * (g % 2), :].rearrange(
                "p a (b c) -> p (a b) c", b=4), ACT.Copy, scale=cv[:, 3, g:g + 1]).then_inc(pool_hi, 1)

    @block.gpsimd
    def _(pool):
        for s in range(2):
            pool.wait_ge(w_scaled, s + 1)
            nc.gpsimd.tensor_tensor(wl[s][:], wf[s][:], wh[s][:], ALU.subtract).then_inc(w_ready, 1)
        with pool.Fori(1, B_ALL // 2) as i:
            for s in range(2):
                await_ge(pool, w_scaled, 2 * i + (s + 1))
                nc.gpsimd.tensor_tensor(wl[s][:], wf[s][:], wh[s][:], ALU.subtract).then_inc(w_ready, 1)
        pool.wait_ge(f_split, 1)
        nc.gpsimd.tensor_tensor(M["fwl"][:], M["fwf"][:], M["fwh"][:], ALU.subtract).then_inc(f_lo, 1)

    @block.tensor
    def _(pe):
        def unit(s, half, by_token):
            out = ps[:, 2 * s + half, :]
            if not by_token:
                tok = slice(512 * half, 512 * half + 512)
                for k in range(KD):
                    m = mm3(pe, out, wh[s][:, k, :], wl[s][:, k, :], xh[:, k, tok], xl[:, k, tok],
                            k == 0, k == KD - 1)
            else:
                for q in range(4):
                    tok = slice(512 * half + P * q, 512 * half + P * q + P)
                    for k in range(KD):
                        m = mm3(pe, out[:, P * q:P * q + P], xh[:, k, tok], xl[:, k, tok],
                                wh[s][:, k, :], wl[s][:, k, :], k == 0, k == KD - 1)
            m.then_inc(unit_done, 1)

        def block_of(b, s, by_token, first=False):
            pe.wait_ge(w_ready, b + 1)
            for half in range(2):
                if not first:
                    pe.wait_ge(evac, 2 * b + (half - 3))
                unit(s, half, by_token)

        pe.wait_ge(x_lo, KD)
        pe.wait_ge(x_hi, KD)
        for s in range(2):
            block_of(s, s, False, first=True)
        with pe.Fori(1, 12) as i:
            for s in range(2):
                block_of(2 * i + s, s, False)
        for b in range(24, B_ALL):
            block_of(b, b % 2, b >= B_T)
            if b == 25:
                pe.wait_ge(tap, 4 * CK)
                for half in range(2):
                    for g in range(4):
                        m = pe.matmul(ps[:, 4 + half, :], M["mean_w"][:], cacc[:, g, 512 * half:512 * half + 512],
                                      start=g == 0, stop=g == 3)
                m.then_inc(mean_mm, 1)
            if b in (27, 29):
                for g in range(b - 27, b - 25):
                    pe.wait_ge(squared, g + 1)
                    for half in range(2):
                        m = pe.matmul(ps[:, 6 + half, :], M["mean_w"][:], sq[g % 2][:, 512 * half:512 * half + 512],
                                      start=g == 0, stop=g == 3)
                    m.then_inc(sq_used, 1)
        pe.wait_ge(f_lo, 1)
        pe.wait_ge(evac, 2 * B_ALL)
        for half in range(2):
            tok = slice(512 * half, 512 * half + 512)
            for k in range(KD):
                m = mm3(pe, ps[0:H, half, :], M["fwh"][:, k, :], M["fwl"][:, k, :], xh[:, k, tok],
                        xl[:, k, tok], k == 0, k == KD - 1)
        m.then_inc(f_mm, 1)
        for g in range(4):
            pe.wait_ge(win, g + 1)
            if g == 0:
                pe.wait_ge(centred, 4)
            if g == 1:
                pe.wait_ge(std, 1)
            if g >= 2:
                pe.wait_ge(pool_lo, g - 1)
            for half in range(2):
                m = pe.matmul(ps[:, 4 + 2 * (g % 2) + half, :], M["pw"][:, g, :],
                              Tt[:, S_PO + g, 512 * half:512 * half + 512], start=True, stop=True)
            m.then_inc(pool_mm, 1)

    @block.vector
    def _(dve):
        nc.vector.memset(M["eps"][:], EPS)
        nc.vector.memset(M["mean_w"][:], 1.0 / 512)
        nc.vector.memset(hc[:, :, 0:CK - 1], 0.0)
        nc.vector.memset(pa[:, 0:16], 0.0)
        nc.vector.memset(pb[:, 0:16], 0.0)
        for k in range(KD):
            dve.wait_ge(x_hi, k + 1)
            nc.vector.tensor_tensor(xl[:, k, :], xf[:, k, :], xh[:, k, :], ALU.subtract).then_inc(x_lo, 1)
        for g in range(4):
            dve.wait_ge(sig, g + 1)
            nc.vector.tensor_tensor(hc[:, g, CK - 1:], Tt[:, S_CA + g, :], Tt[:, S_CG + g, :],
                                    ALU.mult).then_inc(h_done, 1)
        dve.wait_ge(h_done, 4)
        dve.wait_ge(c_in, 16 * len(M["const_loads"]))
        with dve.Fori(0, 2) as q:
            for k in range(CK):
                for r in range(2):
                    g = 2 * q + r
                    acc = cacc[:, bass.ds(g, 1), :].rearrange("p o c -> p (o c)")
                    src = hc[:, bass.ds(g, 1), k:k + T].rearrange("p o c -> p (o c)")
                    w = M["dw"][:, bass.ds(g, 1), k:k + 1].rearrange("p o c -> p (o c)")
                    if k == 0:
                        nc.vector.tensor_scalar(acc, src, w, cv[:, 0, bass.ds(g, 1)], ALU.mult, ALU.add
                                                ).then_inc(tap, 1)
                    else:
                        dve.wait_ge(tap, q * (2 * CK) + (2 * k + r - 1))
                        nc.vector.scalar_tensor_tensor(acc, src, w, acc, ALU.mult, ALU.add).then_inc(tap, 1)
        dve.wait_ge(evac, 2 * 12)
        n = 0
        for g in range(4):
            bufs = [pa, pb]
            nc.vector.tensor_copy(pa[:, 16:], Tt[:, S_PO + g, :]).then_inc(d_pool, 1)
            n += 1
            for s in range(g + 1):
                src, dst = bufs[s % 2], bufs[(s + 1) % 2]
                dve.wait_ge(d_pool, n)
                nc.vector.tensor_tensor(dst[:, 16:], src[:, 16:], src[:, 16 - 2 ** s:16 + T - 2 ** s],
                                        ALU.add).then_inc(d_pool, 1)
                n += 1
            R = bufs[(g + 1) % 2]
            dve.wait_ge(d_pool, n)
            nc.vector.tensor_tensor(M["p16"][:], R[:, 16:32], M["rc"][:, g, :], ALU.mult).then_inc(d_pool, 1)
            nc.vector.scalar_tensor_tensor(Tt[:, S_PO + g, 16:], R[:, 32:], 0.5 ** (g + 1),
                                           Tt[:, S_PO + g, 16:], ALU.mult, ALU.subtract)
            n += 1
            dve.wait_ge(d_pool, n)
            nc.vector.tensor_tensor(Tt[:, S_PO + g, 0:16], M["p16"][:], Tt[:, S_PO + g, 0:16],
                                    ALU.subtract).then_inc(win, 1)
            dve.wait_ge(win, g + 1)
        dve.wait_ge(tap, 4 * CK)
        dve.wait_ge(mean_mm, 1)
        for g in range(4):
            nc.vector.tensor_tensor(cacc[:, g, :], cacc[:, g, :], ps[:, 4:6, :].rearrange("p a b -> p (a b)"),
                                    ALU.subtract).then_inc(centred, 1)
        dve.wait_ge(std, 1)
        nc.vector.reciprocal(rs[:], rs[:])
        dve.drain()
        for g in range(4):
            nc.vector.tensor_tensor(cacc[:, g, :], cacc[:, g, :], rs[:], ALU.mult).then_inc(normed, 1)
        for g in range(4):
            dve.wait_ge(conv_hi, g + 1)
            nc.vector.tensor_tensor(yT_conv[:, g, :, 1, :], cacc[:, g, :].rearrange("p (a b) -> p a b", a=NCH),
                                    yT_conv[:, g, :, 0, :], ALU.subtract)
        for g in range(4):
            dve.wait_ge(pool_hi, g + 1)
            nc.vector.scalar_tensor_tensor(
                yT_pool[:, g, :, 1, :], ps[:, 4 + 2 * (g % 2):6 + 2 * (g % 2), :].rearrange("p a (b c) -> p (a b) c", b=4),
                cv[:, 3, g:g + 1], yT_pool[:, g, :, 0, :], ALU.mult, ALU.subtract).then_inc(pool_lo, 1)



def attention(nc, ctx, M, A):
    sem = lambda n: ctx.enter_context(nc.semaphore(n))
    Tt, ps = M["T"], M["ps"]
    cb, sb, pt, nb, rsum, ident = (M[n] for n in "cb sb pt nb rsum ident".split())
    yT_fox, yT_swa = M["yT_fox"], M["yT_swa"]
    units = [(j, q, r) for j in range(4) for q in range(NCH) for r in range(2)]
    NU = len(units)

    groups = []
    fox_groups, y_group = {}, {}
    for u in range(NU + 2):
        if u < NU:
            q = units[u][1]
            fox_groups[u] = []
            for a in range(0, q + 1, 4):
                fox_groups[u].append(len(groups))
                groups.append(("p", u, a, min(4, q + 1 - a)))
        if u >= 3 and u % 2:
            y_group[u - 2] = len(groups)
            groups.append(("y",) + units[u - 2][:2])
    sp_groups, sy_group = {}, {}
    for n in range(NCH):
        sp_groups[n] = []
        for a in range(0, 16, 4):
            sp_groups[n].append(len(groups))
            groups.append(("sp", n, a, 4))
        sy_group[n] = len(groups)
        groups.append(("sy", n))

    f_abs, f_exp, f_ln, f_z, f_c = (sem(n) for n in "f_abs f_exp f_ln f_sig f_cum".split())
    cb_mm, cb_done = sem("decay_mm"), sem("decay_copied")
    s_done, s_read, p_done = sem("scores"), sem("scores_read"), sem("probs")
    t_done = sem("transposed")
    t_copied = [sem("t_copied_even"), sem("t_copied_odd")]
    y_hi, y_lo = sem("y_hi"), sem("y_lo")
    pv, y_done = sem("pv"), sem("y_written")
    ws_done, ws_max, ws_exp, ws_den, ws_pv, ws_y = (
        sem(n) for n in "swa_scores swa_max swa_exp swa_den swa_pv swa_y".split())
    block = ctx.enter_context(nc.Block())

    zero, zeroed = sem("zero_tile"), sem("weights_zeroed")

    @block.gpsimd
    def _(pool):
        pool.memset(M["zeros"][:], 0.0).then_inc(zero, 1)

    @block.sync
    def _(sp):
        sp.wait_ge(zero, 1)
        with sp.Fori(0, NEXP // P // 2) as n:
            sp.dma_start(A["weights_rows"][bass.ds(n, 1)].rearrange("o p c -> p (o c)"), M["zeros"][:]
                         ).then_inc(zeroed, 16)
        sp.wait_ge(zeroed, 16 * (NEXP // P // 2))

    def group_free(eng, g):
        if g >= 2:
            eng.wait_ge(t_copied[g % 2], g // 2)

    def copied(ins, g):
        ins.then_inc(t_copied[g % 2], 1)

    def scores_bank(u):
        return 2 * (u % 2)

    @block.scalar
    def _(act):
        fz, ft = M["fz"], M["ft"]
        act.activation(ft[:], fz[:], ACT.Abs).then_inc(f_abs, 1)
        act.wait_ge(f_abs, 1)
        act.activation(ft[:], ft[:], ACT.Exp, scale=-1.0).then_inc(f_exp, 1)
        act.wait_ge(f_exp, 1)
        act.activation(ft[:], ft[:], ACT.Ln, bias=1.0).then_inc(f_ln, 1)

        def copy_group(g):
            kind = groups[g][0]
            bank = ps[:, 4 + g % 2, :]
            act.wait_ge(t_done, g + 1)
            if kind == "p":
                _, u, a, nblk = groups[g]
                if a:
                    if u >= 2:
                        act.wait_ge(pv, u - 1)
                    copied(act.activation(pt[u % 2][:, a:a + nblk, :].rearrange("p a b -> p (a b)"),
                                          bank[:, 0:P * nblk], ACT.Copy), g)
            elif kind == "y":
                _, j, q = groups[g]
                act.activation(yT_fox[:, j, q, 0, :], bank[:, 0:P], ACT.Copy).then_inc(y_hi, 1)
            elif kind == "sp":
                _, n, a, nblk = groups[g]
                if a >= 8:
                    if n >= 1:
                        act.wait_ge(ws_pv, n)
                    copied(act.activation(M["spt"][:, a:a + 4, :].rearrange("p a b -> p (a b)"),
                                          bank, ACT.Copy), g)
            else:
                _, n = groups[g]
                act.activation(yT_swa[:, :, n, 0, :], bank.rearrange("p (a b) -> p a b", a=4),
                               ACT.Copy).then_inc(y_hi, 1)

        for i in range(2 * H):
            act.wait_ge(cb_mm, i + 1)
            act.activation(cb[:, i // 2, 512 * (i % 2):512 * (i % 2) + 512], ps[:, 6 + i % 2, :],
                           ACT.Copy).then_inc(cb_done, 1)
        for u in range(NU + 3):
            if u < NU:
                W = (units[u][1] + 1) * P
                act.wait_ge(s_read, u + 1)
                act.activation(sb[u % 3][:, 0:W], sb[u % 3][:, 0:W], ACT.Exp, scale=-1.0,
                               bias=nb[:, u % 4:u % 4 + 1], accum_out=rsum[:, u % 4:u % 4 + 1]).then_inc(p_done, 1)
            if 1 <= u <= NU:
                for g in fox_groups[u - 1]:
                    copy_group(g)
            if u - 3 in y_group:
                copy_group(y_group[u - 3])

        for n in range(NCH):
            k0 = P if n == 0 else 0
            act.wait_ge(ws_max, 2 * n + 2)
            if n >= 1:
                act.wait_ge(t_done, sp_groups[n - 1][-1] + 1)
            act.activation(M["es"][:], M["snb"][:], ACT.Exp).then_inc(ws_exp, 1)
            for h in range(H):
                act.activation(M["sp"][:, h, k0:], ps[:, h // 2, 256 * (h % 2) + k0:256 * (h % 2) + 256],
                               ACT.Exp, scale=SC, bias=M["wnb"][:, h:h + 1],
                               accum_out=M["wrs"][:, h:h + 1]).then_inc(ws_exp, 1)
            for g in sp_groups[n]:
                copy_group(g)
            copy_group(sy_group[n])

    @block.tensor
    def _(pe):
        def scores(u):
            j, q, r = units[u]
            b0 = scores_bank(u)
            W = (q + 1) * P
            if u >= 2:
                pe.wait_ge(s_read, u - 1)
            lo = r * HD
            qs = Tt[lo:lo + HD, S_QF + j, q * P:q * P + P]
            for c in range(0, W, 512):
                w = min(512, W - c)
                m = pe.matmul(ps[:, b0 + c // 512, 0:w], qs, Tt[lo:lo + HD, S_KF + j, c:c + w],
                              start=True, stop=c + w < W)
            d = q * P
            pe.matmul(ps[:, b0 + d // 512, d % 512:d % 512 + P], M["ident_b"][:], M["fox_mask"][:],
                      start=False, stop=True).then_inc(s_done, 1)

        def turn(g):
            group_free(pe, g)
            kind = groups[g][0]
            bank = ps[:, 4 + g % 2, :]
            if kind == "p":
                _, u, a, nblk = groups[g]
                for b in range(nblk):
                    m = pe.transpose(bank[:, P * b:P * b + P], sb[u % 3][:, P * (a + b):P * (a + b) + P], ident[:])
            elif kind == "y":
                _, j, q = groups[g]
                m = pe.transpose(bank[:, 0:P], Tt[:, S_QF + j, q * P:q * P + P], ident[:])
            elif kind == "sp":
                _, n, a, nblk = groups[g]
                for b in range(nblk):
                    h, kb = (a + b) // 2, (a + b) % 2
                    m = pe.transpose(bank[:, P * b:P * b + P], M["sp"][:, h, P * kb:P * kb + P], ident[:])
            else:
                _, n = groups[g]
                for j in range(4):
                    m = pe.transpose(bank[:, P * j:P * j + P], Tt[:, S_QS + j, n * P:n * P + P], ident[:])
            m.then_inc(t_done, 1)

        def values(u):
            j, q, r = units[u]
            for g in fox_groups[u]:
                pe.wait_ge(t_copied[g % 2], g // 2 + 1)
            if u >= 2:
                pe.wait_ge(y_done, u - 1)
            for b in range(q + 1):
                m = pe.matmul(ps[:, 6 + u % 2, 0:HD], pt[u % 2][:, b, :],
                              Tt[:, S_VF + j, b * P + r * HD:b * P + r * HD + HD], start=b == 0, stop=b == q)
            m.then_inc(pv, 1)

        pe.wait_ge(f_c, 1)
        for i in range(2 * H):
            if i >= 2:
                pe.wait_ge(cb_done, i - 1)
            pe.matmul(ps[:, 6 + i % 2, :], M["sel"][:, i // 2, :],
                      M["negc"][:, 512 * (i % 2):512 * (i % 2) + 512], start=True, stop=True).then_inc(cb_mm, 1)
        pe.wait_ge(cb_done, 2 * H)
        scores(0)
        for u in range(NU + 2):
            if u + 1 < NU:
                scores(u + 1)
            if u < NU:
                pe.wait_ge(p_done, u + 1)
                for g in fox_groups[u]:
                    turn(g)
            if 1 <= u <= NU:
                values(u - 1)
            if u - 2 in y_group:
                pe.wait_ge(y_done, u - 1)
                turn(y_group[u - 2])

        for n in range(NCH):
            k0 = P if n == 0 else 0
            if n >= 1:
                pe.wait_ge(ws_exp, 9 * n)
            for h in range(H):
                r, j = h // 4, h % 4
                lo = r * HD
                out = ps[:, h // 2, 256 * (h % 2) + k0:256 * (h % 2) + 256]
                pe.matmul(out, Tt[lo:lo + HD, S_QS + j, n * P:n * P + P],
                          Tt[lo:lo + HD, S_KS, (n - 1) * P + k0:(n + 1) * P], start=True, stop=False)
                m = pe.matmul(out, M["slope"][:, h, :], M["swa_mask"][:, k0:], start=False, stop=True)
            m.then_inc(ws_done, 1)
            pe.wait_ge(ws_exp, 9 * n + 9)
            for g in sp_groups[n]:
                turn(g)
            for g in sp_groups[n]:
                pe.wait_ge(t_copied[g % 2], g // 2 + 1)
            if n >= 1:
                pe.wait_ge(ws_y, n)
            for h in range(H):
                r = h // 4
                for kb in range(1 if n == 0 else 0, 2):
                    c = n - 1 + kb
                    m = pe.matmul(ps[:, 6, HD * h:HD * h + HD], M["spt"][:, 2 * h + kb, :],
                                  Tt[:, S_VS, c * P + r * HD:c * P + r * HD + HD],
                                  start=kb == (1 if n == 0 else 0), stop=kb == 1)
            m.then_inc(ws_pv, 1)
            pe.wait_ge(ws_y, n + 1)
            turn(sy_group[n])

    @block.vector
    def _(dve):
        fz, ft = M["fz"], M["ft"]
        nc.vector.tensor_copy(M["ident_b"][:], ident[:])
        nc.vector.tensor_copy(M["fox_mask"][:], M["masks"][:, 256:384])
        nc.vector.tensor_copy(M["swa_mask"][:], M["masks"][:, 0:256])
        for h in range(H):
            nc.vector.tensor_scalar(M["slope"][:, h, :], ident[:], M["masks"][:, 512 + h:513 + h], None, ALU.mult)
        dve.wait_ge(f_ln, 1)
        nc.vector.scalar_tensor_tensor(fz[:], fz[:], 0.0, ft[:], ALU.min, ALU.subtract).then_inc(f_z, 1)
        nc.vector.memset(M["ones_t"][:], 1.0).then_inc(f_z, 1)
        dve.wait_ge(f_z, 2)
        nc.vector.tensor_tensor_scan(ft[:], M["ones_t"][:], fz[:], 0.0, ALU.mult, ALU.add).then_inc(f_z, 1)
        dve.wait_ge(f_z, 3)
        nc.vector.tensor_scalar(M["negc"][:], ft[:], -1.0 / SC, None, ALU.mult).then_inc(f_c, 1)

        def copy_group(g):
            kind = groups[g][0]
            bank = ps[:, 4 + g % 2, :]
            if kind == "p":
                _, u, a, nblk = groups[g]
                if a == 0:
                    dve.wait_ge(t_done, g + 1)
                    if u >= 2:
                        dve.wait_ge(pv, u - 1)
                    copied(nc.vector.tensor_copy(pt[u % 2][:, 0:nblk, :].rearrange("p a b -> p (a b)"),
                                                 bank[:, 0:P * nblk]), g)
            elif kind == "y":
                _, j, q = groups[g]
                dve.wait_ge(y_hi, j * NCH + q + 1)
                copied(nc.vector.tensor_tensor(yT_fox[:, j, q, 1, :], bank[:, 0:P], yT_fox[:, j, q, 0, :],
                                               ALU.subtract), g)
            elif kind == "sp":
                _, n, a, nblk = groups[g]
                if a < 8:
                    dve.wait_ge(t_done, g + 1)
                    if n >= 1:
                        dve.wait_ge(ws_pv, n)
                    copied(nc.vector.tensor_copy(M["spt"][:, a:a + 4, :].rearrange("p a b -> p (a b)"), bank), g)
            else:
                _, n = groups[g]
                dve.wait_ge(y_hi, 4 * NCH + n + 1)
                copied(nc.vector.tensor_tensor(yT_swa[:, :, n, 1, :], bank.rearrange("p (a b) -> p a b", a=4),
                                               yT_swa[:, :, n, 0, :], ALU.subtract), g)

        def finish(u):
            j, q, r = units[u]
            dve.wait_ge(p_done, u + 1)
            nc.vector.reciprocal(rsum[:, u % 4:u % 4 + 1], rsum[:, u % 4:u % 4 + 1])
            dve.drain()
            dve.wait_ge(pv, u + 1)
            c = q * P + r * HD
            nc.vector.tensor_scalar(Tt[:, S_QF + j, c:c + HD], ps[:, 6 + u % 2, 0:HD],
                                    rsum[:, u % 4:u % 4 + 1], None, ALU.mult).then_inc(y_done, 1)

        dve.wait_ge(cb_done, 2 * H)
        for u in range(NU + 3):
            if u < NU:
                j, q, r = units[u]
                W = (q + 1) * P
                b0 = scores_bank(u)
                dve.wait_ge(s_done, u + 1)
                if u >= 3:
                    dve.wait_ge(t_done, fox_groups[u - 3][-1] + 1)
                nc.vector.tensor_tensor_reduce(
                    sb[u % 3][:, 0:W], ps[:, b0:b0 + 2, :].rearrange("p a b -> p (a b)")[:, 0:W],
                    cb[:, 2 * j + r, 0:W], -SC, 3e38, ALU.add, ALU.min, nb[:, u % 4:u % 4 + 1]).then_inc(s_read, 1)
            if 1 <= u <= NU:
                for g in fox_groups[u - 1]:
                    copy_group(g)
            if 2 <= u <= NU + 1:
                finish(u - 2)
            if u - 3 in y_group:
                copy_group(y_group[u - 3])

        nc.vector.memset(M["sp"][:, :, 0:P], 0.0)
        for n in range(NCH):
            k0 = P if n == 0 else 0
            dve.wait_ge(ws_done, n + 1)
            nc.vector.tensor_reduce(M["wmx"][:], ps[:, 0:4, :].rearrange("p a (b c) -> p (a b) c", b=2)[:, :, k0:],
                                    AX.X, ALU.max)
            dve.drain()
            nc.vector.scalar_tensor_tensor(M["wnb"][:], M["wmx"][:], SC, M["sinks"][:], ALU.mult, ALU.max)
            dve.drain()
            nc.vector.tensor_tensor(M["snb"][:], M["sinks"][:], M["wnb"][:], ALU.subtract).then_inc(ws_max, 1)
            dve.drain()
            nc.vector.tensor_scalar(M["wnb"][:], M["wnb"][:], -1.0, None, ALU.mult).then_inc(ws_max, 1)
            for g in sp_groups[n][:2]:
                copy_group(g)
            dve.wait_ge(ws_exp, 9 * n + 9)
            nc.vector.tensor_tensor(M["wden"][:], M["wrs"][:], M["es"][:], ALU.add)
            dve.drain()
            nc.vector.reciprocal(M["wden"][:], M["wden"][:])
            dve.drain()
            dve.wait_ge(ws_pv, n + 1)
            for r in range(2):
                ins = nc.vector.tensor_tensor(
                    Tt[:, S_QS:S_QS + 4, n * P + r * HD:n * P + r * HD + HD],
                    ps[:, 6, 256 * r:256 * r + 256].rearrange("p (a b) -> p a b", a=4),
                    M["wden"][:, 4 * r:4 * r + 4].rearrange("p (a o) -> p a o", o=1).to_broadcast([P, 4, HD]),
                    ALU.mult)
            ins.then_inc(ws_y, 1)
            copy_group(sy_group[n])


def merge(nc, ctx, M, A):
    sem = lambda n: ctx.enter_context(nc.semaphore(n))
    Tt, ps, xh, xl, sf, sh, sl, sg, tmp = (M[n] for n in "T ps xh xl sf sh sl sg tmp".split())
    yT = [M[n] for n in ("yT_fox", "yT_pool", "yT_conv", "yT_swa")]
    s_in = [sem("strip_in0"), sem("strip_in1")]
    scaled, ready, strip_used = sem("strip_scaled"), sem("strip_ready"), sem("strip_used")
    gate_mm, y_mm, gate, product = sem("gate_mm"), sem("y_mm"), sem("gate"), sem("product")
    free = sem("banks_free")
    block = ctx.enter_context(nc.Block())

    @block.sync
    def _(sp):
        for s in range(2):
            sp.dma_start(sf[s][:], A["strips"][s]).then_inc(s_in[s], 16)
        with sp.Fori(1, NQ * NB // 2) as i:
            for s in range(2):
                sp.wait_ge(ready, 2 * i + (s - 1))
                sp.dma_start(sf[s][:], A["strips"][bass.ds(2 * i + s, 1)].rearrange("o p k c -> p (o k) c")
                             ).then_inc(s_in[s], 16)

    @block.scalar
    def _(act):
        def split(i, s):
            act.wait_ge(s_in[s], 8 * i + (16 - 8 * s))
            act.activation(sh[s][:], sf[s][:], ACT.Copy, scale=WS)
            act.activation(sf[s][:], sf[s][:], ACT.Copy, scale=WS).then_inc(scaled, 1)

        def strips(cq, last):
            for b in range(NB):
                if b < NB - 1 or not last:
                    act.wait_ge(free, 32 * cq + (8 * b + 4))
                    split(4 * cq + (b + 1), (b + 1) % 2)
                for c in range(NCH):
                    i = 32 * cq + (8 * b + c)
                    act.wait_ge(gate_mm, i + 1)
                    act.wait_ge(free, i + 1)
                    act.activation(sg[c % 4][:], ps[:, c % 4, 0:CW], ACT.Sigmoid, scale=RWS).then_inc(gate, 1)

        split(0, 0)
        with act.Fori(0, NQ - 1) as cq:
            strips(cq, False)
        strips(NQ - 1, True)

    @block.gpsimd
    def _(pool):
        with pool.Fori(0, NQ * NB // 2) as i:
            for s in range(2):
                await_ge(pool, scaled, 2 * i + (s + 1))
                nc.gpsimd.tensor_tensor(sl[s][:], sf[s][:], sh[s][:], ALU.subtract).then_inc(ready, 1)

    @block.tensor
    def _(pe):
        with pe.Fori(0, NQ) as cq:
            for b in range(NB):
                s = b % 2
                pe.wait_ge(ready, 4 * cq + (b + 1))
                for c in range(NCH):
                    i = 32 * cq + (8 * b + c)
                    tok = slice(P * c, P * c + P)
                    pe.wait_ge(free, i + 1)
                    for k in range(KD):
                        m = mm3(pe, ps[:, c % 4, 0:CW], xh[:, k, tok], xl[:, k, tok], sh[s][:, k, :],
                                sl[s][:, k, :], k == 0, k == KD - 1)
                    m.then_inc(gate_mm, 1)
                    for j in range(4):
                        m = mm3(pe, ps[:, 4 + c % 4, 0:CW], yT[b][:, j, c, 0, :], yT[b][:, j, c, 1, :],
                                sh[s][:, KD + j, :], sl[s][:, KD + j, :], j == 0, j == 3)
                    m.then_inc(y_mm, 1)

    @block.vector
    def _(dve):
        nc.vector.memset(tmp[0][:], 0.0).then_inc(free, 4)
        with dve.Fori(0, NQ) as cq:
            for b in range(NB):
                for c in range(NCH):
                    i = 32 * cq + (8 * b + c)
                    out = Tt[:, S_X1 + c, bass.ds(cq * CW, CW)]
                    dve.wait_ge(gate, i + 1)
                    dve.wait_ge(y_mm, i + 1)
                    if b == 0:
                        nc.vector.scalar_tensor_tensor(out, ps[:, 4 + c % 4, 0:CW], RWS, sg[c % 4][:],
                                                       ALU.mult, ALU.mult).then_inc(free, 1)
                    else:
                        nc.vector.scalar_tensor_tensor(tmp[c % 2][:], ps[:, 4 + c % 4, 0:CW], RWS, sg[c % 4][:],
                                                       ALU.mult, ALU.mult).then_inc(free, 1)
                        dve.wait_ge(free, i + 5)
                        nc.vector.tensor_tensor(out, out, tmp[c % 2][:], ALU.add)


def layer_norm(nc, dve, M, row, rstd_wait, gain, shift, out):
    st, mv = M["st"], M["mv"]
    for i in range(2):
        nc.vector.bn_stats(st[:, i, :], row[:, 512 * i:512 * i + 512])
    dve.drain()
    nc.vector.bn_aggr(mv[:], st[:].rearrange("p a b -> p (a b)")).then_inc(M["var_done"], 1)
    rstd_wait()
    nc.vector.reciprocal(M["rstd"][:], M["std"][:])
    nc.vector.scalar_tensor_tensor(row, row, mv[:, 0:1], gain, ALU.subtract, ALU.mult)
    dve.drain()
    return nc.vector.scalar_tensor_tensor(out, row, M["rstd"][:, 0:1], shift, ALU.mult, ALU.add)


def first_norm(nc, ctx, M, A):
    sem = lambda n: ctx.enter_context(nc.semaphore(n))
    Tt, ps, ident, mh, ml, row = (M[n] for n in "T ps ident mh ml row".split())
    wo, wq = M["wo"], M["wq"]
    wof = [Tt[:, 8 + i, :] for i in range(2)]
    wqf = [Tt[:, 10 + i, :].rearrange("p (k c) -> p k c", k=KD) for i in range(2)]
    xin = [Tt[:, 20 + i, :] for i in range(2)]
    wo_in, wq_in, x_in = ([sem(f"{n}{i}") for i in range(2)] for n in ("wo_in", "wq_in", "xc_in"))
    ln_in = sem("ln_in")
    wo_scaled, wo_ready, wq_scaled, wq_ready = (sem(n) for n in "wo_scaled wo_ready wq_scaled wq_ready".split())
    turned, m_hi, m_lo, mix, summed, root = (sem(n) for n in "turned m_hi m_lo mix_mm summed root".split())
    M["var_done"] = sem("var_done")
    x1_done = sem("x1_done")
    block = ctx.enter_context(nc.Block())

    @block.sync
    def _(sp):
        for i in range(2):
            sp.dma_start(wof[i], A["w_o"][i]).then_inc(wo_in[i], 16)
            sp.dma_start(xin[i], A["x"][P * i:P * i + P]).then_inc(x_in[i], 16)
        for k in range(2, KD):
            sp.wait_ge(wo_ready, k - 1)
            sp.dma_start(wof[k % 2], A["w_o"][k]).then_inc(wo_in[k % 2], 16)
        sp.dma_start(M["ln"][:], A["ln"][:, 0:2]).then_inc(ln_in, 16)
        sp.dma_start(M["tok"][:], A["tok"]).then_inc(ln_in, 16)
        sp.dma_start(M["kt"][:, 0, :], A["k1_t"]).then_inc(ln_in, 16)
        sp.dma_start(M["kt"][:, 1, :], A["k2_t"]).then_inc(ln_in, 16)
        sp.dma_start(M["iota"][:], A["iota"]).then_inc(ln_in, 16)
        for c in range(NCH):
            for i in range(2):
                if c:
                    sp.wait_ge(wq_ready, 2 * c + i - 1)
                sp.dma_start(wqf[i], A["w_q"][2 * c + i]).then_inc(wq_in[i], 16)
            if 1 <= c < NCH - 1:
                sp.wait_ge(summed, c)
                sp.dma_start(xin[(c + 1) % 2], A["x"][P * (c + 1):P * (c + 2)]).then_inc(x_in[(c + 1) % 2], 16)
        sp.wait_ge(ln_in, 80)

    @block.scalar
    def _(act):
        for k in range(KD):
            act.wait_ge(wo_in[k % 2], 16 * (k // 2 + 1))
            act.activation(wo[:, k, 0, :], wof[k % 2], ACT.Copy, scale=WS)
            act.activation(wof[k % 2], wof[k % 2], ACT.Copy, scale=WS).then_inc(wo_scaled, 1)
        for c in range(NCH + 1):
            if c < NCH:
                act.wait_ge(turned, c + 1)
                if c >= 2:
                    act.wait_ge(mix, c - 1)
                act.activation(mh[c % 2][:], ps[:, 2 * (c % 2):2 * (c % 2) + 2, :].rearrange("p a b -> p (a b)"),
                               ACT.Copy).then_inc(m_hi, 1)
            if c:
                act.wait_ge(M["var_done"], c)
                act.activation(M["std"][:], M["mv"][:, 1:2], ACT.Sqrt, bias=M["eps"][:, 0:1]).then_inc(root, 1)
            for b in (2 * c, 2 * c + 1):
                if b < 2 * H:
                    act.wait_ge(wq_in[b % 2], 16 * (b // 2 + 1))
                    act.activation(wq[:, b, 0, :, :], wqf[b % 2], ACT.Copy, scale=WS)
                    act.activation(wqf[b % 2], wqf[b % 2], ACT.Copy, scale=WS).then_inc(wq_scaled, 1)

    @block.gpsimd
    def _(pool):
        for k in range(KD):
            pool.wait_ge(wo_scaled, k + 1)
            nc.gpsimd.tensor_tensor(wo[:, k, 1, :], wof[k % 2], wo[:, k, 0, :], ALU.subtract).then_inc(wo_ready, 1)
        for b in range(2 * H):
            pool.wait_ge(wq_scaled, b + 1)
            nc.gpsimd.tensor_tensor(wq[:, b, 1, :, :], wqf[b % 2], wq[:, b, 0, :, :], ALU.subtract).then_inc(wq_ready, 1)

    @block.tensor
    def _(pe):
        def turn(c):
            if c >= 2:
                pe.wait_ge(m_lo, c - 1)
            for k in range(KD):
                m = pe.transpose(ps[:, 2 * (c % 2) + k // 4, P * (k % 4):P * (k % 4) + P],
                                 Tt[:, S_X1 + c, P * k:P * k + P], ident[:])
            m.then_inc(turned, 1)

        turn(0)
        for c in range(NCH):
            if c + 1 < NCH:
                turn(c + 1)
            if c == 0:
                pe.wait_ge(wo_ready, KD)
            pe.wait_ge(m_lo, c + 1)
            if c >= 2:
                pe.wait_ge(summed, c - 1)
            for k in range(KD):
                for a, b in ((0, 0), (0, 1), (1, 0)):
                    lhs = (mh, ml)[a][c % 2][:, P * k:P * k + P]
                    for half in range(2):
                        m = pe.matmul(ps[:, 4 + 2 * (c % 2) + half, :], lhs, wo[:, k, b, 512 * half:512 * half + 512],
                                      start=k == a == b == 0, stop=k == KD - 1 and a == 1)
            m.then_inc(mix, 1)

    @block.vector
    def _(dve):
        for c in range(NCH + 1):
            if c < NCH:
                dve.wait_ge(m_hi, c + 1)
                nc.vector.tensor_tensor(ml[c % 2][:], ps[:, 2 * (c % 2):2 * (c % 2) + 2, :].rearrange("p a b -> p (a b)"),
                                        mh[c % 2][:], ALU.subtract).then_inc(m_lo, 1)
            if c:
                d = c - 1
                if d == 0:
                    dve.wait_ge(ln_in, 80)
                dve.wait_ge(x_in[d % 2], 16 * (d // 2 + 1))
                nc.vector.tensor_scalar(xin[d % 2], xin[d % 2], ALPHA, None, ALU.mult)
                dve.drain()
                dve.wait_ge(mix, d + 1)
                nc.vector.scalar_tensor_tensor(row[:], ps[:, 4 + 2 * (d % 2):6 + 2 * (d % 2), :].rearrange(
                    "p a b -> p (a b)"), RWS, xin[d % 2], ALU.mult, ALU.add).then_inc(summed, 1)
                dve.drain()
                layer_norm(nc, dve, M, row[:], lambda: dve.wait_ge(root, d + 1), M["ln"][:, 0, :], M["ln"][:, 1, :],
                           Tt[:, S_X1 + d, :]).then_inc(x1_done, 1)
                dve.drain()


def hidden(nc, ctx, M, A):
    sem = lambda n: ctx.enter_context(nc.semaphore(n))
    Tt, ps, ident, wq = (M[n] for n in "T ps ident wq".split())
    xc, xth, xtl, qt, sc, cand, oh, kt = (M[n] for n in "xc xth xtl qt sc cand oh kt".split())
    v16, ix, ixf, pos, posf, sel_a, sel_b = (M[n] for n in "v16 ix ixf pos posf sel_a sel_b".split())
    top, topj, gg, gsum, idx_next, idx, hid = (M[n] for n in "top topj gg gsum idx_next idx hid".split())
    ut, hout, place, put, tok = (M[n] for n in "ut hout place put tok".split())
    x1t = Tt[:, 0:4, :].rearrange("p a (b t) -> p (a b) t", b=2)
    weights_of = A["weights_flat"]
    ring = M["ring1"]
    NR = len(ring)
    landed = [sem(f"landed{i}") for i in range(NR)]
    free = sem("ring_free")
    chosen, copied_x, turned, x_hi, x_lo = (sem(n) for n in "chosen x1_copied x1_turned x1_hi x1_lo".split())
    q_mm, q_out, s_mm, s_out = (sem(n) for n in "q_mm q_out s_mm s_out".split())
    exp_in, exp_out, selected = (sem(n) for n in "exp_in exp_out selected".split())
    placed = sem("placed")
    scattered = sem("scattered")
    put_free = sem("put_free")
    dense_mm, dense_out = sem("dense_turned"), sem("dense_x1t")
    u_in = [sem(f"u_in{i}") for i in range(NU)]
    h_mm = sem("h_mm")
    h_out = sem("h_out")
    h_stored = [sem("h_stored0"), sem("h_stored1")]
    block = ctx.enter_context(nc.Block())

    @block.gpsimd
    def _(pool):
        with pool.Fori(0, ND) as g:
            await_ge(pool, chosen, g + 1)
            for i in range(NSEL):
                if i % 4 == 0:
                    await_ge(pool, free, NSEL * g + (i + 4))
                nc.gpsimd.indirect_dma_start(
                    ring[i % NR], None, A["u"], bass.IndirectOffsetOnAxis(ap=idx[:, i:i + 1], axis=0)
                ).then_inc(landed[i % NR], 16)
                if i == 64:
                    await_ge(pool, placed, g + 1)
                for e in (2 * i - 128, 2 * i - 127) if i >= 64 else ():
                    if e and e % TOPK == 0:
                        await_ge(pool, scattered, 16 * NSEL * g + 16 * e)
                    nc.gpsimd.indirect_dma_start(
                        weights_of, bass.IndirectOffsetOnAxis(ap=place[:, e:e + 1], axis=0), put[:, e:e + 1],
                        None, compute_op=ALU.add).then_inc(scattered, 16)
            await_ge(pool, scattered, 16 * NSEL * g + 16 * NSEL)
            pool.memset(M["mark"][:], 0.0).then_inc(put_free, 1)

    @block.sync
    def _(sp):
        def half_step(j, more):
            for i in range(16):
                if i < 16 - NU or more:
                    sp.wait_ge(h_mm, 16 * j + (i + 1))
                    sp.dma_start(ut[i % NU], A["u_t"][bass.ds(16 * j + (i + NU), 1)].rearrange("o p k c -> p (o k) c")
                                 ).then_inc(u_in[i % NU], 16)
                sp.wait_ge(h_out, 16 * j + (i + 5))
                sp.dma_start(A["h"][bass.ds(16 * j + i, 1)].rearrange("o p t -> p (o t)"), hout[i % 2][:]
                             ).then_inc(h_stored[i % 2], 16)

        for i in range(NU):
            sp.dma_start(ut[i], A["u_t"][i]).then_inc(u_in[i], 16)
        with sp.Fori(0, 7) as j:
            half_step(j, True)
        half_step(7, False)
        for i in range(2):
            sp.wait_ge(h_stored[i], 16 * 64 + 16)

    @block.tensor
    def _(pe):
        def table_block(j, i):
            pe.wait_ge(u_in[i % NU], (256 // NU) * j + 16 * (i // NU + 1))
            pe.wait_ge(h_out, 16 * j + (i + 1))
            for k in range(KD):
                m = pe.matmul(ps[:, 4 + i % 4, :], ut[i % NU][:, k, :], x1t[:, k, :], start=k == 0, stop=k == KD - 1)
            m.then_inc(h_mm, 1)

        def turn(n):
            pe.wait_ge(copied_x, n + 1)
            for k in range(KD):
                m = pe.transpose(ps[:, k // 4, P * (k % 4):P * (k % 4) + P], xc[:, P * k:P * k + P], ident[:])
            m.then_inc(turned, 1)

        def query_group(n, i):
            if i == 0:
                pe.wait_ge(x_lo, n + 1)
            if i >= 2:
                pe.wait_ge(q_out, 4 * n + (i - 1))
            for b in range(4 * i, 4 * i + 4):
                for k in range(KD):
                    m = mm3(pe, ps[:, 2 + i % 2, P * (b % 4):P * (b % 4) + P], wq[:, b, 0, k, :], wq[:, b, 1, k, :],
                            xth[:, P * k:P * k + P], xtl[:, P * k:P * k + P], k == 0, k == KD - 1)
            m.then_inc(q_mm, 1)

        def scores(n):
            pe.wait_ge(q_out, 4 * n + 4)
            for b in range(2 * H):
                m = pe.matmul(ps[:, b // 4, P * (b % 4):P * (b % 4) + P], qt[:, b, :], kt[:, b % 2, :],
                              start=True, stop=True)
                if b % 4 == 3:
                    m.then_inc(s_mm, 1)

        def queries(n):
            turn(n)
            for i in range(4):
                query_group(n, i)
            scores(n)

        def half_step(j, more):
            for i in range(16):
                table_block(j, i)
                if more:
                    if i == 1:
                        pe.wait_ge(s_out, 4 * j + 8)
                        turn(j + 2)
                    elif 2 <= i < 6:
                        query_group(j + 2, i - 2)
                    elif i == 6:
                        scores(j + 2)

        queries(0)
        for d in range(ND):
            if d >= 2:
                pe.wait_ge(dense_out, d - 1)
            for k in range(KD):
                m = pe.transpose(ps[:, 4 + 2 * (d % 2) + k // 4, P * (k % 4):P * (k % 4) + P],
                                 Tt[:, S_X1 + 2 * d + 1, P * k:P * k + P], ident[:])
            m.then_inc(dense_mm, 1)
        pe.wait_ge(s_out, 4)
        queries(1)
        with pe.Fori(0, 6) as j:
            half_step(j, True)
        with pe.Fori(6, 8) as j:
            half_step(j, False)

    @block.scalar
    def _(act):
        def copy_x(n):
            act.activation(xc[:], Tt[:, bass.ds(S_X1 + n, 1), :].rearrange("p o c -> p (o c)"), ACT.Copy
                           ).then_inc(copied_x, 1)

        def x_high(n):
            act.wait_ge(turned, n + 1)
            act.activation(xth[:], ps[:, 0:2, :].rearrange("p a b -> p (a b)"), ACT.Copy).then_inc(x_hi, 1)

        def query_group(n, i):
            act.wait_ge(q_mm, 4 * n + (i + 1))
            act.activation(qt[:, 4 * i:4 * i + 4, :].rearrange("p a b -> p (a b)"), ps[:, 2 + i % 2, :], ACT.Copy,
                           scale=RWS).then_inc(q_out, 1)

        def scores(n):
            for i in range(4):
                act.wait_ge(s_mm, 4 * n + (i + 1))
                act.activation(sc[:, 4 * i:4 * i + 4, :].rearrange("p a b -> p (a b)"), ps[:, i, :], ACT.Copy
                               ).then_inc(s_out, 1)

        def weights(n):
            act.wait_ge(exp_in, n + 1)
            act.activation(gg[:], gg[:], ACT.Exp).then_inc(exp_out, 1)

        def table_block(j, i):
            act.wait_ge(h_mm, 16 * j + (i + 1))
            act.wait_ge(h_stored[i % 2], 128 * j + 16 * (i // 2 + 1))
            act.activation(hout[i % 2][:], ps[:, 4 + i % 4, :], ACT.Gelu).then_inc(h_out, 1)

        def half_step(j, choose, more):
            for i in range(16):
                table_block(j, i)
                if i == 0 and choose:
                    act.wait_ge(selected, j + 1)
                    scores(j + 1)
                if i == 0 and more:
                    copy_x(j + 2)
                if i == 1 and more:
                    x_high(j + 2)
                if 2 <= i < 6 and more:
                    query_group(j + 2, i - 2)
                if i == 12 and choose:
                    weights(j + 1)

        copy_x(0)
        x_high(0)
        for i in range(4):
            query_group(0, i)
        scores(0)
        for d in range(ND):
            act.wait_ge(dense_mm, d + 1)
            act.activation(x1t[:, :, P * d:P * d + P],
                           ps[:, 4 + 2 * (d % 2):6 + 2 * (d % 2), :].rearrange("p a (k c) -> p (a k) c", c=P), ACT.Copy
                           ).then_inc(dense_out, 1)
        copy_x(1)
        x_high(1)
        act.activation(hout[0][0:1, 0:1], hout[0][0:1, 0:1], ACT.Copy, scale=0.0).then_inc(h_out, 4)
        for i in range(4):
            query_group(1, i)
        weights(0)
        with act.Fori(0, 6) as j:
            half_step(j, True, True)
        half_step(6, True, False)
        half_step(7, False, False)

    @block.vector
    def _(dve):
        def x_low(n):
            dve.wait_ge(x_hi, n + 1)
            nc.vector.tensor_tensor(xtl[:], ps[:, 0:2, :].rearrange("p a b -> p (a b)"), xth[:], ALU.subtract
                                    ).then_inc(x_lo, 1)

        def choose(k, n, dense):
            if k == 0:
                await_ge(dve, s_out, 4 * n + 4)
            if k < 16:
                nc.vector.max(v16[:, k, 0:8], sc[:, k, :])
                if k == 15:
                    dve.drain()
            elif k < 48:
                b = (k - 16) // 2
                if k % 2 == 0:
                    nc.vector.max_index(ix[:, b, 0:8], v16[:, b, 0:8], sc[:, b, :])
                else:
                    nc.vector.match_replace(sc[:, b, :], v16[:, b, 0:8], sc[:, b, :], -3e38)
                if k == 47:
                    dve.drain()
            elif k < 64:
                nc.vector.max(v16[:, k - 48, 8:16], sc[:, k - 48, :])
                if k == 63:
                    dve.drain()
            elif k < 80:
                nc.vector.max_index(ix[:, k - 64, 8:16], v16[:, k - 64, 8:16], sc[:, k - 64, :])
            elif k < 88:
                h = k - 80
                nc.vector.tensor_tensor(
                    cand[:, h, :].rearrange("p (a b) -> p a b", a=16),
                    v16[:, 2 * h, :].rearrange("p (a o) -> p a o", o=1).to_broadcast([P, 16, 16]),
                    v16[:, 2 * h + 1:2 * h + 2, :].to_broadcast([P, 16, 16]), ALU.add)
                if k == 87:
                    dve.drain()
            elif k < 96:
                nc.vector.max(top[:, k - 88, 0:8], cand[:, k - 88, :])
                if k == 95:
                    dve.drain()
            elif k < 112:
                h = (k - 96) // 2
                if k % 2 == 0:
                    nc.vector.max_index(pos[:, h, 0:8], top[:, h, 0:8], cand[:, h, :])
                else:
                    nc.vector.match_replace(cand[:, h, :], top[:, h, 0:8], cand[:, h, :], -3e38)
                if k == 111:
                    dve.drain()
            elif k < 120:
                nc.vector.max(top[:, k - 112, 8:16], cand[:, k - 112, :])
                if k == 119:
                    dve.drain()
            elif k < 128:
                nc.vector.max_index(pos[:, k - 120, 8:16], top[:, k - 120, 8:16], cand[:, k - 120, :])
                if k == 127:
                    dve.drain()
            elif k == 128:
                nc.vector.tensor_tensor(gg[:].rearrange("p (h k) -> p h k", h=H), top[:],
                                        top[:, :, 0:1].to_broadcast([P, H, TOPK]), ALU.subtract).then_inc(exp_in, 1)
                nc.vector.tensor_copy(ixf, ix[:])
                nc.vector.tensor_scalar(topj[:, 0, :], pos[:].rearrange("p h k -> p (h k)"), 4, None,
                                        ALU.logical_shift_right)
                nc.vector.tensor_scalar(topj[:, 1, :], pos[:].rearrange("p h k -> p (h k)"), 15, None,
                                        ALU.bitwise_and)
                dve.drain()
            elif k == 129:
                nc.vector.tensor_copy(posf, topj)
                dve.drain()
            elif k in (130, 134):
                s = (k - 130) // 4
                nc.vector.tensor_tensor(oh[:], posf[:, s, :].rearrange("p (a o) -> p a o", o=1).to_broadcast([P, NSEL, 16]),
                                        M["iota"][:].rearrange("p (o a) -> p o a", o=1).to_broadcast([P, NSEL, 16]),
                                        ALU.is_equal)
                dve.drain()
            elif k in (131, 135):
                s = (k - 131) // 4
                for h in range(H):
                    nc.vector.tensor_tensor(oh[:, 16 * h:16 * h + 16, :], oh[:, 16 * h:16 * h + 16, :],
                                            ixf[:, 2 * h + s:2 * h + s + 1, :].to_broadcast([P, 16, 16]), ALU.mult)
                dve.drain()
            elif k in (132, 136):
                s = (k - 132) // 4
                nc.vector.tensor_reduce((sel_a, sel_b)[s], oh[:], AX.X, ALU.add)
                dve.drain()
            elif k == 137:
                if dense is None:
                    nc.vector.scalar_tensor_tensor(idx_next[:], sel_a, float(NKEY), sel_b, ALU.mult, ALU.add)
                else:
                    nc.vector.scalar_tensor_tensor(sel_a, sel_a, float(NKEY), sel_b, ALU.mult, ALU.add)
                dve.wait_ge(exp_out, n + 1)
                nc.vector.tensor_reduce(gsum[:], gg[:].rearrange("p (h k) -> p h k", h=H), AX.X, ALU.add)
                dve.drain()
            elif k == 138:
                nc.vector.reciprocal(gsum[:], gsum[:])
                if dense is not None:
                    await_ge(dve, put_free, dense + 1)
                    nc.vector.tensor_scalar(place[:], sel_a, float(DT), tok[:, 0:1], ALU.mult, ALU.add)
                dve.drain()
            elif k == 139:
                nc.vector.tensor_tensor((gg if dense is None else put)[:].rearrange("p (h k) -> p h k", h=H),
                                        gg[:].rearrange("p (h k) -> p h k", h=H),
                                        gsum[:].rearrange("p (h o) -> p h o", o=1).to_broadcast([P, H, TOPK]),
                                        ALU.mult).then_inc(selected, 1)
                if dense is not None:
                    nc.vector.tensor_scalar(tok[:], tok[:], float(P), None, ALU.add).then_inc(placed, 1)
                dve.drain()

        def rows(g, more):
            x1 = M["x1c"][:]
            nc.vector.tensor_copy(x1, Tt[:, bass.ds(S_X1 + 2 * g, 1), :].rearrange("p o c -> p (o c)"))
            dve.drain()
            for e in range(NSEL):
                half, r = divmod(e, 64)
                dve.wait_ge(landed[e % NR], (16 * NSEL // NR) * g + 16 * (e // NR + 1))
                nc.vector.tensor_tensor_reduce(ring[e % NR], ring[e % NR], x1, 1.0, 0.0, ALU.mult, ALU.add,
                                               hid[:, e:e + 1]).then_inc(free, 1)
                if r == 14 and more:
                    x_low(2 * g + (half + 2))
                if r >= 6 and (more or not half):
                    for k in range(3 * r - 18, min(3 * r - 15, 140)):
                        choose(k, 2 * g + (half + 1), g if half == 0 else None)
            if more:
                nc.vector.tensor_copy(idx[:], idx_next[:]).then_inc(chosen, 1)
                keep_choice(g + 1)
            dve.drain()
            nc.vector.tensor_copy(M["hid_all"][:, bass.ds(g, 1), :].rearrange("p o e -> p (o e)"), hid[:])

        def keep_choice(g):
            nc.vector.tensor_copy(M["idx_all"][:, bass.ds(g, 1), :].rearrange("p o e -> p (o e)"), idx_next[:])
            nc.vector.tensor_copy(M["gg_all"][:, bass.ds(g, 1), :].rearrange("p o e -> p (o e)"), gg[:])

        nc.vector.memset(hid[:], 0.0).then_inc(free, NR)
        nc.vector.memset(put[:], 0.0).then_inc(put_free, 1)
        for i in range(2):
            nc.vector.memset(hout[i][:], 0.0).then_inc(h_stored[i], 16)
        x_low(0)
        for k in range(140):
            choose(k, 0, None)
            if k == 20:
                x_low(1)
        nc.vector.tensor_copy(idx[:], idx_next[:]).then_inc(chosen, 1)
        keep_choice(0)
        with dve.Fori(0, ND - 1) as g:
            rows(g, True)
        rows(ND - 1, False)


def values(nc, ctx, M, A, out):
    sem = lambda n: ctx.enter_context(nc.semaphore(n))
    Tt, ps = M["T"], M["ps"]
    idx, wgt, wgt_all, acc, res, ring = (M[n] for n in "idx2 wgt wgt_all acc res ring2".split())
    vt, gt, ht, wt = (M[n] for n in "vt gt ht wt".split())
    NR = len(ring)
    landed = [sem(f"v_landed{i}") for i in range(NR)]
    free = sem("v_ring_free")
    chosen = sem("v_indices")
    gelu, root, row_done, ln_in = (sem(n) for n in "gelu root2 row_done ln2_in".split())
    v_in, gh_in = ([sem(f"{n}{i}") for i in range(4)] for n in ("v_in", "gh_in"))
    ready = sem("block_weights")
    used = sem("block_used")
    stored = sem("res_free")
    M["var_done"] = sem("var2_done")
    block = ctx.enter_context(nc.Block())

    @block.gpsimd
    def _(pool):
        with pool.Fori(0, ND) as g:
            for i in range(NSEL):
                if i % 64 == 0:
                    await_ge(pool, chosen, 2 * g + (i // 64 + 1))
                if i % 4 == 0:
                    await_ge(pool, free, NSEL * g + (i + 4))
                nc.gpsimd.indirect_dma_start(
                    ring[i % NR], None, A["v"], bass.IndirectOffsetOnAxis(ap=idx[:, i:i + 1], axis=0)
                ).then_inc(landed[i % NR], 16)

    @block.sync
    def _(sp):
        def load(q, i):
            b = bass.ds(4 * q + i, 1)
            sp.dma_start(gt[i], A["weights"][b].rearrange("o p t -> p (o t)")).then_inc(gh_in[i], 16)
            sp.dma_start(ht[i], A["h"][b].rearrange("o p t -> p (o t)")).then_inc(gh_in[i], 16)
            sp.dma_start(vt[i], A["v_blocks"][b].rearrange("o p c -> p (o c)")).then_inc(v_in[i], 16)

        for i in range(4):
            load(0, i)
        sp.dma_start(M["ln2"][:], A["ln"][:, 2:4]).then_inc(ln_in, 16)
        with sp.Fori(1, 32) as q:
            for i in range(4):
                sp.wait_ge(used, 4 * q + (i + 1))
                load(q, i)

    @block.tensor
    def _(pe):
        def blocks(q, first=False, last=False):
            for i in range(4):
                pe.wait_ge(v_in[i], 16 * q + 16)
                pe.wait_ge(ready, 4 * q + (i + 1))
                for t in range(ND):
                    for half in range(2):
                        m = pe.matmul(ps[:, 2 * t + half, :], wt[i][:, P * t:P * t + P],
                                      vt[i][:, 512 * half:512 * half + 512],
                                      start=first and i == 0, stop=last and i == 3)
                m.then_inc(used, 1)

        blocks(0, first=True)
        with pe.Fori(1, 31) as q:
            blocks(q)
        blocks(31, last=True)

    @block.scalar
    def _(act):
        def finish(c, rows):
            act.wait_ge(M["var_done"], c + 1)
            act.activation(M["std"][:], M["mv"][:, 1:2], ACT.Sqrt, bias=M["eps"][:, 0:1]).then_inc(root, 1)
            act.wait_ge(row_done, c + 1)
            act.dma_start(out[rows, :], res[:]).then_inc(stored, 16)

        act.activation(M["act_all"][:], M["hid_all"][:].rearrange("p g e -> p (g e)"), ACT.Gelu).then_inc(gelu, 1)
        with act.Fori(0, ND) as g:
            finish(g, bass.ds(2 * P * g, P))
        for d in range(ND):
            finish(ND + d, slice((2 * d + 1) * P, (2 * d + 2) * P))
        act.wait_ge(stored, 16 * NCH + 16)

    @block.vector
    def _(dve):
        def indices(g, half):
            nc.vector.tensor_copy(idx[:, 64 * half:64 * half + 64],
                                  M["idx_all"][:, bass.ds(g, 1), 64 * half:64 * half + 64].rearrange("p o e -> p (o e)")
                                  ).then_inc(chosen, 1)

        def norm(c):
            dve.drain()
            def waits():
                dve.wait_ge(root, c + 1)
                dve.wait_ge(stored, 16 * c + 16)
            layer_norm(nc, dve, M, acc[0][:], waits, M["ln2"][:, 0, :], M["ln2"][:, 1, :], res[:]).then_inc(row_done, 1)

        def chunk(g, more):
            x1 = M["x1c"][:]
            nc.vector.tensor_copy(wgt[:], wgt_all[:, bass.ds(g, 1), :].rearrange("p o e -> p (o e)"))
            nc.vector.tensor_copy(x1, Tt[:, bass.ds(S_X1 + 2 * g, 1), :].rearrange("p o c -> p (o c)"))
            dve.drain()
            for e in range(NSEL):
                r = e % NR
                dve.wait_ge(landed[r], (16 * NSEL // NR) * g + 16 * (e // NR + 1))
                if e < 2:
                    nc.vector.tensor_scalar(acc[e][:], ring[r], wgt[:, e:e + 1], None, ALU.mult).then_inc(free, 1)
                else:
                    dve.wait_ge(free, NSEL * g + (NR + e - 1))
                    nc.vector.scalar_tensor_tensor(acc[e % 2][:], ring[r], wgt[:, e:e + 1], acc[e % 2][:],
                                                   ALU.mult, ALU.add).then_inc(free, 1)
                if e % 4 == 3:
                    i = e // 4
                    dve.wait_ge(gh_in[i % 4], 256 * g + 32 * (i // 4 + 1))
                    dve.wait_ge(used, 32 * g + (i + 1))
                    nc.vector.tensor_tensor(wt[i % 4], gt[i % 4], ht[i % 4], ALU.mult).then_inc(ready, 1)
                if more and e in (100, NSEL - 1):
                    indices(g + 1, int(e > 100))
            dve.drain()
            nc.vector.tensor_tensor(acc[0][:], acc[0][:], acc[1][:], ALU.add)
            dve.drain()
            nc.vector.scalar_tensor_tensor(acc[0][:], x1, ALPHA, acc[0][:], ALU.mult, ALU.add)
            norm(g)

        nc.vector.memset(acc[0][:], 0.0).then_inc(stored, 16)
        nc.vector.memset(acc[1][:], 0.0).then_inc(free, NR)
        nc.vector.memset(wgt[:], 0.0).then_inc(used, 4)
        indices(0, 0)
        indices(0, 1)
        dve.wait_ge(gelu, 1)
        dve.wait_ge(ln_in, 16)
        nc.vector.tensor_tensor(wgt_all[:].rearrange("p g e -> p (g e)"), M["gg_all"][:].rearrange("p g e -> p (g e)"),
                                M["act_all"][:], ALU.mult)
        dve.drain()
        with dve.Fori(0, ND - 1) as g:
            chunk(g, True)
        chunk(ND - 1, False)
        dve.wait_ge(used, 4 + 128)
        for d in range(ND):
            dve.drain()
            nc.vector.scalar_tensor_tensor(acc[0][:], Tt[:, S_X1 + 2 * d + 1, :], ALPHA,
                                           ps[:, 2 * d:2 * d + 2, :].rearrange("p a b -> p (a b)"), ALU.mult, ALU.add)
            norm(ND + d)


def build_mix(nc, ctx, A, out):
    keep = lambda n, s, d: ctx.enter_context(nc.sbuf_tensor(n, s, d))
    M = {}
    M["T"] = keep("tiles", [P, NSLOT, T], F32)
    M["ps"] = ctx.enter_context(nc.psum_tensor("ps", [P, 8, 512], F32))
    M["ident"] = keep("ident", [P, P], F32)
    M["eps"] = keep("eps", [P, 1], F32)
    Tt = M["T"]

    def pair_view(ap):
        return ap.bitcast(F16).rearrange("p j (q h c) -> p j q h c", q=NCH, h=2)

    M["yT_fox"] = pair_view(Tt[:, S_QF:S_QF + 4, :])
    M["yT_pool"] = pair_view(Tt[:, S_PO:S_PO + 4, :])
    M["yT_swa"] = pair_view(Tt[:, S_QS:S_QS + 4, :])
    A = dict(A)
    both = [nc.dram_tensor(n, (NEXP // P, P, DT), F32, kind="Internal").ap() for n in ("weights", "gelu_h")]
    A["weights"], A["h"] = both
    A["weights_flat"] = both[0].rearrange("b e (t o) -> (b e t) o", o=1)
    A["weights_rows"] = both[0].rearrange("(n a) e t -> n (a e t)", a=2).rearrange("n (p c) -> n p c", p=P)
    A["v_blocks"] = A["v"].rearrange("(b e) c -> b e c", e=P)
    with ExitStack() as early:
        sb = lambda n, s, d: early.enter_context(nc.sbuf_tensor(n, s, d))
        M["xh"], M["xl"] = sb("x_hi_t", [P, KD, T], F16), sb("x_lo_t", [P, KD, T], F16)
        hc_raw = sb("conv_in", [P, 4 * (T + CK - 1)], F32)
        M["hc"] = hc_raw[:].rearrange("p (g t) -> p g t", g=4)
        M["yT_conv"] = pair_view(hc_raw[:, 0:4 * T].rearrange("p (j t) -> p j t", j=4))
        M["fz"] = sb("forget", [H, T], F32)
        M["sinks"] = sb("sinks_sb", [P, H], F32)
        M["masks"] = sb("masks_sb", [P, 512 + H], F32)
        M["sel"] = sb("sel_sb", [H, H, P], F32)
        with ExitStack() as c1:
            s1 = lambda n, s, d: c1.enter_context(nc.sbuf_tensor(n, s, d))
            M["cacc"] = s1("conv_acc", [P, 4, T], F32)
            M["wf"] = [s1(f"w_f32_{i}", [P, KD, P], F32) for i in range(2)]
            M["wh"] = [s1(f"w_hi_{i}", [P, KD, P], F16) for i in range(2)]
            M["wl"] = [s1(f"w_lo_{i}", [P, KD, P], F16) for i in range(2)]
            M["pa"], M["pb"] = s1("window_a", [P, 16 + T], F32), s1("window_b", [P, 16 + T], F32)
            M["sq"] = [s1(f"square_{i}", [P, T], F32) for i in range(2)]
            M["rs"] = s1("conv_rstd", [P, T], F32)
            M["chan"] = s1("chan_sb", [P, 4, 4], F32)
            M["dw"] = s1("dw_sb", [P, 4, CK], F32)
            M["pw"] = s1("pool_w_sb", [P, 4, P], F32)
            M["rc"] = s1("rc_sb", [P, 4, 16], F32)
            M["p16"] = s1("p16", [P, 16], F32)
            M["bf"] = s1("b_f_sb", [H, 1], F32)
            M["fwf"] = s1("wf_f32", [P, KD, H], F32)
            M["fwh"], M["fwl"] = s1("wf_hi", [P, KD, H], F16), s1("wf_lo", [P, KD, H], F16)
            M["mean_w"] = s1("mean_w", [P, P], F32)
            M["const_loads"] = [
                (M["chan"][:], A["chan"]), (M["dw"][:], A["dw"]), (M["pw"][:], A["pool_w"]),
                (M["rc"][:], A["rc"]), (M["bf"][:], A["b_f"]), (M["fwf"][:], A["w_f"]),
                (M["sinks"][:], A["sinks"]), (M["masks"][:], A["masks"]), (M["sel"][:], A["sel"]),
                (M["ident"][:], A["masks"][:, 384:512])]
            project(nc, c1, M, A)
        with ExitStack() as c2:
            s2 = lambda n, s, d: c2.enter_context(nc.sbuf_tensor(n, s, d))
            M["cb"] = s2("decay", [P, H, T], F32)
            probs = s2("probs_sb", [P, 3, T], F32)
            M["sb"] = [probs[:, i, :] for i in range(3)]
            turned = s2("probs_t", [P, 16, P], F32)
            M["pt"] = [turned[:, 0:8, :], turned[:, 8:16, :]]
            M["ft"], M["ones_t"], M["negc"] = (probs[0:H, i, :] for i in range(3))
            M["sp"] = probs[:, 0:2, :].rearrange("p a (h k) -> p (a h) k", h=4)
            M["spt"] = turned
            M["nb"], M["rsum"] = s2("nb", [P, 4], F32), s2("rsum", [P, 4], F32)
            M["ident_b"] = s2("ident_b", [P, P], BF16)
            M["fox_mask"] = s2("fox_mask", [P, P], BF16)
            M["swa_mask"] = s2("swa_mask", [P, 2 * P], BF16)
            M["slope"] = s2("slope", [P, H, P], BF16)
            for n in "wmx wnb snb es wrs wden".split():
                M[n] = s2(n, [P, H], F32)
            M["zeros"] = s2("zeros", [P, 2 * DT], F32)
            attention(nc, c2, M, A)
        with ExitStack() as c3:
            s3 = lambda n, s, d: c3.enter_context(nc.sbuf_tensor(n, s, d))
            M["sf"] = [s3(f"strip_f32_{i}", [P, KD + 4, CW], F32) for i in range(2)]
            M["sh"] = [s3(f"strip_hi_{i}", [P, KD + 4, CW], F16) for i in range(2)]
            M["sl"] = [s3(f"strip_lo_{i}", [P, KD + 4, CW], F16) for i in range(2)]
            M["sg"] = [s3(f"gate_{i}", [P, CW], F32) for i in range(4)]
            M["tmp"] = [s3(f"product_{i}", [P, CW], F32) for i in range(2)]
            merge(nc, c3, M, A)
    with ExitStack() as late:
        sb = lambda n, s, d: late.enter_context(nc.sbuf_tensor(n, s, d))
        M["kt"] = sb("keys_t", [P, 2, NKEY], F32)
        M["iota"] = sb("iota_sb", [P, 16], F32)
        M["st"], M["mv"] = sb("bn_st", [P, 2, 6], F32), sb("bn_mv", [P, 2], F32)
        M["std"], M["rstd"] = sb("std", [P, 1], F32), sb("rstd", [P, 1], F32)
        for n, dt in (("idx_all", U32), ("gg_all", F32), ("hid_all", F32)):
            M[n] = sb(n, [P, ND, NSEL], dt)
        M["tok"] = sb("dense_token", [P, 1], F32)
        wq_ctx = late.enter_context(ExitStack())
        M["wq"] = wq_ctx.enter_context(nc.sbuf_tensor("wq_pairs", [P, 2 * H, 2, KD, P], F16))
        M["wo"] = Tt[:, S_WO:S_WO + 8, :].bitcast(F16).rearrange("p k (h c) -> p k h c", h=2)
        with ExitStack() as c4:
            s4 = lambda n, s, d: c4.enter_context(nc.sbuf_tensor(n, s, d))
            M["ln"] = s4("ln1_sb", [P, 2, D], F32)
            M["mh"] = [s4(f"m_hi_{i}", [P, D], F16) for i in range(2)]
            M["ml"] = [s4(f"m_lo_{i}", [P, D], F16) for i in range(2)]
            M["row"] = s4("row", [P, D], F32)
            first_norm(nc, c4, M, A)
        with ExitStack() as c5:
            s5 = lambda n, s, d: c5.enter_context(nc.sbuf_tensor(n, s, d))
            M["xth"], M["xtl"] = s5("x1t_hi", [P, D], F16), s5("x1t_lo", [P, D], F16)
            qc = s5("sums_of_keys", [P, 2 * H, P], F32)
            so = s5("scores_or_onehot", [P, 2 * H, NKEY], F32)
            M["qt"] = s5("queries", [P, 2 * H, P], F32)
            M["cand"] = qc[:].rearrange("p (h a) b -> p h (a b)", a=2)
            M["sc"], M["oh"] = so, so[:].rearrange("p a (b c) -> p (a b) c", c=16)
            M["v16"], M["ix"] = s5("best_keys", [P, 2 * H, 16], F32), s5("best_key_ids", [P, 2 * H, 16], U32)
            M["top"], M["pos"] = s5("best_sums", [P, H, 16], F32), s5("best_places", [P, H, 16], U32)
            M["ixf"] = qc[:, 0:2, :].rearrange("p a (b c) -> p (a b) c", c=16)
            M["topj"], M["posf"] = qc[:, 2:4, :].bitcast(U32), qc[:, 4:6, :]
            M["sel_a"], M["sel_b"] = qc[:, 6, :], qc[:, 7, :]
            M["x1c"], M["xc"] = s5("x1_rows", [P, D], F32), s5("x1_chunk", [P, D], F32)
            for n in "gg hid put".split():
                M[n] = s5(n, [P, NSEL], F32)
            M["gsum"], M["mark"] = s5("gsum", [P, H], F32), s5("mark", [P, 1], F32)
            for n in "idx_next idx place".split():
                M[n] = s5(n, [P, NSEL], U32)
            M["hout"] = [s5(f"gelu_out{i}", [P, DT], F32) for i in range(2)]
            M["ut"] = [Tt[:, 4 + i, :].rearrange("p (k e) -> p k e", k=KD) for i in range(NU)]
            M["ring1"] = [Tt[:, i, :] for i in (6, 7, 8, 9, 10, 11, 20, 21)]
            hidden(nc, c5, M, A)
        wq_ctx.close()
        with ExitStack() as c6:
            s6 = lambda n, s, d: c6.enter_context(nc.sbuf_tensor(n, s, d))
            M["ln2"] = s6("ln2_sb", [P, 2, D], F32)
            M["acc"] = [s6(f"acc{i}", [P, D], F32) for i in range(2)]
            M["res"], M["x1c"] = s6("result", [P, D], F32), s6("x1_rows2", [P, D], F32)
            M["wgt"], M["wgt_all"] = s6("wgt", [P, NSEL], F32), s6("wgt_all", [P, ND, NSEL], F32)
            M["act_all"] = s6("act_all", [P, ND * NSEL], F32)
            M["idx2"] = s6("v_idx", [P, NSEL], U32)
            M["vt"] = [s6(f"v_block{i}", [P, D], F32)[:] for i in range(4)]
            for n in ("gt", "ht", "wt"):
                M[n] = [s6(f"{n}_block{i}", [P, DT], F32)[:] for i in range(4)]
            extra = [s6(f"ring_extra{i}", [P, D], F32) for i in range(2)]
            M["ring2"] = [Tt[:, i, :] for i in list(range(12)) + [20, 21]] + [e[:] for e in extra]
            values(nc, c6, M, A, out)


def layout(x, w_in, b_f, swa_sinks, pool_w, pool_scale, dw_w, dw_b, conv_ln_g, conv_ln_b,
           p_fox, p_swa, p_pool, p_conv, w_out, ln1_g, ln1_b,
           peer_wq, peer_k1, peer_k2, peer_u, peer_v, ln2_g, ln2_b):
    x = np.asarray(x)[0]
    w = np.asarray(w_in)[0]
    sizes = [512, 512, 512, 8, 512, 128, 128, 512, 512, 512, 4 * D]
    names = "qf kf vf f qs ks vs po ca cg gl".split()
    at = dict(zip(names, zip(np.cumsum([0] + sizes[:-1]), sizes)))
    cols = {n: w[:, a:a + s] for n, (a, s) in at.items()}
    swa = np.concatenate([np.r_[j * HD:(j + 1) * HD, (4 + j) * HD:(5 + j) * HD] for j in range(4)])
    cols["qs"] = cols["qs"][:, swa]
    wt = np.concatenate([cols[n] for n in "ca cg po qs qf kf ks vf vs".split()], 1)
    assert wt.shape[1] == B_ALL * P

    def kblocks(m, width):
        k = m.shape[0] // P
        return m.reshape(k, P, -1, width).transpose(2, 1, 0, 3)

    def rows(v):
        return np.broadcast_to(np.asarray(v)[0][None, :], (P, np.asarray(v).shape[1]))

    def chans(v):
        return np.asarray(v)[0].reshape(-1, P).T

    gl = cols["gl"].reshape(D, NB, D)
    ps_ = {"fox": np.asarray(p_fox)[0], "pool": np.asarray(p_pool)[0], "conv": np.asarray(p_conv)[0],
           "swa": np.asarray(p_swa)[0][swa]}
    strips = np.stack([np.concatenate([kblocks(gl[:, b], CW), kblocks(ps_[n], CW)], 2)
                       for b, n in enumerate(["fox", "pool", "conv", "swa"])], 1)
    i, j = np.arange(P)[:, None], np.arange(2 * P)[None, :]
    dist = i + P - j
    swa_mask = np.where((dist >= 0) & (dist < P), -8.0 * dist, -1e30)
    fox_mask = np.where(np.arange(P)[None, :] <= i, 0.0, -1e30)
    slopes = np.repeat(2.0 ** -np.arange(1, H + 1)[None, :], P, 0)
    masks = np.concatenate([swa_mask, fox_mask, np.eye(P), slopes], 1)
    sel = np.zeros((H, H, P))
    for h in range(H):
        sel[h, h] = 1.0
    rc = np.zeros((P, 4, 16))
    for g in range(4):
        rc[:, g] = 1.0 / np.minimum(np.arange(1, 17), 2 ** (g + 1))
    out = {
        "x": x, "x_t": x.T.reshape(KD, P, T).transpose(1, 0, 2),
        "w_t": kblocks(wt, P), "w_f": kblocks(cols["f"], H)[0],
        "strips": strips.reshape(NQ * NB, P, 12, CW),
        "w_o": np.asarray(w_out)[0].reshape(KD, P, D),
        "w_q": kblocks(np.asarray(peer_wq)[0], P),
        "b_f": np.asarray(b_f)[0][:, None], "sinks": rows(swa_sinks),
        "pool_w": np.asarray(pool_w)[0].transpose(1, 0, 2),
        "chan": np.stack([chans(dw_b), chans(conv_ln_g), chans(conv_ln_b), chans(pool_scale)], 1),
        "dw": np.asarray(dw_w)[0].reshape(CK, 4, P).transpose(2, 1, 0),
        "ln": np.stack([rows(ln1_g), rows(ln1_b), rows(ln2_g), rows(ln2_b)], 1),
        "k1_t": np.asarray(peer_k1)[0].T, "k2_t": np.asarray(peer_k2)[0].T,
        "u_t": np.asarray(peer_u)[0].reshape(NEXP // P, P, KD, P).transpose(0, 3, 2, 1),
        "tok": np.arange(float(P))[:, None],
        "u": np.asarray(peer_u)[0], "v": np.asarray(peer_v)[0],
        "masks": masks, "sel": sel, "rc": rc,
        "iota": np.repeat(np.arange(16.0)[None, :], P, 0),
    }
    return {n: np.ascontiguousarray(a, np.float32) for n, a in out.items()}


def kernel(**inputs):
    import concourse.bacc as bacc
    from concourse.bass_utils import run_bass_kernel_spmd

    nc = bacc.Bacc("TRN2", target_bir_lowering=False, num_devices=1)
    arrays = layout(**inputs)
    A = {n: nc.dram_tensor(n, a.shape, mybir.dt.from_np(a.dtype), kind="ExternalInput").ap()
         for n, a in arrays.items()}
    out = nc.dram_tensor("out", (T, D), F32, kind="ExternalOutput").ap()
    with ExitStack() as ctx:
        build_mix(nc, ctx, A, out)
    r = run_bass_kernel_spmd(nc, [arrays], core_ids=[0])
    return r.results[0]["out"].reshape(1, T, D)
```

```python
from contextlib import ExitStack

import concourse.bass as bass
from concourse import mybir
import numpy as np

ALU = mybir.AluOpType
ACT = mybir.ActivationFunctionType
AX = mybir.AxisListType
F32 = mybir.dt.float32
F16 = mybir.dt.float16
BF16 = mybir.dt.bfloat16
U32 = mybir.dt.uint32

P = 128
D = 1024
T = 1024
KD = D // P
NCH = T // P
H = 8
HD = 64
CK = 31
NB = 4
TOPK = 16
NKEY = 128
NSEL = H * TOPK
NEXP = NKEY * NKEY
ND = NCH // 2
DT = ND * P
NU = 2
NV = 8
DENSE_AT = [90, 96, 102, 108]
SC = 0.125
EPS = 1e-5
ALPHA = 2.0 ** 0.25
WS = 256.0
RWS = 1.0 / WS

B_T = 25
B_ALL = 30
S_PO, S_QS, S_QF, S_KF, S_KS, S_VF, S_VS = 0, 4, 8, 12, 16, 17, 21
S_CA, S_CG = S_QF, S_KF
NSLOT = 22
S_X1 = 12
S_WOF = 20
S_WO = 0
CW = 256
NQ = D // CW


def await_ge(eng, sem, value):
    eng.wait_ge(sem, value)
    if not isinstance(value, int):
        eng.nop(nofuse=True)


def mm3(pe, out, a_hi, a_lo, b_hi, b_lo, first, last):
    pe.matmul(out, a_hi, b_hi, start=first, stop=False)
    pe.matmul(out, a_hi, b_lo, start=False, stop=False)
    return pe.matmul(out, a_lo, b_hi, start=False, stop=last)


def project(nc, ctx, M, A):
    sem = lambda n: ctx.enter_context(nc.semaphore(n))
    Tt, xh, xl, hc, cacc, wf, wh, wl, pa, pb, sq, rs = (
        M[n] for n in "T xh xl hc cacc wf wh wl pa pb sq rs".split())
    ps = M["ps"]
    cv = M["chan"]
    yT_pool, yT_conv = M["yT_pool"], M["yT_conv"]
    w_in = [sem("w_in0"), sem("w_in1")]
    x_in = [sem(f"x_in{i}") for i in range(4)]
    c_in = sem("consts_in")
    x_hi, x_lo = sem("x_hi"), sem("x_lo")
    w_scaled, w_ready = sem("w_scaled"), sem("w_ready")
    unit_done, evac = sem("unit_done"), sem("evac")
    sig, h_done = sem("conv_sigmoid"), sem("conv_gated")
    tap = sem("conv_tap")
    f_split, f_lo, f_mm = sem("f_split"), sem("f_lo"), sem("f_mm")
    mean_mm, centred, squared, sq_used, std, normed, silu = (
        sem(n) for n in "mean_mm centred squared sq_used conv_std normed silu".split())
    conv_hi = sem("conv_hi")
    win, pool_mm, pool_hi, pool_lo = sem("windows"), sem("pool_mm"), sem("pool_hi"), sem("pool_lo")
    d_pool = sem("d_pool")
    block = ctx.enter_context(nc.Block())

    xf = Tt[:, 0:KD, :]

    @block.sync
    def _(sp):
        for b in range(2):
            sp.dma_start(wf[b][:], A["w_t"][b]).then_inc(w_in[b], 16)
        for i in range(4):
            sp.dma_start(xf[:, 2 * i:2 * i + 2], A["x_t"][:, 2 * i:2 * i + 2]).then_inc(x_in[i], 16)
        for dst, src in M["const_loads"]:
            sp.dma_start(dst, src).then_inc(c_in, 16)
        with sp.Fori(1, B_ALL // 2) as i:
            for s in range(2):
                sp.wait_ge(w_ready, 2 * i + (s - 1))
                sp.dma_start(wf[s][:], A["w_t"][bass.ds(2 * i + s, 1)].rearrange("o p k c -> p (o k) c")
                             ).then_inc(w_in[s], 16)

    @block.scalar
    def _(act):
        def split(b, s):
            act.wait_ge(w_in[s], b * 8 + (16 - 8 * s))
            act.activation(wh[s][:], wf[s][:], ACT.Copy, scale=WS)
            act.activation(wf[s][:], wf[s][:], ACT.Copy, scale=WS).then_inc(w_scaled, 1)

        def evacuate(b, s, slot):
            for half in range(2):
                act.wait_ge(unit_done, 2 * b + (half + 1))
                act.activation(Tt[:, bass.ds(slot, 1), half * 512:half * 512 + 512].rearrange(
                    "p o c -> p (o c)"), ps[:, 2 * s + half, :], ACT.Copy, scale=RWS).then_inc(evac, 1)

        def pool_high(g):
            act.wait_ge(pool_mm, g + 1)
            act.activation(yT_pool[:, g, :, 0, :], ps[:, 4 + 2 * (g % 2):6 + 2 * (g % 2), :].rearrange(
                "p a (b c) -> p (a b) c", b=4), ACT.Copy, scale=cv[:, 3, g:g + 1]).then_inc(pool_hi, 1)

        split(0, 0)
        split(1, 1)
        for k in range(KD):
            if k % 2 == 0:
                act.wait_ge(x_in[k // 2], 16)
            act.activation(xh[:, k, :], xf[:, k, :], ACT.Copy).then_inc(x_hi, 1)
        act.wait_ge(x_lo, KD)
        with act.Fori(0, 4) as i:
            for s in range(2):
                evacuate(2 * i + s, s, 2 * i + (s + 8))
                split(2 * i + (s + 2), s)
        act.drain()
        for g in range(4):
            act.activation(Tt[:, S_CG + g, :], Tt[:, S_CG + g, :], ACT.Sigmoid).then_inc(sig, 1)
        with act.Fori(4, 8) as i:
            for s in range(2):
                evacuate(2 * i + s, s, 2 * i + (s - 8))
                split(2 * i + (s + 2), s)
        act.wait_ge(h_done, 4)
        with act.Fori(8, 12) as i:
            for s in range(2):
                evacuate(2 * i + s, s, 2 * i + (s - 8))
                split(2 * i + (s + 2), s)
        act.wait_ge(c_in, 16 * len(M["const_loads"]))
        act.activation(M["fwh"][:], M["fwf"][:], ACT.Copy, scale=WS)
        act.activation(M["fwf"][:], M["fwf"][:], ACT.Copy, scale=WS).then_inc(f_split, 1)
        for b in range(24, B_ALL):
            s = b % 2
            if b == B_ALL - 1:
                pool_high(0)
                pool_high(1)
            evacuate(b, s, b - 8)
            if b + 2 < B_ALL:
                split(b + 2, s)
            if b in (25, 26):
                for g in (0, 1) if b == 25 else (2, 3):
                    act.wait_ge(centred, g + 1)
                    if g >= 2:
                        act.wait_ge(sq_used, g - 1)
                    act.activation(sq[g % 2][:], cacc[:, g, :], ACT.Square).then_inc(squared, 1)
            if b == 27:
                act.wait_ge(sq_used, 4)
                act.activation(rs[:], ps[:, 6:8, :].rearrange("p a b -> p (a b)"), ACT.Sqrt,
                               bias=M["eps"][:, 0:1]).then_inc(std, 1)
            if b == 28:
                for g in range(4):
                    act.wait_ge(normed, g + 1)
                    act.activation(cacc[:, g, :], cacc[:, g, :], ACT.Silu, scale=cv[:, 1, g:g + 1],
                                   bias=cv[:, 2, g:g + 1]).then_inc(silu, 1)
                for g in range(4):
                    act.wait_ge(silu, g + 1)
                    act.activation(yT_conv[:, g, :, 0, :], cacc[:, g, :].rearrange("p (a b) -> p a b", a=NCH),
                                   ACT.Copy).then_inc(conv_hi, 1)
        pool_high(2)
        pool_high(3)
        act.wait_ge(f_mm, 1)
        act.activation(M["fz"][:], ps[0:H, 0:2, :].rearrange("p a b -> p (a b)"), ACT.Identity,
                       scale=RWS, bias=M["bf"][:, 0:1]).then_inc(evac, 1)

    @block.gpsimd
    def _(pool):
        for s in range(2):
            pool.wait_ge(w_scaled, s + 1)
            nc.gpsimd.tensor_tensor(wl[s][:], wf[s][:], wh[s][:], ALU.subtract).then_inc(w_ready, 1)
        with pool.Fori(1, B_ALL // 2) as i:
            for s in range(2):
                await_ge(pool, w_scaled, 2 * i + (s + 1))
                nc.gpsimd.tensor_tensor(wl[s][:], wf[s][:], wh[s][:], ALU.subtract).then_inc(w_ready, 1)
        pool.wait_ge(f_split, 1)
        nc.gpsimd.tensor_tensor(M["fwl"][:], M["fwf"][:], M["fwh"][:], ALU.subtract).then_inc(f_lo, 1)

    @block.tensor
    def _(pe):
        def unit(s, half, by_token, first=False):
            out = ps[:, 2 * s + half, :]
            if not by_token:
                tok = slice(512 * half, 512 * half + 512)
                for k in range(KD):
                    if first:
                        pe.wait_ge(x_lo, k + 1)
                    m = mm3(pe, out, wh[s][:, k, :], wl[s][:, k, :], xh[:, k, tok], xl[:, k, tok],
                            k == 0, k == KD - 1)
            else:
                for q in range(4):
                    tok = slice(512 * half + P * q, 512 * half + P * q + P)
                    for k in range(KD):
                        m = mm3(pe, out[:, P * q:P * q + P], xh[:, k, tok], xl[:, k, tok],
                                wh[s][:, k, :], wl[s][:, k, :], k == 0, k == KD - 1)
            m.then_inc(unit_done, 1)

        def block_of(b, s, by_token, first=False):
            pe.wait_ge(w_ready, b + 1)
            for half in range(2):
                if not first:
                    pe.wait_ge(evac, 2 * b + (half - 3))
                unit(s, half, by_token, first)

        def mix_windows(g):
            pe.wait_ge(win, g + 1)
            for half in range(2):
                m = pe.matmul(ps[:, 4 + 2 * (g % 2) + half, :], M["pw"][:, g, :],
                              Tt[:, S_PO + g, 512 * half:512 * half + 512], start=True, stop=True)
            m.then_inc(pool_mm, 1)

        for s in range(2):
            block_of(s, s, False, first=True)
        with pe.Fori(1, 12) as i:
            for s in range(2):
                block_of(2 * i + s, s, False)
        for b in range(24, B_ALL):
            block_of(b, b % 2, b >= B_T)
            if b == 24:
                pe.wait_ge(tap, 4 * CK)
                for half in range(2):
                    for g in range(4):
                        m = pe.matmul(ps[:, 4 + half, :], M["mean_w"][:], cacc[:, g, 512 * half:512 * half + 512],
                                      start=g == 0, stop=g == 3)
                m.then_inc(mean_mm, 1)
            if b in (26, 27):
                for g in (0, 1) if b == 26 else (2, 3):
                    pe.wait_ge(squared, g + 1)
                    for half in range(2):
                        m = pe.matmul(ps[:, 6 + half, :], M["mean_w"][:], sq[g % 2][:, 512 * half:512 * half + 512],
                                      start=g == 0, stop=g == 3)
                    m.then_inc(sq_used, 1)
            if b == 28:
                pe.wait_ge(centred, 4)
                mix_windows(0)
                pe.wait_ge(std, 1)
                mix_windows(1)
        for g in (2, 3):
            pe.wait_ge(pool_lo, g - 1)
            mix_windows(g)
        pe.wait_ge(f_lo, 1)
        pe.wait_ge(evac, 2 * B_ALL - 2)
        for half in range(2):
            tok = slice(512 * half, 512 * half + 512)
            for k in range(KD):
                m = mm3(pe, ps[0:H, half, :], M["fwh"][:, k, :], M["fwl"][:, k, :], xh[:, k, tok],
                        xl[:, k, tok], k == 0, k == KD - 1)
        m.then_inc(f_mm, 1)

    @block.vector
    def _(dve):
        nc.vector.memset(M["eps"][:], EPS)
        nc.vector.memset(M["mean_w"][:], 1.0 / 512)
        nc.vector.memset(hc[:, :, 0:CK - 1], 0.0)
        nc.vector.memset(pa[:, 0:16], 0.0)
        nc.vector.memset(pb[:, 0:16], 0.0)
        for k in range(KD):
            dve.wait_ge(x_hi, k + 1)
            nc.vector.tensor_tensor(xl[:, k, :], xf[:, k, :], xh[:, k, :], ALU.subtract).then_inc(x_lo, 1)
        for g in range(4):
            dve.wait_ge(sig, g + 1)
            nc.vector.tensor_tensor(hc[:, g, CK - 1:], Tt[:, S_CA + g, :], Tt[:, S_CG + g, :],
                                    ALU.mult).then_inc(h_done, 1)
        dve.wait_ge(h_done, 4)
        dve.wait_ge(c_in, 16 * len(M["const_loads"]))
        with dve.Fori(0, 2) as q:
            for k in range(CK):
                for r in range(2):
                    g = 2 * q + r
                    acc = cacc[:, bass.ds(g, 1), :].rearrange("p o c -> p (o c)")
                    src = hc[:, bass.ds(g, 1), k:k + T].rearrange("p o c -> p (o c)")
                    w = M["dw"][:, bass.ds(g, 1), k:k + 1].rearrange("p o c -> p (o c)")
                    if k == 0:
                        nc.vector.tensor_scalar(acc, src, w, cv[:, 0, bass.ds(g, 1)], ALU.mult, ALU.add
                                                ).then_inc(tap, 1)
                    else:
                        dve.wait_ge(tap, q * (2 * CK) + (2 * k + r - 1))
                        nc.vector.scalar_tensor_tensor(acc, src, w, acc, ALU.mult, ALU.add).then_inc(tap, 1)
        dve.wait_ge(evac, 2 * 12)
        n = 0
        for g in range(4):
            bufs = [pa, pb]
            nc.vector.tensor_copy(pa[:, 16:], Tt[:, S_PO + g, :]).then_inc(d_pool, 1)
            n += 1
            for s in range(g + 1):
                src, dst = bufs[s % 2], bufs[(s + 1) % 2]
                dve.wait_ge(d_pool, n)
                nc.vector.tensor_tensor(dst[:, 16:], src[:, 16:], src[:, 16 - 2 ** s:16 + T - 2 ** s],
                                        ALU.add).then_inc(d_pool, 1)
                n += 1
            R = bufs[(g + 1) % 2]
            dve.wait_ge(d_pool, n)
            nc.vector.tensor_tensor(M["p16"][:], R[:, 16:32], M["rc"][:, g, :], ALU.mult).then_inc(d_pool, 1)
            nc.vector.scalar_tensor_tensor(Tt[:, S_PO + g, 16:], R[:, 32:], 0.5 ** (g + 1),
                                           Tt[:, S_PO + g, 16:], ALU.mult, ALU.subtract)
            n += 1
            dve.wait_ge(d_pool, n)
            nc.vector.tensor_tensor(Tt[:, S_PO + g, 0:16], M["p16"][:], Tt[:, S_PO + g, 0:16],
                                    ALU.subtract).then_inc(win, 1)
            dve.wait_ge(win, g + 1)
        dve.wait_ge(tap, 4 * CK)
        dve.wait_ge(mean_mm, 1)
        for g in range(4):
            nc.vector.tensor_tensor(cacc[:, g, :], cacc[:, g, :], ps[:, 4:6, :].rearrange("p a b -> p (a b)"),
                                    ALU.subtract).then_inc(centred, 1)
        dve.wait_ge(std, 1)
        nc.vector.reciprocal(rs[:], rs[:])
        dve.drain()
        for g in range(4):
            nc.vector.tensor_tensor(cacc[:, g, :], cacc[:, g, :], rs[:], ALU.mult).then_inc(normed, 1)
        for g in range(4):
            dve.wait_ge(conv_hi, g + 1)
            nc.vector.tensor_tensor(yT_conv[:, g, :, 1, :], cacc[:, g, :].rearrange("p (a b) -> p a b", a=NCH),
                                    yT_conv[:, g, :, 0, :], ALU.subtract)
        for g in range(4):
            dve.wait_ge(pool_hi, g + 1)
            nc.vector.scalar_tensor_tensor(
                yT_pool[:, g, :, 1, :], ps[:, 4 + 2 * (g % 2):6 + 2 * (g % 2), :].rearrange("p a (b c) -> p (a b) c", b=4),
                cv[:, 3, g:g + 1], yT_pool[:, g, :, 0, :], ALU.mult, ALU.subtract).then_inc(pool_lo, 1)



def attention(nc, ctx, M, A):
    sem = lambda n: ctx.enter_context(nc.semaphore(n))
    Tt, ps = M["T"], M["ps"]
    cb, sb, pt, nb, rsum, ident = (M[n] for n in "cb sb pt nb rsum ident".split())
    yT_fox, yT_swa = M["yT_fox"], M["yT_swa"]
    units = [(j, q, r) for j in range(4) for q in range(NCH) for r in range(2)]
    NU = len(units)

    groups = []
    fox_groups, y_group = {}, {}
    for u in range(NU + 2):
        if u < NU:
            q = units[u][1]
            fox_groups[u] = []
            for a in range(0, q + 1, 4):
                fox_groups[u].append(len(groups))
                groups.append(("p", u, a, min(4, q + 1 - a)))
        if u >= 3 and u % 2:
            y_group[u - 2] = len(groups)
            groups.append(("y",) + units[u - 2][:2])
    sp_groups, sy_group = {}, {}
    for n in range(NCH + 1):
        if n < NCH:
            sp_groups[n] = []
            for a in range(0, 16, 4):
                sp_groups[n].append(len(groups))
                groups.append(("sp", n, a, 4))
        if n:
            sy_group[n - 1] = len(groups)
            groups.append(("sy", n - 1))

    f_abs, f_exp, f_ln, f_z, f_c = (sem(n) for n in "f_abs f_exp f_ln f_sig f_cum".split())
    cb_mm, cb_done = sem("decay_mm"), sem("decay_copied")
    s_done, s_read, p_done = sem("scores"), sem("scores_read"), sem("probs")
    t_done = sem("transposed")
    t_copied = [sem("t_copied_even"), sem("t_copied_odd")]
    y_hi = sem("y_hi")
    pv, y_done = sem("pv"), sem("y_written")
    ws_done, ws_max, ws_exp, ws_den, ws_pv, ws_y = (
        sem(n) for n in "swa_scores swa_max swa_exp swa_den swa_pv swa_y".split())
    block = ctx.enter_context(nc.Block())

    zero, zeroed = sem("zero_tile"), sem("weights_zeroed")

    @block.gpsimd
    def _(pool):
        pool.memset(M["zeros"][:], 0.0).then_inc(zero, 1)

    @block.sync
    def _(sp):
        sp.wait_ge(zero, 1)
        with sp.Fori(0, NEXP // P // 2) as n:
            sp.dma_start(A["weights_rows"][bass.ds(n, 1)].rearrange("o p c -> p (o c)"), M["zeros"][:]
                         ).then_inc(zeroed, 16)
        sp.wait_ge(zeroed, 16 * (NEXP // P // 2))

    def group_free(eng, g):
        if g >= 2:
            eng.wait_ge(t_copied[g % 2], g // 2)

    def copied(ins, g):
        ins.then_inc(t_copied[g % 2], 1)

    def scores_bank(u):
        return 2 * (u % 2)

    @block.scalar
    def _(act):
        fz, ft = M["fz"], M["ft"]
        act.activation(ft[:], fz[:], ACT.Abs).then_inc(f_abs, 1)
        act.wait_ge(f_abs, 1)
        act.activation(ft[:], ft[:], ACT.Exp, scale=-1.0).then_inc(f_exp, 1)
        act.wait_ge(f_exp, 1)
        act.activation(ft[:], ft[:], ACT.Ln, bias=1.0).then_inc(f_ln, 1)

        def copy_group(g):
            kind = groups[g][0]
            bank = ps[:, 4 + g % 2, :]
            act.wait_ge(t_done, g + 1)
            if kind == "p":
                _, u, a, nblk = groups[g]
                if a:
                    if u >= 2:
                        act.wait_ge(pv, u - 1)
                    copied(act.activation(pt[u % 2][:, a:a + nblk, :].rearrange("p a b -> p (a b)"),
                                          bank[:, 0:P * nblk], ACT.Copy), g)
            elif kind == "y":
                _, j, q = groups[g]
                act.activation(yT_fox[:, j, q, 0, :], bank[:, 0:P], ACT.Copy).then_inc(y_hi, 1)
            elif kind == "sp":
                _, n, a, nblk = groups[g]
                if a >= 8:
                    if n >= 1:
                        act.wait_ge(ws_pv, n)
                    copied(act.activation(M["spt"][:, a:a + 4, :].rearrange("p a b -> p (a b)"),
                                          bank, ACT.Copy), g)
            else:
                _, n = groups[g]
                act.activation(yT_swa[:, :, n, 0, :], bank.rearrange("p (a b) -> p a b", a=4),
                               ACT.Copy).then_inc(y_hi, 1)

        for i in range(2 * H):
            act.wait_ge(cb_mm, i + 1)
            act.activation(cb[:, i // 2, 512 * (i % 2):512 * (i % 2) + 512], ps[:, 6 + i % 2, :],
                           ACT.Copy).then_inc(cb_done, 1)
        for u in range(NU + 3):
            if u < NU:
                W = (units[u][1] + 1) * P
                act.wait_ge(s_read, u + 1)
                act.activation(sb[u % 3][:, 0:W], sb[u % 3][:, 0:W], ACT.Exp, scale=-1.0,
                               bias=nb[:, u % 4:u % 4 + 1], accum_out=rsum[:, u % 4:u % 4 + 1]).then_inc(p_done, 1)
            if 1 <= u <= NU:
                for g in fox_groups[u - 1]:
                    copy_group(g)
            if u - 3 in y_group:
                copy_group(y_group[u - 3])

        def swa_exps(n):
            k0 = P if n == 0 else 0
            act.wait_ge(ws_max, 2 * n + 2)
            if n >= 1:
                act.wait_ge(t_done, sp_groups[n - 1][-1] + 1)
            act.activation(M["es"][:], M["snb"][:], ACT.Exp).then_inc(ws_exp, 1)
            for h in range(H):
                act.activation(M["sp"][:, h, k0:], ps[:, h // 2, 256 * (h % 2) + k0:256 * (h % 2) + 256],
                               ACT.Exp, scale=SC, bias=M["wnb"][:, h:h + 1],
                               accum_out=M["wrs"][:, h:h + 1]).then_inc(ws_exp, 1)

        swa_exps(0)
        for n in range(NCH + 1):
            if n < NCH:
                for g in sp_groups[n]:
                    copy_group(g)
            if n:
                copy_group(sy_group[n - 1])
            if n + 1 < NCH:
                swa_exps(n + 1)

    @block.tensor
    def _(pe):
        def scores(u):
            j, q, r = units[u]
            b0 = scores_bank(u)
            W = (q + 1) * P
            if u >= 2:
                pe.wait_ge(s_read, u - 1)
            lo = r * HD
            qs = Tt[lo:lo + HD, S_QF + j, q * P:q * P + P]
            for c in range(0, W, 512):
                w = min(512, W - c)
                m = pe.matmul(ps[:, b0 + c // 512, 0:w], qs, Tt[lo:lo + HD, S_KF + j, c:c + w],
                              start=True, stop=c + w < W)
            d = q * P
            pe.matmul(ps[:, b0 + d // 512, d % 512:d % 512 + P], M["ident_b"][:], M["fox_mask"][:],
                      start=False, stop=True).then_inc(s_done, 1)

        def turn(g):
            group_free(pe, g)
            kind = groups[g][0]
            bank = ps[:, 4 + g % 2, :]
            if kind == "p":
                _, u, a, nblk = groups[g]
                for b in range(nblk):
                    m = pe.transpose(bank[:, P * b:P * b + P], sb[u % 3][:, P * (a + b):P * (a + b) + P], ident[:])
            elif kind == "y":
                _, j, q = groups[g]
                m = pe.transpose(bank[:, 0:P], Tt[:, S_QF + j, q * P:q * P + P], ident[:])
            elif kind == "sp":
                _, n, a, nblk = groups[g]
                for b in range(nblk):
                    h, kb = (a + b) // 2, (a + b) % 2
                    m = pe.transpose(bank[:, P * b:P * b + P], M["sp"][:, h, P * kb:P * kb + P], ident[:])
            else:
                _, n = groups[g]
                for j in range(4):
                    m = pe.transpose(bank[:, P * j:P * j + P], Tt[:, S_QS + j, n * P:n * P + P], ident[:])
            m.then_inc(t_done, 1)

        def values(u):
            j, q, r = units[u]
            for g in fox_groups[u]:
                pe.wait_ge(t_copied[g % 2], g // 2 + 1)
            if u >= 2:
                pe.wait_ge(y_done, u - 1)
            for b in range(q + 1):
                m = pe.matmul(ps[:, 6 + u % 2, 0:HD], pt[u % 2][:, b, :],
                              Tt[:, S_VF + j, b * P + r * HD:b * P + r * HD + HD], start=b == 0, stop=b == q)
            m.then_inc(pv, 1)

        pe.wait_ge(f_c, 1)
        for i in range(2 * H):
            if i >= 2:
                pe.wait_ge(cb_done, i - 1)
            pe.matmul(ps[:, 6 + i % 2, :], M["sel"][:, i // 2, :],
                      M["negc"][:, 512 * (i % 2):512 * (i % 2) + 512], start=True, stop=True).then_inc(cb_mm, 1)
        pe.wait_ge(cb_done, 2 * H)
        scores(0)
        for u in range(NU + 2):
            if u + 1 < NU:
                scores(u + 1)
            if u < NU:
                pe.wait_ge(p_done, u + 1)
                for g in fox_groups[u]:
                    turn(g)
            if 1 <= u <= NU:
                values(u - 1)
            if u - 2 in y_group:
                pe.wait_ge(y_done, u - 1)
                turn(y_group[u - 2])

        def swa_scores(n):
            k0 = P if n == 0 else 0
            for h in range(H):
                r, j = h // 4, h % 4
                lo = r * HD
                out = ps[:, h // 2, 256 * (h % 2) + k0:256 * (h % 2) + 256]
                pe.matmul(out, Tt[lo:lo + HD, S_QS + j, n * P:n * P + P],
                          Tt[lo:lo + HD, S_KS, (n - 1) * P + k0:(n + 1) * P], start=True, stop=False)
                m = pe.matmul(out, M["slope"][:, h, :], M["swa_mask"][:, k0:], start=False, stop=True)
            m.then_inc(ws_done, 1)

        def swa_values(n):
            for g in sp_groups[n]:
                pe.wait_ge(t_copied[g % 2], g // 2 + 1)
            if n >= 1:
                pe.wait_ge(ws_y, n)
            for h in range(H):
                r = h // 4
                for kb in range(1 if n == 0 else 0, 2):
                    c = n - 1 + kb
                    m = pe.matmul(ps[:, 6, HD * h:HD * h + HD], M["spt"][:, 2 * h + kb, :],
                                  Tt[:, S_VS, c * P + r * HD:c * P + r * HD + HD],
                                  start=kb == (1 if n == 0 else 0), stop=kb == 1)
            m.then_inc(ws_pv, 1)

        swa_scores(0)
        for n in range(NCH + 1):
            if n < NCH:
                pe.wait_ge(ws_exp, 9 * n + 9)
                for g in sp_groups[n][:2]:
                    turn(g)
                if n + 1 < NCH:
                    swa_scores(n + 1)
                for g in sp_groups[n][2:]:
                    turn(g)
            if n:
                pe.wait_ge(ws_y, n)
                turn(sy_group[n - 1])
            if n < NCH:
                swa_values(n)

    @block.vector
    def _(dve):
        fz, ft = M["fz"], M["ft"]
        nc.vector.tensor_copy(M["ident_b"][:], ident[:])
        nc.vector.tensor_copy(M["fox_mask"][:], M["masks"][:, 256:384])
        nc.vector.tensor_copy(M["swa_mask"][:], M["masks"][:, 0:256])
        for h in range(H):
            nc.vector.tensor_scalar(M["slope"][:, h, :], ident[:], M["masks"][:, 512 + h:513 + h], None, ALU.mult)
        dve.wait_ge(f_ln, 1)
        nc.vector.scalar_tensor_tensor(fz[:], fz[:], 0.0, ft[:], ALU.min, ALU.subtract).then_inc(f_z, 1)
        nc.vector.memset(M["ones_t"][:], 1.0).then_inc(f_z, 1)
        dve.wait_ge(f_z, 2)
        nc.vector.tensor_tensor_scan(ft[:], M["ones_t"][:], fz[:], 0.0, ALU.mult, ALU.add).then_inc(f_z, 1)
        dve.wait_ge(f_z, 3)
        nc.vector.tensor_scalar(M["negc"][:], ft[:], -1.0 / SC, None, ALU.mult).then_inc(f_c, 1)

        def copy_group(g):
            kind = groups[g][0]
            bank = ps[:, 4 + g % 2, :]
            if kind == "p":
                _, u, a, nblk = groups[g]
                if a == 0:
                    dve.wait_ge(t_done, g + 1)
                    if u >= 2:
                        dve.wait_ge(pv, u - 1)
                    copied(nc.vector.tensor_copy(pt[u % 2][:, 0:nblk, :].rearrange("p a b -> p (a b)"),
                                                 bank[:, 0:P * nblk]), g)
            elif kind == "y":
                _, j, q = groups[g]
                dve.wait_ge(y_hi, j * NCH + q + 1)
                copied(nc.vector.tensor_tensor(yT_fox[:, j, q, 1, :], bank[:, 0:P], yT_fox[:, j, q, 0, :],
                                               ALU.subtract), g)
            elif kind == "sp":
                _, n, a, nblk = groups[g]
                if a < 8:
                    dve.wait_ge(t_done, g + 1)
                    if n >= 1:
                        dve.wait_ge(ws_pv, n)
                    copied(nc.vector.tensor_copy(M["spt"][:, a:a + 4, :].rearrange("p a b -> p (a b)"), bank), g)
            else:
                _, n = groups[g]
                dve.wait_ge(y_hi, 4 * NCH + n + 1)
                copied(nc.vector.tensor_tensor(yT_swa[:, :, n, 1, :], bank.rearrange("p (a b) -> p a b", a=4),
                                               yT_swa[:, :, n, 0, :], ALU.subtract), g)

        def finish(u):
            j, q, r = units[u]
            dve.wait_ge(p_done, u + 1)
            nc.vector.reciprocal(rsum[:, u % 4:u % 4 + 1], rsum[:, u % 4:u % 4 + 1])
            dve.drain()
            dve.wait_ge(pv, u + 1)
            c = q * P + r * HD
            nc.vector.tensor_scalar(Tt[:, S_QF + j, c:c + HD], ps[:, 6 + u % 2, 0:HD],
                                    rsum[:, u % 4:u % 4 + 1], None, ALU.mult).then_inc(y_done, 1)

        dve.wait_ge(cb_done, 2 * H)
        for u in range(NU + 3):
            if u < NU:
                j, q, r = units[u]
                W = (q + 1) * P
                b0 = scores_bank(u)
                dve.wait_ge(s_done, u + 1)
                if u >= 3:
                    dve.wait_ge(t_done, fox_groups[u - 3][-1] + 1)
                nc.vector.tensor_tensor_reduce(
                    sb[u % 3][:, 0:W], ps[:, b0:b0 + 2, :].rearrange("p a b -> p (a b)")[:, 0:W],
                    cb[:, 2 * j + r, 0:W], -SC, 3e38, ALU.add, ALU.min, nb[:, u % 4:u % 4 + 1]).then_inc(s_read, 1)
            if 1 <= u <= NU:
                for g in fox_groups[u - 1]:
                    copy_group(g)
            if 2 <= u <= NU + 1:
                finish(u - 2)
            if u - 3 in y_group:
                copy_group(y_group[u - 3])

        def swa_max(n):
            k0 = P if n == 0 else 0
            dve.wait_ge(ws_done, n + 1)
            nc.vector.tensor_reduce(M["wmx"][:], ps[:, 0:4, :].rearrange("p a (b c) -> p (a b) c", b=2)[:, :, k0:],
                                    AX.X, ALU.max)
            dve.drain()
            nc.vector.scalar_tensor_tensor(M["wnb"][:], M["wmx"][:], SC, M["sinks"][:], ALU.mult, ALU.max)
            dve.drain()
            nc.vector.tensor_tensor(M["snb"][:], M["sinks"][:], M["wnb"][:], ALU.subtract).then_inc(ws_max, 1)
            dve.drain()
            nc.vector.tensor_scalar(M["wnb"][:], M["wnb"][:], -1.0, None, ALU.mult).then_inc(ws_max, 1)

        def swa_finish(n):
            dve.wait_ge(ws_pv, n + 1)
            for r in range(2):
                ins = nc.vector.tensor_tensor(
                    Tt[:, S_QS:S_QS + 4, n * P + r * HD:n * P + r * HD + HD],
                    ps[:, 6, 256 * r:256 * r + 256].rearrange("p (a b) -> p a b", a=4),
                    M["wden"][:, 4 * r:4 * r + 4].rearrange("p (a o) -> p a o", o=1).to_broadcast([P, 4, HD]),
                    ALU.mult)
            ins.then_inc(ws_y, 1)

        nc.vector.memset(M["sp"][:, :, 0:P], 0.0)
        swa_max(0)
        for n in range(NCH + 1):
            if n < NCH:
                dve.wait_ge(ws_exp, 9 * n + 9)
                if n:
                    dve.wait_ge(ws_y, n)
                nc.vector.tensor_tensor(M["wden"][:], M["wrs"][:], M["es"][:], ALU.add)
                dve.drain()
                nc.vector.reciprocal(M["wden"][:], M["wden"][:])
                for g in sp_groups[n][:2]:
                    copy_group(g)
                if n + 1 < NCH:
                    swa_max(n + 1)
            if n:
                copy_group(sy_group[n - 1])
            if n < NCH:
                dve.drain()
                swa_finish(n)


def merge(nc, ctx, M, A):
    sem = lambda n: ctx.enter_context(nc.semaphore(n))
    Tt, ps, xh, xl, sf, sh, sl, sg, tmp = (M[n] for n in "T ps xh xl sf sh sl sg tmp".split())
    yT = [M[n] for n in ("yT_fox", "yT_pool", "yT_conv", "yT_swa")]
    s_in = [sem("strip_in0"), sem("strip_in1")]
    first_in, first_high = [sem("first_third"), sem("second_third")], sem("first_strip_hi")
    wo_early = sem("w_out_early")
    scaled, ready = sem("strip_scaled"), sem("strip_ready")
    gate_mm, y_mm, gate, product = sem("gate_mm"), sem("y_mm"), sem("gate"), sem("product")
    free = sem("banks_free")
    block = ctx.enter_context(nc.Block())

    @block.sync
    def _(sp):
        for t in range(3):
            sp.dma_start(sf[0][:, 4 * t:4 * t + 4, :], A["strips"][0, :, 4 * t:4 * t + 4, :]
                         ).then_inc(first_in[t] if t < 2 else s_in[0], 16)
        sp.dma_start(sf[1][:], A["strips"][1]).then_inc(s_in[1], 16)
        for k in range(2):
            sp.dma_start(Tt[:, S_WOF + k, :], A["w_o"][k]).then_inc(wo_early, 16)
        sp.wait_ge(wo_early, 32)
        with sp.Fori(1, NQ * NB // 2) as i:
            for s in range(2):
                sp.wait_ge(ready, 2 * i + (s - 1))
                sp.dma_start(sf[s][:], A["strips"][bass.ds(2 * i + s, 1)].rearrange("o p k c -> p (o k) c")
                             ).then_inc(s_in[s], 16)

    @block.scalar
    def _(act):
        def split(i, s):
            act.wait_ge(s_in[s], 8 * i + (16 - 8 * s))
            act.activation(sh[s][:], sf[s][:], ACT.Copy, scale=WS)
            act.activation(sf[s][:], sf[s][:], ACT.Copy, scale=WS).then_inc(scaled, 1)

        def strips(cq, last):
            for b in range(NB):
                if b < NB - 1 or not last:
                    act.wait_ge(free, 32 * cq + (8 * b + 4))
                    split(4 * cq + (b + 1), (b + 1) % 2)
                for c in range(NCH):
                    i = 32 * cq + (8 * b + c)
                    act.wait_ge(gate_mm, i + 1)
                    act.wait_ge(free, i + 1)
                    act.activation(sg[c % 4][:], ps[:, c % 4, 0:CW], ACT.Sigmoid, scale=RWS).then_inc(gate, 1)

        for t in range(3):
            act.wait_ge(first_in[t] if t < 2 else s_in[0], 16)
            act.activation(sh[0][:, 4 * t:4 * t + 4, :], sf[0][:, 4 * t:4 * t + 4, :], ACT.Copy, scale=WS
                           ).then_inc(first_high, 1)
        with act.Fori(0, NQ - 1) as cq:
            strips(cq, False)
        strips(NQ - 1, True)

    @block.gpsimd
    def _(pool):
        def low(i, s):
            await_ge(pool, scaled, 2 * i + s)
            nc.gpsimd.tensor_tensor(sl[s][:], sf[s][:], sh[s][:], ALU.subtract).then_inc(ready, 1)

        pool.wait_ge(ready, 1)
        low(0, 1)
        with pool.Fori(1, NQ * NB // 2) as i:
            for s in range(2):
                low(i, s)

    @block.tensor
    def _(pe):
        with pe.Fori(0, NQ) as cq:
            for b in range(NB):
                s = b % 2
                pe.wait_ge(ready, 4 * cq + (b + 1))
                for c in range(NCH):
                    i = 32 * cq + (8 * b + c)
                    tok = slice(P * c, P * c + P)
                    pe.wait_ge(free, i + 1)
                    for k in range(KD):
                        m = mm3(pe, ps[:, c % 4, 0:CW], xh[:, k, tok], xl[:, k, tok], sh[s][:, k, :],
                                sl[s][:, k, :], k == 0, k == KD - 1)
                    m.then_inc(gate_mm, 1)
                    for j in range(4):
                        m = mm3(pe, ps[:, 4 + c % 4, 0:CW], yT[b][:, j, c, 0, :], yT[b][:, j, c, 1, :],
                                sh[s][:, KD + j, :], sl[s][:, KD + j, :], j == 0, j == 3)
                    m.then_inc(y_mm, 1)

    @block.vector
    def _(dve):
        nc.vector.memset(tmp[0][:], 0.0).then_inc(free, 4)
        for t in range(3):
            dve.wait_ge(first_high, t + 1)
            third = slice(4 * t, 4 * t + 4)
            ins = nc.vector.scalar_tensor_tensor(sl[0][:, third, :], sf[0][:, third, :], WS, sh[0][:, third, :],
                                                 ALU.mult, ALU.subtract)
        ins.then_inc(ready, 1)
        with dve.Fori(0, NQ) as cq:
            for b in range(NB):
                for c in range(NCH):
                    i = 32 * cq + (8 * b + c)
                    out = Tt[:, S_X1 + c, bass.ds(cq * CW, CW)]
                    dve.wait_ge(gate, i + 1)
                    dve.wait_ge(y_mm, i + 1)
                    if b == 0:
                        nc.vector.scalar_tensor_tensor(out, ps[:, 4 + c % 4, 0:CW], RWS, sg[c % 4][:],
                                                       ALU.mult, ALU.mult).then_inc(free, 1)
                    else:
                        nc.vector.scalar_tensor_tensor(tmp[c % 2][:], ps[:, 4 + c % 4, 0:CW], RWS, sg[c % 4][:],
                                                       ALU.mult, ALU.mult).then_inc(free, 1)
                        dve.wait_ge(free, i + 5)
                        nc.vector.tensor_tensor(out, out, tmp[c % 2][:], ALU.add)


def layer_norm(nc, dve, M, row, rstd_wait, gain, shift, out):
    st, mv = M["st"], M["mv"]
    for i in range(2):
        nc.vector.bn_stats(st[:, i, :], row[:, 512 * i:512 * i + 512])
    dve.drain()
    nc.vector.bn_aggr(mv[:], st[:].rearrange("p a b -> p (a b)")).then_inc(M["var_done"], 1)
    rstd_wait()
    nc.vector.reciprocal(M["rstd"][:], M["std"][:])
    nc.vector.scalar_tensor_tensor(row, row, mv[:, 0:1], gain, ALU.subtract, ALU.mult)
    dve.drain()
    return nc.vector.scalar_tensor_tensor(out, row, M["rstd"][:, 0:1], shift, ALU.mult, ALU.add)


def first_norm(nc, ctx, M, A):
    sem = lambda n: ctx.enter_context(nc.semaphore(n))
    Tt, ps, ident, mh, ml, row = (M[n] for n in "T ps ident mh ml row".split())
    wo, wq = M["wo"], M["wq"]
    wof = [Tt[:, S_WOF + i, :] for i in range(2)]
    wqf = [Tt[:, 10 + i, :].rearrange("p (k c) -> p k c", k=KD) for i in range(2)]
    xin = [Tt[:, 8 + i, :] for i in range(2)]
    wo_in, wq_in, x_in = ([sem(f"{n}{i}") for i in range(2)] for n in ("wo_in", "wq_in", "xc_in"))
    ln_in = sem("ln_in")
    wo_high, wo_ready, wq_scaled, wq_ready = (sem(n) for n in "wo_high wo_ready wq_scaled wq_ready".split())
    turned, m_hi, m_lo, mix, summed, root = (sem(n) for n in "turned m_hi m_lo mix_mm summed root".split())
    M["var_done"] = sem("var_done")
    x1_done = sem("x1_done")
    block = ctx.enter_context(nc.Block())

    @block.sync
    def _(sp):
        for i in range(2):
            sp.dma_start(xin[i], A["x"][P * i:P * i + P]).then_inc(x_in[i], 16)
        for k in range(2, KD):
            sp.wait_ge(wo_ready, k - 1)
            sp.dma_start(wof[k % 2], A["w_o"][k]).then_inc(wo_in[k % 2], 16)
        sp.dma_start(M["ln"][:], A["ln"][:, 0:2]).then_inc(ln_in, 16)
        sp.dma_start(M["tok"][:], A["tok"]).then_inc(ln_in, 16)
        sp.dma_start(M["kt"][:, 0, :], A["k1_t"]).then_inc(ln_in, 16)
        sp.dma_start(M["kt"][:, 1, :], A["k2_t"]).then_inc(ln_in, 16)
        sp.dma_start(M["iota"][:], A["iota"]).then_inc(ln_in, 16)
        for c in range(NCH):
            for i in range(2):
                if c:
                    sp.wait_ge(wq_ready, 2 * c + i - 1)
                sp.dma_start(wqf[i], A["w_q"][2 * c + i]).then_inc(wq_in[i], 16)
            if 1 <= c < NCH - 1:
                sp.wait_ge(summed, c)
                sp.dma_start(xin[(c + 1) % 2], A["x"][P * (c + 1):P * (c + 2)]).then_inc(x_in[(c + 1) % 2], 16)
        sp.wait_ge(ln_in, 80)

    @block.scalar
    def _(act):
        for c in range(NCH + 1):
            if c < NCH:
                act.wait_ge(turned, c + 1)
                if c >= 2:
                    act.wait_ge(mix, c - 1)
                act.activation(mh[c % 2][:], ps[:, 2 * (c % 2):2 * (c % 2) + 2, :].rearrange("p a b -> p (a b)"),
                               ACT.Copy).then_inc(m_hi, 1)
            if c == 0:
                for k in range(KD):
                    if k >= 2:
                        act.wait_ge(wo_in[k % 2], 16 * (k // 2))
                    act.activation(wo[:, k, 0, :], wof[k % 2], ACT.Copy, scale=WS).then_inc(wo_high, 1)
            if c:
                act.wait_ge(M["var_done"], c)
                act.activation(M["std"][:], M["mv"][:, 1:2], ACT.Sqrt, bias=M["eps"][:, 0:1]).then_inc(root, 1)
            for b in (2 * c, 2 * c + 1):
                if b < 2 * H:
                    act.wait_ge(wq_in[b % 2], 16 * (b // 2 + 1))
                    act.activation(wq[:, b, 0, :, :], wqf[b % 2], ACT.Copy, scale=WS)
                    act.activation(wqf[b % 2], wqf[b % 2], ACT.Copy, scale=WS).then_inc(wq_scaled, 1)

    @block.gpsimd
    def _(pool):
        for b in range(2 * H):
            pool.wait_ge(wq_scaled, b + 1)
            nc.gpsimd.tensor_tensor(wq[:, b, 1, :, :], wqf[b % 2], wq[:, b, 0, :, :], ALU.subtract).then_inc(wq_ready, 1)

    @block.tensor
    def _(pe):
        def turn(c):
            if c >= 2:
                pe.wait_ge(m_lo, c - 1)
            for k in range(KD):
                m = pe.transpose(ps[:, 2 * (c % 2) + k // 4, P * (k % 4):P * (k % 4) + P],
                                 Tt[:, S_X1 + c, P * k:P * k + P], ident[:])
            m.then_inc(turned, 1)

        turn(0)
        for c in range(NCH):
            if c + 1 < NCH:
                turn(c + 1)
            pe.wait_ge(m_lo, c + 1)
            if c >= 2:
                pe.wait_ge(summed, c - 1)
            for k in range(KD):
                if c == 0:
                    pe.wait_ge(wo_ready, k + 1)
                for a, b in ((0, 0), (0, 1), (1, 0)):
                    lhs = (mh, ml)[a][c % 2][:, P * k:P * k + P]
                    for half in range(2):
                        m = pe.matmul(ps[:, 4 + 2 * (c % 2) + half, :], lhs, wo[:, k, b, 512 * half:512 * half + 512],
                                      start=k == a == b == 0, stop=k == KD - 1 and a == 1)
            m.then_inc(mix, 1)

    @block.vector
    def _(dve):
        for c in range(NCH + 1):
            if c < NCH:
                dve.wait_ge(m_hi, c + 1)
                nc.vector.tensor_tensor(ml[c % 2][:], ps[:, 2 * (c % 2):2 * (c % 2) + 2, :].rearrange("p a b -> p (a b)"),
                                        mh[c % 2][:], ALU.subtract).then_inc(m_lo, 1)
            if c == 0:
                for k in range(KD):
                    dve.wait_ge(wo_high, k + 1)
                    nc.vector.scalar_tensor_tensor(wo[:, k, 1, :], wof[k % 2], WS, wo[:, k, 0, :], ALU.mult,
                                                   ALU.subtract).then_inc(wo_ready, 1)
            if c:
                d = c - 1
                if d == 0:
                    dve.wait_ge(ln_in, 80)
                dve.wait_ge(x_in[d % 2], 16 * (d // 2 + 1))
                nc.vector.tensor_scalar(xin[d % 2], xin[d % 2], ALPHA, None, ALU.mult)
                dve.drain()
                dve.wait_ge(mix, d + 1)
                nc.vector.scalar_tensor_tensor(row[:], ps[:, 4 + 2 * (d % 2):6 + 2 * (d % 2), :].rearrange(
                    "p a b -> p (a b)"), RWS, xin[d % 2], ALU.mult, ALU.add).then_inc(summed, 1)
                dve.drain()
                layer_norm(nc, dve, M, row[:], lambda: dve.wait_ge(root, d + 1), M["ln"][:, 0, :], M["ln"][:, 1, :],
                           Tt[:, S_X1 + d, :]).then_inc(x1_done, 1)
                dve.drain()


def scatter(nc, pool, M, g, e, scattered, base=0):
    before = 16 * NSEL * g + (16 * e + base)
    if e % TOPK == 0 and e and not (isinstance(before, int) and before == 0):
        await_ge(pool, scattered, before)
    nc.gpsimd.indirect_dma_start(
        M["weights_flat"], bass.IndirectOffsetOnAxis(ap=M["place"][:, e:e + 1], axis=0), M["put"][:, e:e + 1],
        None, compute_op=ALU.add).then_inc(scattered, 16)


def hidden(nc, ctx, M, A):
    sem = lambda n: ctx.enter_context(nc.semaphore(n))
    Tt, ps, ident, wq = (M[n] for n in "T ps ident wq".split())
    xc, xth, xtl, qt, sc, cand, oh, kt = (M[n] for n in "xc xth xtl qt sc cand oh kt".split())
    v16, ix, ixf, pos, posf, sel_a, sel_b = (M[n] for n in "v16 ix ixf pos posf sel_a sel_b".split())
    top, topj, gg, gsum, idx_next, idx, hid = (M[n] for n in "top topj gg gsum idx_next idx hid".split())
    ut, hout, place, put, tok = (M[n] for n in "ut hout place put tok".split())
    x1t = Tt[:, 0:4, :].rearrange("p a (b t) -> p (a b) t", b=2)
    ring = M["ring1"]
    NR = len(ring)
    landed = [sem(f"landed{i}") for i in range(NR)]
    free = sem("ring_free")
    chosen, copied_x, turned, x_hi, x_lo = (sem(n) for n in "chosen x1_copied x1_turned x1_hi x1_lo".split())
    q_mm, q_out, s_mm, s_out = (sem(n) for n in "q_mm q_out s_mm s_out".split())
    exp_in, exp_out, selected = (sem(n) for n in "exp_in exp_out selected".split())
    placed = sem("placed")
    scattered = sem("scattered")
    put_free = sem("put_free")
    dense_mm, dense_out = sem("dense_turned"), sem("dense_x1t")
    u_in = [sem(f"u_in{i}") for i in range(NU)]
    h_mm = sem("h_mm")
    h_out = sem("h_out")
    h_stored = [sem("h_stored0"), sem("h_stored1")]
    block = ctx.enter_context(nc.Block())

    @block.gpsimd
    def _(pool):
        def gather(g, i):
            if i % 4 == 0:
                await_ge(pool, free, NSEL * g + (i + 4))
            nc.gpsimd.indirect_dma_start(
                ring[i % NR], None, A["u"], bass.IndirectOffsetOnAxis(ap=idx[:, i:i + 1], axis=0)
            ).then_inc(landed[i % NR], 16)

        def half_of_chunk(g, half, dense):
            for i in range(64):
                gather(g, 64 * half + i)
                k, r = divmod(i, 14)
                if dense is not None and k < 4 and r < 12:
                    for e in range(TOPK * r // 12, TOPK * (r + 1) // 12):
                        scatter(nc, pool, M, dense, 64 * (1 - half) + TOPK * k + e, scattered)
                if dense is not None and half == 0 and i == 57:
                    await_ge(pool, scattered, 16 * NSEL * dense + 16 * NSEL)
                    pool.memset(M["mark"][:], 0.0).then_inc(put_free, 1)

        pool.wait_ge(chosen, 1)
        half_of_chunk(0, 0, None)
        with pool.Fori(0, ND - 1) as g:
            await_ge(pool, placed, g + 1)
            half_of_chunk(g, 1, g)
            await_ge(pool, chosen, g + 2)
            half_of_chunk(g + 1, 0, g)
        pool.wait_ge(placed, ND)
        half_of_chunk(ND - 1, 1, ND - 1)
        pool.wait_ge(scattered, 16 * (NSEL * ND - 64))

    @block.sync
    def _(sp):
        def half_step(j, more):
            for i in range(16):
                if i < 16 - NU or more:
                    sp.wait_ge(h_mm, 16 * j + (i + 1))
                    sp.dma_start(ut[i % NU], A["u_t"][bass.ds(16 * j + (i + NU), 1)].rearrange("o p k c -> p (o k) c")
                                 ).then_inc(u_in[i % NU], 16)
                sp.wait_ge(h_out, 16 * j + (i + 5))
                sp.dma_start(A["h"][bass.ds(16 * j + i, 1)].rearrange("o p t -> p (o t)"), hout[i % 2][:]
                             ).then_inc(h_stored[i % 2], 16)

        for i in range(NU):
            sp.dma_start(ut[i], A["u_t"][i]).then_inc(u_in[i], 16)
        with sp.Fori(0, 7) as j:
            half_step(j, True)
        half_step(7, False)
        for i in range(2):
            sp.wait_ge(h_stored[i], 16 * 64 + 16)

    @block.tensor
    def _(pe):
        def table_block(j, i):
            pe.wait_ge(u_in[i % NU], (256 // NU) * j + 16 * (i // NU + 1))
            pe.wait_ge(h_out, 16 * j + (i + 1))
            for k in range(KD):
                m = pe.matmul(ps[:, 4 + i % 4, :], ut[i % NU][:, k, :], x1t[:, k, :], start=k == 0, stop=k == KD - 1)
            m.then_inc(h_mm, 1)

        def turn(n):
            pe.wait_ge(copied_x, n + 1)
            for k in range(KD):
                m = pe.transpose(ps[:, k // 4, P * (k % 4):P * (k % 4) + P], xc[:, P * k:P * k + P], ident[:])
            m.then_inc(turned, 1)

        def query_group(n, i):
            if i == 0:
                pe.wait_ge(x_lo, n + 1)
            if i >= 2:
                pe.wait_ge(q_out, 4 * n + (i - 1))
            for b in range(4 * i, 4 * i + 4):
                for k in range(KD):
                    m = mm3(pe, ps[:, 2 + i % 2, P * (b % 4):P * (b % 4) + P], wq[:, b, 0, k, :], wq[:, b, 1, k, :],
                            xth[:, P * k:P * k + P], xtl[:, P * k:P * k + P], k == 0, k == KD - 1)
            m.then_inc(q_mm, 1)

        def scores(n):
            pe.wait_ge(q_out, 4 * n + 4)
            for b in range(2 * H):
                m = pe.matmul(ps[:, b // 4, P * (b % 4):P * (b % 4) + P], qt[:, b, :], kt[:, b % 2, :],
                              start=True, stop=True)
                if b % 4 == 3:
                    m.then_inc(s_mm, 1)

        def queries(n):
            turn(n)
            for i in range(4):
                query_group(n, i)
            scores(n)

        def half_step(j, more):
            for i in range(16):
                table_block(j, i)
                if more:
                    if i == 1:
                        pe.wait_ge(s_out, 4 * j + 8)
                        turn(j + 2)
                    elif 4 <= i < 8:
                        query_group(j + 2, i - 4)
                    elif i == 8:
                        scores(j + 2)

        queries(0)
        for d in range(ND):
            if d >= 2:
                pe.wait_ge(dense_out, d - 1)
            for k in range(KD):
                m = pe.transpose(ps[:, 4 + 2 * (d % 2) + k // 4, P * (k % 4):P * (k % 4) + P],
                                 Tt[:, S_X1 + 2 * d + 1, P * k:P * k + P], ident[:])
            m.then_inc(dense_mm, 1)
        pe.wait_ge(s_out, 4)
        queries(1)
        with pe.Fori(0, 6) as j:
            half_step(j, True)
        with pe.Fori(6, 8) as j:
            half_step(j, False)

    @block.scalar
    def _(act):
        def copy_x(n):
            act.activation(xc[:], Tt[:, bass.ds(S_X1 + n, 1), :].rearrange("p o c -> p (o c)"), ACT.Copy
                           ).then_inc(copied_x, 1)

        def x_high(n):
            act.wait_ge(turned, n + 1)
            act.activation(xth[:], ps[:, 0:2, :].rearrange("p a b -> p (a b)"), ACT.Copy).then_inc(x_hi, 1)

        def query_group(n, i):
            act.wait_ge(q_mm, 4 * n + (i + 1))
            act.activation(qt[:, 4 * i:4 * i + 4, :].rearrange("p a b -> p (a b)"), ps[:, 2 + i % 2, :], ACT.Copy,
                           scale=RWS).then_inc(q_out, 1)

        def scores(n):
            for i in range(4):
                act.wait_ge(s_mm, 4 * n + (i + 1))
                act.activation(sc[:, 4 * i:4 * i + 4, :].rearrange("p a b -> p (a b)"), ps[:, i, :], ACT.Copy
                               ).then_inc(s_out, 1)

        def weights(n):
            act.wait_ge(exp_in, n + 1)
            act.activation(gg[:], gg[:], ACT.Exp).then_inc(exp_out, 1)

        def table_block(j, i):
            act.wait_ge(h_mm, 16 * j + (i + 1))
            act.wait_ge(h_stored[i % 2], 128 * j + 16 * (i // 2 + 1))
            act.activation(hout[i % 2][:], ps[:, 4 + i % 4, :], ACT.Gelu).then_inc(h_out, 1)

        def half_step(j, choose, more, exp_after):
            for i in range(16):
                table_block(j, i)
                if i == 0 and choose:
                    act.wait_ge(selected, j + 1)
                    scores(j + 1)
                if i == 0 and more:
                    copy_x(j + 2)
                if i == 1 and more:
                    x_high(j + 2)
                if 4 <= i < 8 and more:
                    query_group(j + 2, i - 4)
                if exp_after and i == exp_after[0]:
                    weights(exp_after[1])

        copy_x(0)
        x_high(0)
        for i in range(4):
            query_group(0, i)
        scores(0)
        for d in range(ND):
            act.wait_ge(dense_mm, d + 1)
            act.activation(x1t[:, :, P * d:P * d + P],
                           ps[:, 4 + 2 * (d % 2):6 + 2 * (d % 2), :].rearrange("p a (k c) -> p (a k) c", c=P), ACT.Copy
                           ).then_inc(dense_out, 1)
        copy_x(1)
        x_high(1)
        act.activation(hout[0][0:1, 0:1], hout[0][0:1, 0:1], ACT.Copy, scale=0.0).then_inc(h_out, 4)
        for i in range(4):
            query_group(1, i)
        weights(0)
        with act.Fori(0, 6) as j:
            half_step(j, True, True, (12, j + 1))
        half_step(6, True, False, None)
        half_step(7, False, False, (3, 7))

    @block.vector
    def _(dve):
        def x_low(n):
            dve.wait_ge(x_hi, n + 1)
            nc.vector.tensor_tensor(xtl[:], ps[:, 0:2, :].rearrange("p a b -> p (a b)"), xth[:], ALU.subtract
                                    ).then_inc(x_lo, 1)

        def choose(k, n, dense):
            if k == 0:
                await_ge(dve, s_out, 4 * n + 4)
            if k < 16:
                nc.vector.max(v16[:, k, 0:8], sc[:, k, :])
                if k == 15:
                    dve.drain()
            elif k < 48:
                b = (k - 16) // 2
                if k % 2 == 0:
                    nc.vector.max_index(ix[:, b, 0:8], v16[:, b, 0:8], sc[:, b, :])
                else:
                    nc.vector.match_replace(sc[:, b, :], v16[:, b, 0:8], sc[:, b, :], -3e38)
                if k == 47:
                    dve.drain()
            elif k < 64:
                nc.vector.max(v16[:, k - 48, 8:16], sc[:, k - 48, :])
                if k == 63:
                    dve.drain()
            elif k < 80:
                nc.vector.max_index(ix[:, k - 64, 8:16], v16[:, k - 64, 8:16], sc[:, k - 64, :])
            elif k < 88:
                h = k - 80
                nc.vector.tensor_tensor(
                    cand[:, h, :].rearrange("p (a b) -> p a b", a=16),
                    v16[:, 2 * h, :].rearrange("p (a o) -> p a o", o=1).to_broadcast([P, 16, 16]),
                    v16[:, 2 * h + 1:2 * h + 2, :].to_broadcast([P, 16, 16]), ALU.add)
                if k == 87:
                    dve.drain()
            elif k < 96:
                nc.vector.max(top[:, k - 88, 0:8], cand[:, k - 88, :])
                if k == 95:
                    dve.drain()
            elif k < 112:
                h = (k - 96) // 2
                if k % 2 == 0:
                    nc.vector.max_index(pos[:, h, 0:8], top[:, h, 0:8], cand[:, h, :])
                else:
                    nc.vector.match_replace(cand[:, h, :], top[:, h, 0:8], cand[:, h, :], -3e38)
                if k == 111:
                    dve.drain()
            elif k < 120:
                nc.vector.max(top[:, k - 112, 8:16], cand[:, k - 112, :])
                if k == 119:
                    dve.drain()
            elif k < 128:
                nc.vector.max_index(pos[:, k - 120, 8:16], top[:, k - 120, 8:16], cand[:, k - 120, :])
                if k == 127:
                    dve.drain()
            elif k == 128:
                nc.vector.tensor_tensor(gg[:].rearrange("p (h k) -> p h k", h=H), top[:],
                                        top[:, :, 0:1].to_broadcast([P, H, TOPK]), ALU.subtract).then_inc(exp_in, 1)
                nc.vector.tensor_copy(ixf, ix[:])
                nc.vector.tensor_scalar(topj[:, 0, :], pos[:].rearrange("p h k -> p (h k)"), 4, None,
                                        ALU.logical_shift_right)
                nc.vector.tensor_scalar(topj[:, 1, :], pos[:].rearrange("p h k -> p (h k)"), 15, None,
                                        ALU.bitwise_and)
                dve.drain()
            elif k == 129:
                nc.vector.tensor_copy(posf, topj)
                dve.drain()
            elif k in (130, 134):
                s = (k - 130) // 4
                nc.vector.tensor_tensor(oh[:], posf[:, s, :].rearrange("p (a o) -> p a o", o=1).to_broadcast([P, NSEL, 16]),
                                        M["iota"][:].rearrange("p (o a) -> p o a", o=1).to_broadcast([P, NSEL, 16]),
                                        ALU.is_equal)
                dve.drain()
            elif k in (131, 135):
                s = (k - 131) // 4
                for h in range(H):
                    nc.vector.tensor_tensor(oh[:, 16 * h:16 * h + 16, :], oh[:, 16 * h:16 * h + 16, :],
                                            ixf[:, 2 * h + s:2 * h + s + 1, :].to_broadcast([P, 16, 16]), ALU.mult)
                dve.drain()
            elif k in (132, 136):
                s = (k - 132) // 4
                nc.vector.tensor_reduce((sel_a, sel_b)[s], oh[:], AX.X, ALU.add)
                dve.drain()
            elif k == 137:
                if dense is None:
                    nc.vector.scalar_tensor_tensor(idx_next[:], sel_a, float(NKEY), sel_b, ALU.mult, ALU.add)
                else:
                    nc.vector.scalar_tensor_tensor(sel_a, sel_a, float(NKEY), sel_b, ALU.mult, ALU.add)
                dve.wait_ge(exp_out, n + 1)
                nc.vector.tensor_reduce(gsum[:], gg[:].rearrange("p (h k) -> p h k", h=H), AX.X, ALU.add)
                dve.drain()
            elif k == 138:
                nc.vector.reciprocal(gsum[:], gsum[:])
                if dense is not None:
                    await_ge(dve, put_free, dense + 1)
                    nc.vector.tensor_scalar(place[:], sel_a, float(DT), tok[:, 0:1], ALU.mult, ALU.add)
                dve.drain()
            elif k == 139:
                nc.vector.tensor_tensor((gg if dense is None else put)[:].rearrange("p (h k) -> p h k", h=H),
                                        gg[:].rearrange("p (h k) -> p h k", h=H),
                                        gsum[:].rearrange("p (h o) -> p h o", o=1).to_broadcast([P, H, TOPK]),
                                        ALU.mult).then_inc(selected, 1)
                if dense is not None:
                    nc.vector.tensor_scalar(tok[:], tok[:], float(P), None, ALU.add).then_inc(placed, 1)
                dve.drain()

        def rows(g, more):
            x1 = M["x1c"][:]
            nc.vector.tensor_copy(x1, Tt[:, bass.ds(S_X1 + 2 * g, 1), :].rearrange("p o c -> p (o c)"))
            dve.drain()
            for e in range(NSEL):
                half, r = divmod(e, 64)
                dve.wait_ge(landed[e % NR], (16 * NSEL // NR) * g + 16 * (e // NR + 1))
                nc.vector.tensor_tensor_reduce(ring[e % NR], ring[e % NR], x1, 1.0, 0.0, ALU.mult, ALU.add,
                                               hid[:, e:e + 1]).then_inc(free, 1)
                if r == 10 and more:
                    x_low(2 * g + (half + 2))
                if r >= 6 and (more or not half):
                    for k in range(3 * r - 18, min(3 * r - 15, 137)):
                        choose(k, 2 * g + (half + 1), g if half == 0 else None)
                if 60 <= r < 63 and (more or not half):
                    choose(r + 77, 2 * g + (half + 1), g if half == 0 else None)
            if more:
                nc.vector.tensor_copy(idx[:], idx_next[:]).then_inc(chosen, 1)
                keep_choice(g + 1)
            dve.drain()
            nc.vector.tensor_copy(M["hid_all"][:, bass.ds(g, 1), :].rearrange("p o e -> p (o e)"), hid[:])

        def keep_choice(g):
            nc.vector.tensor_copy(M["idx_all"][:, bass.ds(g, 1), :].rearrange("p o e -> p (o e)"), idx_next[:])
            nc.vector.tensor_copy(M["gg_all"][:, bass.ds(g, 1), :].rearrange("p o e -> p (o e)"), gg[:])

        nc.vector.memset(hid[:], 0.0).then_inc(free, NR)
        nc.vector.memset(put[:], 0.0).then_inc(put_free, 1)
        for i in range(2):
            nc.vector.memset(hout[i][:], 0.0).then_inc(h_stored[i], 16)
        x_low(0)
        for k in range(140):
            choose(k, 0, None)
            if k == 20:
                x_low(1)
        nc.vector.tensor_copy(idx[:], idx_next[:]).then_inc(chosen, 1)
        keep_choice(0)
        with dve.Fori(0, ND - 1) as g:
            rows(g, True)
        rows(ND - 1, False)


def values(nc, ctx, M, A, out):
    sem = lambda n: ctx.enter_context(nc.semaphore(n))
    Tt, ps = M["T"], M["ps"]
    idx, wgt, wgt_all, acc, res, ring = (M[n] for n in "idx2 wgt wgt_all acc res ring2".split())
    vt, gt, ht, wt = (M[n] for n in "vt gt ht wt".split())
    NR = len(ring)
    landed = [sem(f"v_landed{i}") for i in range(NR)]
    free = sem("v_ring_free")
    chosen = sem("v_indices")
    gelu, root, row_done, ln_in = (sem(n) for n in "gelu root2 row_done ln2_in".split())
    block_in = [sem(f"block_in{i}") for i in range(NV)]
    ready = sem("block_weights")
    scattered = sem("last_scattered")
    used = sem("block_used")
    stored = sem("res_free")
    M["var_done"] = sem("var2_done")
    block = ctx.enter_context(nc.Block())

    @block.gpsimd
    def _(pool):
        def chunk(g, last_weights=False):
            for i in range(NSEL):
                if i % 64 == 0:
                    await_ge(pool, chosen, 2 * g + (i // 64 + 1))
                if i % 4 == 0:
                    await_ge(pool, free, NSEL * g + (i + 4))
                nc.gpsimd.indirect_dma_start(
                    ring[i % NR], None, A["v"], bass.IndirectOffsetOnAxis(ap=idx[:, i:i + 1], axis=0)
                ).then_inc(landed[i % NR], 16)
                if last_weights and i < 64:
                    scatter(nc, pool, M, 0, 64 + i, scattered, base=-16 * 64)

        chunk(0, True)
        with pool.Fori(1, ND) as g:
            chunk(g)

    @block.sync
    def _(sp):
        def load(q, i):
            b = bass.ds(NV * q + i, 1)
            sp.dma_start(vt[i], A["v_blocks"][b].rearrange("o p c -> p (o c)")).then_inc(block_in[i], 16)
            sp.dma_start(ht[i], A["h"][b].rearrange("o p t -> p (o t)")).then_inc(block_in[i], 16)
            if isinstance(q, int):
                return
            load_weights(q, i)

        def load_weights(q, i):
            sp.dma_start(gt[i], A["weights"][bass.ds(NV * q + i, 1)].rearrange("o p t -> p (o t)")
                         ).then_inc(block_in[i], 16)

        sp.dma_start(M["ln2"][:], A["ln"][:, 2:4]).then_inc(ln_in, 16)
        for i in range(NV):
            load(0, i)
        sp.wait_ge(scattered, 16 * 64)
        for i in range(NV):
            load_weights(0, i)
        with sp.Fori(1, NEXP // P // NV) as q:
            for i in range(NV):
                sp.wait_ge(used, NV * q + (i + 5 - NV))
                load(q, i)

    @block.tensor
    def _(pe):
        def blocks(q, first=False, last=False):
            for i in range(NV):
                pe.wait_ge(block_in[i], 48 * q + 48)
                pe.wait_ge(ready, NV * q + (i + 1))
                for t in range(ND):
                    for half in range(2):
                        m = pe.matmul(ps[:, 2 * t + half, :], wt[i % 4][:, P * t:P * t + P],
                                      vt[i][:, 512 * half:512 * half + 512],
                                      start=first and i == 0, stop=last and i == NV - 1)
                m.then_inc(used, 1)

        blocks(0, first=True)
        with pe.Fori(1, NEXP // P // NV - 1) as q:
            blocks(q)
        blocks(NEXP // P // NV - 1, last=True)

    @block.scalar
    def _(act):
        def finish(c, rows):
            act.wait_ge(M["var_done"], c + 1)
            act.activation(M["std"][:], M["mv"][:, 1:2], ACT.Sqrt, bias=M["eps"][:, 0:1]).then_inc(root, 1)
            act.wait_ge(row_done, c + 1)
            act.dma_start(out[rows, :], res[:]).then_inc(stored, 16)

        hid = M["hid_all"][:].rearrange("p g e -> p (g e)")
        act.activation(hid, hid, ACT.Gelu).then_inc(gelu, 1)
        with act.Fori(0, ND - 1) as g:
            finish(g, bass.ds(2 * P * g, P))
        for d in range(ND):
            finish(ND - 1 + d, slice((2 * d + 1) * P, (2 * d + 2) * P))
        finish(NCH - 1, slice((NCH - 2) * P, (NCH - 1) * P))
        act.wait_ge(stored, 16 * NCH + 16)

    @block.vector
    def _(dve):
        def indices(g, half):
            nc.vector.tensor_copy(idx[:, 64 * half:64 * half + 64],
                                  M["idx_all"][:, bass.ds(g, 1), 64 * half:64 * half + 64].rearrange("p o e -> p (o e)")
                                  ).then_inc(chosen, 1)

        def norm(c, total=acc[0][:]):
            dve.drain()
            def waits():
                dve.wait_ge(root, c + 1)
                dve.wait_ge(stored, 16 * c + 16)
            layer_norm(nc, dve, M, total, waits, M["ln2"][:, 0, :], M["ln2"][:, 1, :], res[:]).then_inc(row_done, 1)

        def dense_chunk(d):
            if d:
                dve.wait_ge(row_done, ND - 1 + d)
            dve.wait_ge(used, 4 + NEXP // P)
            nc.vector.scalar_tensor_tensor(M["dense_sum"][:], Tt[:, S_X1 + 2 * d + 1, :], ALPHA,
                                           ps[:, 2 * d:2 * d + 2, :].rearrange("p a b -> p (a b)"), ALU.mult, ALU.add)
            norm(ND - 1 + d, M["dense_sum"][:])

        def chunk(g, more, before, blocks, first=0, last=NSEL):
            x1 = M["x1c"][:]
            nc.vector.tensor_copy(wgt[:], wgt_all[:, bass.ds(g, 1), :].rearrange("p o e -> p (o e)"))
            nc.vector.tensor_copy(x1, Tt[:, bass.ds(S_X1 + 2 * g, 1), :].rearrange("p o c -> p (o c)"))
            dve.drain()
            for e in range(NSEL):
                r = e % NR
                dve.wait_ge(landed[r], (16 * NSEL // NR) * g + 16 * (e // NR + 1))
                if e < 2:
                    nc.vector.tensor_scalar(acc[e][:], ring[r], wgt[:, e:e + 1], None, ALU.mult).then_inc(free, 1)
                else:
                    dve.wait_ge(free, NSEL * g + (NR + e - 1))
                    nc.vector.scalar_tensor_tensor(acc[e % 2][:], ring[r], wgt[:, e:e + 1], acc[e % 2][:],
                                                   ALU.mult, ALU.add).then_inc(free, 1)
                for i in range(blocks * max(e - first, 0) // (last - first),
                               blocks * max(e + 1 - first, 0) // (last - first) if e < last else 0):
                    dve.wait_ge(block_in[i % NV], (48 // NV) * blocks * g + (48 // NV * before + 48 * (i // NV + 1)))
                    dve.wait_ge(used, blocks * g + (before + i + 1))
                    nc.vector.tensor_tensor(wt[i % 4], gt[i % NV], ht[i % NV], ALU.mult).then_inc(ready, 1)
                if not more and e in DENSE_AT:
                    dense_chunk(DENSE_AT.index(e))
                if more and e in (100, NSEL - 1):
                    indices(g + 1, int(e > 100))
            dve.drain()
            nc.vector.tensor_tensor(acc[0][:], acc[0][:], acc[1][:], ALU.add)
            dve.drain()
            nc.vector.scalar_tensor_tensor(acc[0][:], x1, ALPHA, acc[0][:], ALU.mult, ALU.add)
            norm(g if more else NCH - 1)

        nc.vector.memset(acc[0][:], 0.0).then_inc(stored, 16)
        nc.vector.memset(acc[1][:], 0.0).then_inc(free, NR)
        nc.vector.memset(wgt[:], 0.0).then_inc(used, 4)
        indices(0, 0)
        indices(0, 1)
        dve.wait_ge(gelu, 1)
        dve.wait_ge(ln_in, 16)
        nc.vector.tensor_tensor(wgt_all[:].rearrange("p g e -> p (g e)"), M["gg_all"][:].rearrange("p g e -> p (g e)"),
                                M["hid_all"][:].rearrange("p g e -> p (g e)"), ALU.mult)
        dve.drain()
        chunk(0, True, 0, 8, 80)
        with dve.Fori(1, ND - 1) as g:
            chunk(g, True, 8 - 48, 48)
        chunk(ND - 1, False, 32, 24, last=72)


def build_mix(nc, ctx, A, out):
    keep = lambda n, s, d: ctx.enter_context(nc.sbuf_tensor(n, s, d))
    M = {}
    M["T"] = keep("tiles", [P, NSLOT, T], F32)
    M["ps"] = ctx.enter_context(nc.psum_tensor("ps", [P, 8, 512], F32))
    M["ident"] = keep("ident", [P, P], F32)
    M["eps"] = keep("eps", [P, 1], F32)
    Tt = M["T"]

    def pair_view(ap):
        return ap.bitcast(F16).rearrange("p j (q h c) -> p j q h c", q=NCH, h=2)

    M["yT_fox"] = pair_view(Tt[:, S_QF:S_QF + 4, :])
    M["yT_pool"] = pair_view(Tt[:, S_PO:S_PO + 4, :])
    M["yT_swa"] = pair_view(Tt[:, S_QS:S_QS + 4, :])
    A = dict(A)
    both = [nc.dram_tensor(n, (NEXP // P, P, DT), F32, kind="Internal").ap() for n in ("weights", "gelu_h")]
    A["weights"], A["h"] = both
    M["weights_flat"] = both[0].rearrange("b e (t o) -> (b e t) o", o=1)
    A["weights_rows"] = both[0].rearrange("(n a) e t -> n (a e t)", a=2).rearrange("n (p c) -> n p c", p=P)
    A["v_blocks"] = A["v"].rearrange("(b e) c -> b e c", e=P)
    with ExitStack() as early:
        sb = lambda n, s, d: early.enter_context(nc.sbuf_tensor(n, s, d))
        M["xh"], M["xl"] = sb("x_hi_t", [P, KD, T], F16), sb("x_lo_t", [P, KD, T], F16)
        hc_raw = sb("conv_in", [P, 4 * (T + CK - 1)], F32)
        M["hc"] = hc_raw[:].rearrange("p (g t) -> p g t", g=4)
        M["yT_conv"] = pair_view(hc_raw[:, 0:4 * T].rearrange("p (j t) -> p j t", j=4))
        M["fz"] = sb("forget", [H, T], F32)
        M["sinks"] = sb("sinks_sb", [P, H], F32)
        M["masks"] = sb("masks_sb", [P, 512 + H], F32)
        M["sel"] = sb("sel_sb", [H, H, P], F32)
        with ExitStack() as c1:
            s1 = lambda n, s, d: c1.enter_context(nc.sbuf_tensor(n, s, d))
            M["cacc"] = s1("conv_acc", [P, 4, T], F32)
            M["wf"] = [s1(f"w_f32_{i}", [P, KD, P], F32) for i in range(2)]
            M["wh"] = [s1(f"w_hi_{i}", [P, KD, P], F16) for i in range(2)]
            M["wl"] = [s1(f"w_lo_{i}", [P, KD, P], F16) for i in range(2)]
            M["pa"], M["pb"] = s1("window_a", [P, 16 + T], F32), s1("window_b", [P, 16 + T], F32)
            M["sq"] = [s1(f"square_{i}", [P, T], F32) for i in range(2)]
            M["rs"] = s1("conv_rstd", [P, T], F32)
            M["chan"] = s1("chan_sb", [P, 4, 4], F32)
            M["dw"] = s1("dw_sb", [P, 4, CK], F32)
            M["pw"] = s1("pool_w_sb", [P, 4, P], F32)
            M["rc"] = s1("rc_sb", [P, 4, 16], F32)
            M["p16"] = s1("p16", [P, 16], F32)
            M["bf"] = s1("b_f_sb", [H, 1], F32)
            M["fwf"] = s1("wf_f32", [P, KD, H], F32)
            M["fwh"], M["fwl"] = s1("wf_hi", [P, KD, H], F16), s1("wf_lo", [P, KD, H], F16)
            M["mean_w"] = s1("mean_w", [P, P], F32)
            M["const_loads"] = [
                (M["chan"][:], A["chan"]), (M["dw"][:], A["dw"]), (M["pw"][:], A["pool_w"]),
                (M["rc"][:], A["rc"]), (M["bf"][:], A["b_f"]), (M["fwf"][:], A["w_f"]),
                (M["sinks"][:], A["sinks"]), (M["masks"][:], A["masks"]), (M["sel"][:], A["sel"]),
                (M["ident"][:], A["masks"][:, 384:512])]
            project(nc, c1, M, A)
        with ExitStack() as c2:
            s2 = lambda n, s, d: c2.enter_context(nc.sbuf_tensor(n, s, d))
            M["cb"] = s2("decay", [P, H, T], F32)
            probs = s2("probs_sb", [P, 3, T], F32)
            M["sb"] = [probs[:, i, :] for i in range(3)]
            turned = s2("probs_t", [P, 16, P], F32)
            M["pt"] = [turned[:, 0:8, :], turned[:, 8:16, :]]
            M["ft"], M["ones_t"], M["negc"] = (probs[0:H, i, :] for i in range(3))
            M["sp"] = probs[:, 0:2, :].rearrange("p a (h k) -> p (a h) k", h=4)
            M["spt"] = turned
            M["nb"], M["rsum"] = s2("nb", [P, 4], F32), s2("rsum", [P, 4], F32)
            M["ident_b"] = s2("ident_b", [P, P], BF16)
            M["fox_mask"] = s2("fox_mask", [P, P], BF16)
            M["swa_mask"] = s2("swa_mask", [P, 2 * P], BF16)
            M["slope"] = s2("slope", [P, H, P], BF16)
            for n in "wmx wnb snb es wrs wden".split():
                M[n] = s2(n, [P, H], F32)
            M["zeros"] = s2("zeros", [P, 2 * DT], F32)
            attention(nc, c2, M, A)
        with ExitStack() as c3:
            s3 = lambda n, s, d: c3.enter_context(nc.sbuf_tensor(n, s, d))
            M["sf"] = [s3(f"strip_f32_{i}", [P, KD + 4, CW], F32) for i in range(2)]
            M["sh"] = [s3(f"strip_hi_{i}", [P, KD + 4, CW], F16) for i in range(2)]
            M["sl"] = [s3(f"strip_lo_{i}", [P, KD + 4, CW], F16) for i in range(2)]
            M["sg"] = [s3(f"gate_{i}", [P, CW], F32) for i in range(4)]
            M["tmp"] = [s3(f"product_{i}", [P, CW], F32) for i in range(2)]
            merge(nc, c3, M, A)
    with ExitStack() as late:
        sb = lambda n, s, d: late.enter_context(nc.sbuf_tensor(n, s, d))
        M["kt"] = sb("keys_t", [P, 2, NKEY], F32)
        M["iota"] = sb("iota_sb", [P, 16], F32)
        M["st"], M["mv"] = sb("bn_st", [P, 2, 6], F32), sb("bn_mv", [P, 2], F32)
        M["std"], M["rstd"] = sb("std", [P, 1], F32), sb("rstd", [P, 1], F32)
        for n, dt in (("idx_all", U32), ("gg_all", F32), ("hid_all", F32)):
            M[n] = sb(n, [P, ND, NSEL], dt)
        M["tok"] = sb("dense_token", [P, 1], F32)
        M["place"], M["put"] = sb("place", [P, NSEL], U32), sb("put", [P, NSEL], F32)
        wq_ctx = late.enter_context(ExitStack())
        M["wq"] = wq_ctx.enter_context(nc.sbuf_tensor("wq_pairs", [P, 2 * H, 2, KD, P], F16))
        M["wo"] = Tt[:, S_WO:S_WO + 8, :].bitcast(F16).rearrange("p k (h c) -> p k h c", h=2)
        with ExitStack() as c4:
            s4 = lambda n, s, d: c4.enter_context(nc.sbuf_tensor(n, s, d))
            M["ln"] = s4("ln1_sb", [P, 2, D], F32)
            M["mh"] = [s4(f"m_hi_{i}", [P, D], F16) for i in range(2)]
            M["ml"] = [s4(f"m_lo_{i}", [P, D], F16) for i in range(2)]
            M["row"] = s4("row", [P, D], F32)
            first_norm(nc, c4, M, A)
        with ExitStack() as c5:
            s5 = lambda n, s, d: c5.enter_context(nc.sbuf_tensor(n, s, d))
            M["xth"], M["xtl"] = s5("x1t_hi", [P, D], F16), s5("x1t_lo", [P, D], F16)
            qc = s5("sums_of_keys", [P, 2 * H, P], F32)
            so = s5("scores_or_onehot", [P, 2 * H, NKEY], F32)
            M["qt"] = s5("queries", [P, 2 * H, P], F32)
            M["cand"] = qc[:].rearrange("p (h a) b -> p h (a b)", a=2)
            M["sc"], M["oh"] = so, so[:].rearrange("p a (b c) -> p (a b) c", c=16)
            M["v16"], M["ix"] = s5("best_keys", [P, 2 * H, 16], F32), s5("best_key_ids", [P, 2 * H, 16], U32)
            M["top"], M["pos"] = s5("best_sums", [P, H, 16], F32), s5("best_places", [P, H, 16], U32)
            M["ixf"] = qc[:, 0:2, :].rearrange("p a (b c) -> p (a b) c", c=16)
            M["topj"], M["posf"] = qc[:, 2:4, :].bitcast(U32), qc[:, 4:6, :]
            M["sel_a"], M["sel_b"] = qc[:, 6, :], qc[:, 7, :]
            M["x1c"], M["xc"] = s5("x1_rows", [P, D], F32), s5("x1_chunk", [P, D], F32)
            for n in "gg hid".split():
                M[n] = s5(n, [P, NSEL], F32)
            M["gsum"], M["mark"] = s5("gsum", [P, H], F32), s5("mark", [P, 1], F32)
            for n in "idx_next idx".split():
                M[n] = s5(n, [P, NSEL], U32)
            M["hout"] = [s5(f"gelu_out{i}", [P, DT], F32) for i in range(2)]
            M["ut"] = [Tt[:, 4 + i, :].rearrange("p (k e) -> p k e", k=KD) for i in range(NU)]
            M["ring1"] = [Tt[:, i, :] for i in (6, 7, 8, 9, 10, 11, 20, 21)]
            hidden(nc, c5, M, A)
        wq_ctx.close()
        with ExitStack() as c6:
            s6 = lambda n, s, d: c6.enter_context(nc.sbuf_tensor(n, s, d))
            M["ln2"] = s6("ln2_sb", [P, 2, D], F32)
            M["acc"] = [s6(f"acc{i}", [P, D], F32) for i in range(2)]
            M["res"], M["x1c"] = s6("result", [P, D], F32), s6("x1_rows2", [P, D], F32)
            M["wgt"], M["wgt_all"] = s6("wgt", [P, NSEL], F32), s6("wgt_all", [P, ND, NSEL], F32)
            M["dense_sum"] = s6("dense_sum", [P, D], F32)
            M["idx2"] = s6("v_idx", [P, NSEL], U32)
            M["vt"] = [s6(f"v_block{i}", [P, D], F32)[:] for i in range(NV)]
            for n, k in (("gt", NV), ("ht", NV), ("wt", 4)):
                M[n] = [s6(f"{n}_block{i}", [P, DT], F32)[:] for i in range(k)]
            extra = [s6(f"ring_extra{i}", [P, D], F32) for i in range(2)]
            M["ring2"] = [Tt[:, i, :] for i in list(range(12)) + [20, 21]] + [e[:] for e in extra]
            values(nc, c6, M, A, out)


def layout(x, w_in, b_f, swa_sinks, pool_w, pool_scale, dw_w, dw_b, conv_ln_g, conv_ln_b,
           p_fox, p_swa, p_pool, p_conv, w_out, ln1_g, ln1_b,
           peer_wq, peer_k1, peer_k2, peer_u, peer_v, ln2_g, ln2_b):
    x = np.asarray(x)[0]
    w = np.asarray(w_in)[0]
    sizes = [512, 512, 512, 8, 512, 128, 128, 512, 512, 512, 4 * D]
    names = "qf kf vf f qs ks vs po ca cg gl".split()
    at = dict(zip(names, zip(np.cumsum([0] + sizes[:-1]), sizes)))
    cols = {n: w[:, a:a + s] for n, (a, s) in at.items()}
    swa = np.concatenate([np.r_[j * HD:(j + 1) * HD, (4 + j) * HD:(5 + j) * HD] for j in range(4)])
    cols["qs"] = cols["qs"][:, swa]
    wt = np.concatenate([cols[n] for n in "ca cg po qs qf kf ks vf vs".split()], 1)
    assert wt.shape[1] == B_ALL * P

    def kblocks(m, width):
        k = m.shape[0] // P
        return m.reshape(k, P, -1, width).transpose(2, 1, 0, 3)

    def rows(v):
        return np.broadcast_to(np.asarray(v)[0][None, :], (P, np.asarray(v).shape[1]))

    def chans(v):
        return np.asarray(v)[0].reshape(-1, P).T

    gl = cols["gl"].reshape(D, NB, D)
    ps_ = {"fox": np.asarray(p_fox)[0], "pool": np.asarray(p_pool)[0], "conv": np.asarray(p_conv)[0],
           "swa": np.asarray(p_swa)[0][swa]}
    strips = np.stack([np.concatenate([kblocks(gl[:, b], CW), kblocks(ps_[n], CW)], 2)
                       for b, n in enumerate(["fox", "pool", "conv", "swa"])], 1)
    i, j = np.arange(P)[:, None], np.arange(2 * P)[None, :]
    dist = i + P - j
    swa_mask = np.where((dist >= 0) & (dist < P), -8.0 * dist, -1e30)
    fox_mask = np.where(np.arange(P)[None, :] <= i, 0.0, -1e30)
    slopes = np.repeat(2.0 ** -np.arange(1, H + 1)[None, :], P, 0)
    masks = np.concatenate([swa_mask, fox_mask, np.eye(P), slopes], 1)
    sel = np.zeros((H, H, P))
    for h in range(H):
        sel[h, h] = 1.0
    rc = np.zeros((P, 4, 16))
    for g in range(4):
        rc[:, g] = 1.0 / np.minimum(np.arange(1, 17), 2 ** (g + 1))
    out = {
        "x": x, "x_t": x.T.reshape(KD, P, T).transpose(1, 0, 2),
        "w_t": kblocks(wt, P), "w_f": kblocks(cols["f"], H)[0],
        "strips": strips.reshape(NQ * NB, P, 12, CW),
        "w_o": np.asarray(w_out)[0].reshape(KD, P, D),
        "w_q": kblocks(np.asarray(peer_wq)[0], P),
        "b_f": np.asarray(b_f)[0][:, None], "sinks": rows(swa_sinks),
        "pool_w": np.asarray(pool_w)[0].transpose(1, 0, 2),
        "chan": np.stack([chans(dw_b), chans(conv_ln_g), chans(conv_ln_b), chans(pool_scale)], 1),
        "dw": np.asarray(dw_w)[0].reshape(CK, 4, P).transpose(2, 1, 0),
        "ln": np.stack([rows(ln1_g), rows(ln1_b), rows(ln2_g), rows(ln2_b)], 1),
        "k1_t": np.asarray(peer_k1)[0].T, "k2_t": np.asarray(peer_k2)[0].T,
        "u_t": np.asarray(peer_u)[0].reshape(NEXP // P, P, KD, P).transpose(0, 3, 2, 1),
        "tok": np.arange(float(P))[:, None],
        "u": np.asarray(peer_u)[0], "v": np.asarray(peer_v)[0],
        "masks": masks, "sel": sel, "rc": rc,
        "iota": np.repeat(np.arange(16.0)[None, :], P, 0),
    }
    return {n: np.ascontiguousarray(a, np.float32) for n, a in out.items()}


def kernel(**inputs):
    import concourse.bacc as bacc
    from concourse.bass_utils import run_bass_kernel_spmd

    nc = bacc.Bacc("TRN2", target_bir_lowering=False, num_devices=1)
    arrays = layout(**inputs)
    A = {n: nc.dram_tensor(n, a.shape, mybir.dt.from_np(a.dtype), kind="ExternalInput").ap()
         for n, a in arrays.items()}
    out = nc.dram_tensor("out", (T, D), F32, kind="ExternalOutput").ap()
    with ExitStack() as ctx:
        build_mix(nc, ctx, A, out)
    r = run_bass_kernel_spmd(nc, [arrays], core_ids=[0])
    return r.results[0]["out"].reshape(1, T, D)
```
